# Optimizing a Trainium2 kernel written in Bass

```python
import math
import jax, jax.numpy as jnp
from jax import lax
import numpy as np

D_MODEL = 1024
BATCH = 1
SEQ = 512
DEPTH = 4

CHUNK = 64
N_MIXERS = 3
EPS = 1e-6
N_FOX = (DEPTH + 2) // 3
N_S5 = (DEPTH + 1) // 3
N_POOL = DEPTH // 3
FOX_HEADS = 16
FOX_HEAD_DIM = D_MODEL // FOX_HEADS
Q_BLOCK = 128
FOX_IN = 3 * D_MODEL + FOX_HEADS
FORGET_BIAS_CENTER = 3.0
S5_GROUP = 16
S5_GROUPS = D_MODEL // S5_GROUP
S5_STATE = 64
S5_DT_MIN = 1e-3
S5_DT_MAX = 1e-1
POOL_WINDOWS = (2, 4, 8, 16)
POOL_GROUPS = len(POOL_WINDOWS)
POOL_WIDTH = D_MODEL // POOL_GROUPS
D_FF = -(-8 * D_MODEL // (3 * 256)) * 256


F32 = jnp.float32

def rms_norm(x, g):
    xf = x.astype(F32)
    y = xf * lax.rsqrt(jnp.mean(xf * xf, axis=-1, keepdims=True) + EPS)
    return (y * g.astype(F32)).astype(x.dtype)

def forgetting_attention(h, w_in, b_f, w_out):
    B, S, _ = h.shape
    proj = h @ w_in
    q, k, v, f_logit = jnp.split(proj, [D_MODEL, 2 * D_MODEL, 3 * D_MODEL], axis=-1)

    def heads(t):
        return t.reshape(B, S, FOX_HEADS, FOX_HEAD_DIM).transpose(0, 2, 1, 3).astype(F32)

    q, k, v = heads(q), heads(k), heads(v)
    log_f = jax.nn.log_sigmoid(f_logit.astype(F32) + b_f.astype(F32))
    c = jnp.cumsum(log_f, axis=1).transpose(0, 2, 1)
    n_blk = S // Q_BLOCK
    q_blocks = q.reshape(B, FOX_HEADS, n_blk, Q_BLOCK, FOX_HEAD_DIM).transpose(2, 0, 1, 3, 4)
    c_blocks = c.reshape(B, FOX_HEADS, n_blk, Q_BLOCK).transpose(2, 0, 1, 3)
    starts = jnp.arange(n_blk, dtype=jnp.int32) * Q_BLOCK
    key_pos = jnp.arange(S, dtype=jnp.int32)
    scale = FOX_HEAD_DIM ** -0.5

    def one_block(args):
        q_b, c_b, start = args
        logits = jnp.einsum('bhqd,bhkd->bhqk', q_b, k) * scale
        logits = logits + c_b[..., :, None] - c[..., None, :]
        q_pos = start + jnp.arange(Q_BLOCK, dtype=jnp.int32)
        mask = key_pos[None, :] <= q_pos[:, None]
        p = jax.nn.softmax(jnp.where(mask, logits, -jnp.inf), axis=-1)
        return jnp.einsum('bhqk,bhkd->bhqd', p, v)

    out = lax.map(one_block, (q_blocks, c_blocks, starts))
    out = out.transpose(1, 0, 3, 2, 4).reshape(B, S, D_MODEL).astype(h.dtype)
    return out @ w_out

def s5_layer(h, w_in, a_re, a_im, log_dt, b_re, b_im, c_re, c_im, d, w_glu):
    B, S, _ = h.shape
    u = (h @ w_in).astype(F32)
    u_g = u.reshape(B, S, S5_GROUPS, S5_GROUP).astype(jnp.complex64)
    lam = lax.complex(a_re.astype(F32), a_im.astype(F32))
    dt = jnp.exp(log_dt.astype(F32))[:, None]
    lam_bar = jnp.exp(lam * dt)
    b_mat = lax.complex(b_re.astype(F32), b_im.astype(F32))
    b_bar = ((lam_bar - 1.0) / lam)[..., None] * b_mat
    bu = jnp.einsum('gpc,bsgc->bsgp', b_bar, u_g)
    lam_seq = jnp.broadcast_to(lam_bar, bu.shape)

    def combine(left, right):
        a_l, s_l = left
        a_r, s_r = right
        return a_r * a_l, a_r * s_l + s_r

    _, states = lax.associative_scan(combine, (lam_seq, bu), axis=1)
    c_mat = lax.complex(c_re.astype(F32), c_im.astype(F32))
    y = jnp.einsum('gcp,bsgp->bsgc', c_mat, states).real.reshape(B, S, D_MODEL)
    y = y + d.astype(F32) * u
    g = jax.nn.gelu(y).astype(h.dtype)
    val, gate = jnp.split(g @ w_glu, 2, axis=-1)
    return val * jax.nn.sigmoid(gate)

def multiscale_pool(h, w_grp, b_grp, scale):
    B, S, _ = h.shape
    hf = h.astype(F32).reshape(B, S, POOL_GROUPS, POOL_WIDTH)
    count_base = jnp.arange(1, S + 1, dtype=F32)[None, :, None]
    outs = []
    for gi, w in enumerate(POOL_WINDOWS):
        xg = hf[:, :, gi]
        cs = jnp.cumsum(xg, axis=1)
        lag = jnp.pad(cs[:, :-w], ((0, 0), (w, 0), (0, 0)))
        mean = (cs - lag) / jnp.minimum(count_base, float(w))
        outs.append(jnp.einsum('bsc,cd->bsd', mean - xg, w_grp[gi].astype(F32)))
    y = jnp.concatenate(outs, axis=-1) + b_grp.astype(F32)
    return (y * scale.astype(F32)).astype(h.dtype)

def swiglu(h, w_gate_up, w_down):
    g, u = jnp.split(h @ w_gate_up, 2, axis=-1)
    return (jax.nn.silu(g) * u) @ w_down

def first_inputs(seed: int = 0) -> dict:
    key = jax.random.key(seed)
    ks = jax.random.split(key, 24)
    D, H, G, P, C = D_MODEL, FOX_HEADS, S5_GROUPS, S5_STATE, S5_GROUP
    nrm = jax.random.normal
    x = nrm(ks[0], (BATCH, SEQ, D), F32)
    mix_norm_g = 1.0 + 0.05 * nrm(ks[1], (DEPTH, D), F32)
    ffn_norm_g = 1.0 + 0.05 * nrm(ks[2], (DEPTH, D), F32)
    final_norm_g = 1.0 + 0.05 * nrm(ks[3], (D,), F32)
    fox_w_in = nrm(ks[4], (N_FOX, D, FOX_IN), F32) * D ** -0.5
    fox_b_f = FORGET_BIAS_CENTER + 0.5 * nrm(ks[5], (N_FOX, H), F32)
    fox_w_out = nrm(ks[6], (N_FOX, D, D), F32) * D ** -0.5
    s5_w_in = nrm(ks[7], (N_S5, D, D), F32) * D ** -0.5
    s5_a_re = -0.5 + 0.01 * nrm(ks[8], (N_S5, G, P), F32)
    s5_a_im = math.pi * jnp.arange(P, dtype=F32)[None, None, :] + 0.01 * nrm(ks[9], (N_S5, G, P), F32)
    s5_log_dt = jax.random.uniform(ks[10], (N_S5, G), F32, math.log(S5_DT_MIN), math.log(S5_DT_MAX))
    s5_b_re = nrm(ks[11], (N_S5, G, P, C), F32) * (2 * C) ** -0.5
    s5_b_im = nrm(ks[12], (N_S5, G, P, C), F32) * (2 * C) ** -0.5
    s5_c_re = nrm(ks[13], (N_S5, G, C, P), F32) * P ** -0.5
    s5_c_im = nrm(ks[14], (N_S5, G, C, P), F32) * P ** -0.5
    s5_d = nrm(ks[15], (N_S5, D), F32)
    s5_w_glu = nrm(ks[16], (N_S5, D, 2 * D), F32) * D ** -0.5
    pool_w = nrm(ks[17], (N_POOL, POOL_GROUPS, POOL_WIDTH, POOL_WIDTH), F32) * POOL_WIDTH ** -0.5
    pool_b = 0.01 * nrm(ks[18], (N_POOL, D), F32)
    pool_scale = 0.5 + 0.05 * nrm(ks[19], (N_POOL, D), F32)
    ffn_w_gate_up = nrm(ks[20], (DEPTH, D, 2 * D_FF), F32) * D ** -0.5
    ffn_w_down = nrm(ks[21], (DEPTH, D_FF, D), F32) * D_FF ** -0.5
    return {"x": x, "mix_norm_g": mix_norm_g, "ffn_norm_g": ffn_norm_g, "final_norm_g": final_norm_g,
            "fox_w_in": fox_w_in, "fox_b_f": fox_b_f, "fox_w_out": fox_w_out,
            "s5_w_in": s5_w_in, "s5_a_re": s5_a_re, "s5_a_im": s5_a_im, "s5_log_dt": s5_log_dt,
            "s5_b_re": s5_b_re, "s5_b_im": s5_b_im, "s5_c_re": s5_c_re, "s5_c_im": s5_c_im,
            "s5_d": s5_d, "s5_w_glu": s5_w_glu,
            "pool_w": pool_w, "pool_b": pool_b, "pool_scale": pool_scale,
            "ffn_w_gate_up": ffn_w_gate_up, "ffn_w_down": ffn_w_down}

def first_block(x, mix_norm_g, ffn_norm_g, final_norm_g, fox_w_in, fox_b_f, fox_w_out,
              s5_w_in, s5_a_re, s5_a_im, s5_log_dt, s5_b_re, s5_b_im, s5_c_re, s5_c_im,
              s5_d, s5_w_glu, pool_w, pool_b, pool_scale, ffn_w_gate_up, ffn_w_down):
    for i in range(DEPTH):
        h = rms_norm(x, mix_norm_g[i])
        kind, j = i % N_MIXERS, i // N_MIXERS
        if kind == 0:
            mix = forgetting_attention(h, fox_w_in[j], fox_b_f[j], fox_w_out[j])
        elif kind == 1:
            mix = s5_layer(h, s5_w_in[j], s5_a_re[j], s5_a_im[j], s5_log_dt[j], s5_b_re[j], s5_b_im[j],
                           s5_c_re[j], s5_c_im[j], s5_d[j], s5_w_glu[j])
        else:
            mix = multiscale_pool(h, pool_w[j], pool_b[j], pool_scale[j])
        x = x + mix.astype(x.dtype)
        x = x + swiglu(rms_norm(x, ffn_norm_g[i]), ffn_w_gate_up[i], ffn_w_down[i]).astype(x.dtype)
    return rms_norm(x, final_norm_g)


DEPTH_2 = 2

MLA_HEADS = 8
QK_NOPE_DIM = 64
QK_ROPE_DIM = 32
V_HEAD_DIM = 64
Q_LORA_RANK = 256
KV_LORA_RANK = 128
QK_HEAD_DIM = QK_NOPE_DIM + QK_ROPE_DIM
D_ATTN = MLA_HEADS * V_HEAD_DIM
ROPE_THETA = 10000.0
SSD_HEADS = 8
SSD_HEAD_DIM = 64
SSD_GROUPS = 2
SSD_STATE = 128
CONV_WIDTH = 4
CHUNK_2 = 128
D_SSD = SSD_HEADS * SSD_HEAD_DIM
D_CONV = D_SSD + 2 * SSD_GROUPS * SSD_STATE
D_MIX = D_ATTN + D_SSD
D_IN = Q_LORA_RANK + KV_LORA_RANK + QK_ROPE_DIM + D_SSD + D_CONV + SSD_HEADS
D_FF_2 = ((-(-8 * D_MODEL // 3) + 255) // 256) * 256
N_MOD = 6


def rmsnorm(x, w):
    xf = x.astype(jnp.float32)
    y = xf * lax.rsqrt(jnp.mean(xf * xf, axis=-1, keepdims=True) + EPS)
    return (y * w.astype(jnp.float32)).astype(x.dtype)

def rope(x, cos, sin):
    x1, x2 = jnp.split(x, 2, axis=-1)
    return jnp.concatenate([x1 * cos - x2 * sin, x2 * cos + x1 * sin], axis=-1)

def causal_attention(q, k, v):
    b, h, s, d = q.shape
    nb = s // Q_BLOCK
    scale = d ** -0.5
    qb = q.reshape(b, h, nb, Q_BLOCK, d).transpose(2, 0, 1, 3, 4)
    kpos = jnp.arange(s)

    def one_block(args):
        qi, i = args
        sc = jnp.einsum('bhqd,bhkd->bhqk', qi, k).astype(jnp.float32) * scale
        qpos = i * Q_BLOCK + jnp.arange(Q_BLOCK)
        mask = kpos[None, :] <= qpos[:, None]
        sc = jnp.where(mask, sc, jnp.finfo(jnp.float32).min)
        p = jax.nn.softmax(sc, axis=-1)
        return jnp.einsum('bhqk,bhkd->bhqd', p.astype(v.dtype), v)

    out = lax.map(one_block, (qb, jnp.arange(nb)))
    return out.transpose(1, 0, 3, 2, 4).reshape(b, s, h * v.shape[-1])

def ssd_chunked(x, dt, a, bm, cm):
    b, l, h, p = x.shape
    rep = h // bm.shape[2]
    nc = l // CHUNK_2
    xf = x.astype(jnp.float32)
    xdt = xf * dt[..., None]
    adt = dt * a
    bh = jnp.repeat(bm.astype(jnp.float32), rep, axis=2)
    ch = jnp.repeat(cm.astype(jnp.float32), rep, axis=2)
    n = bh.shape[-1]
    xc = xdt.reshape(b, nc, CHUNK_2, h, p)
    bc = bh.reshape(b, nc, CHUNK_2, h, n)
    cc = ch.reshape(b, nc, CHUNK_2, h, n)
    acs = jnp.cumsum(adt.reshape(b, nc, CHUNK_2, h), axis=2)
    seg = acs[:, :, :, None, :] - acs[:, :, None, :, :]
    tri = jnp.tril(jnp.ones((CHUNK_2, CHUNK_2), dtype=bool))[None, None, :, :, None]
    lmat = jnp.exp(jnp.where(tri, seg, -jnp.inf))
    scores = jnp.einsum('bclhn,bcshn->bclsh', cc, bc) * lmat
    y_diag = jnp.einsum('bclsh,bcshp->bclhp', scores, xc)
    decay_states = jnp.exp(acs[:, :, -1:, :] - acs)
    states = jnp.einsum('bcshn,bcsh,bcshp->bchpn', bc, decay_states, xc)
    chunk_decay = jnp.exp(acs[:, :, -1, :])

    def step(carry, inp):
        s_c, d_c = inp
        new = d_c[:, :, None, None] * carry + s_c
        return new, carry

    init = jnp.zeros((b, h, p, n), jnp.float32)
    _, prev = lax.scan(step, init, (states.transpose(1, 0, 2, 3, 4), chunk_decay.transpose(1, 0, 2)))
    prev = prev.transpose(1, 0, 2, 3, 4)
    y_off = jnp.einsum('bclhn,bchpn,bclh->bclhp', cc, prev, jnp.exp(acs))
    return (y_diag + y_off).reshape(b, l, h, p)

def hybrid_mixer(h, cos, sin, w_in, q_a_norm_w, w_q_up, kv_a_norm_w, w_kv_up,
                 q_nope_norm_w, q_pe_norm_w, k_nope_norm_w, k_pe_norm_w,
                 conv_w, conv_b, dt_bias, a_log, d_skip, ssd_norm_w, w_out):
    b, s, _ = h.shape
    proj = h @ w_in
    cuts = np.cumsum([Q_LORA_RANK, KV_LORA_RANK, QK_ROPE_DIM, D_SSD, D_CONV])
    q_a, kv_a, k_pe, z, xbc, dt_raw = jnp.split(proj, [int(i) for i in cuts], axis=-1)

    q = (rmsnorm(q_a, q_a_norm_w) @ w_q_up).reshape(b, s, MLA_HEADS, QK_HEAD_DIM)
    q_nope, q_pe = jnp.split(q, [QK_NOPE_DIM], axis=-1)
    kv = (rmsnorm(kv_a, kv_a_norm_w) @ w_kv_up).reshape(b, s, MLA_HEADS, QK_NOPE_DIM + V_HEAD_DIM)
    k_nope, v = jnp.split(kv, [QK_NOPE_DIM], axis=-1)
    q_nope = rmsnorm(q_nope, q_nope_norm_w)
    q_pe = rope(rmsnorm(q_pe, q_pe_norm_w), cos, sin)
    k_nope = rmsnorm(k_nope, k_nope_norm_w)
    k_pe = rope(rmsnorm(k_pe[:, :, None, :], k_pe_norm_w), cos, sin)
    q_full = jnp.concatenate([q_nope, q_pe], axis=-1)
    k_full = jnp.concatenate([k_nope, jnp.broadcast_to(k_pe, (b, s, MLA_HEADS, QK_ROPE_DIM))], axis=-1)
    attn_out = causal_attention(q_full.transpose(0, 2, 1, 3), k_full.transpose(0, 2, 1, 3),
                                v.transpose(0, 2, 1, 3))

    xbc = lax.conv_general_dilated(xbc, conv_w[:, None, :], window_strides=(1,),
                                   padding=[(CONV_WIDTH - 1, 0)],
                                   dimension_numbers=('NWC', 'WIO', 'NWC'),
                                   feature_group_count=D_CONV)
    xbc = jax.nn.silu(xbc + conv_b)
    xs, bm, cm = jnp.split(xbc, [D_SSD, D_SSD + SSD_GROUPS * SSD_STATE], axis=-1)
    xs = xs.reshape(b, s, SSD_HEADS, SSD_HEAD_DIM)
    bm = bm.reshape(b, s, SSD_GROUPS, SSD_STATE)
    cm = cm.reshape(b, s, SSD_GROUPS, SSD_STATE)
    dt = jax.nn.softplus(dt_raw.astype(jnp.float32) + dt_bias.astype(jnp.float32))
    a = -jnp.exp(a_log.astype(jnp.float32))
    y = ssd_chunked(xs, dt, a, bm, cm) + d_skip.astype(jnp.float32)[:, None] * xs.astype(jnp.float32)
    y = y.astype(h.dtype).reshape(b, s, D_SSD)
    yg = (y * jax.nn.silu(z)).reshape(b, s, SSD_GROUPS, D_SSD // SSD_GROUPS)
    yg = rmsnorm(yg, jnp.ones((D_SSD // SSD_GROUPS,), h.dtype)).reshape(b, s, D_SSD) * ssd_norm_w

    return jnp.concatenate([attn_out, yg], axis=-1) @ w_out

def swiglu_2(h, w_gate_up, w_down):
    g, u = jnp.split(h @ w_gate_up, 2, axis=-1)
    return (jax.nn.silu(g) * u) @ w_down

def second_inputs(seed: int = 0) -> dict:
    key = jax.random.key(seed)
    ks = jax.random.split(key, 32)
    f32 = jnp.float32

    def nrm(k, shape, scale):
        return jax.random.normal(k, shape, f32) * scale

    def gain(k, shape):
        return 1.0 + 0.05 * jax.random.normal(k, shape, f32)

    L = DEPTH_2
    dt0 = jnp.exp(jax.random.uniform(ks[18], (L, SSD_HEADS), f32, np.log(1e-3), np.log(1e-1)))
    dt_bias = dt0 + jnp.log(-jnp.expm1(-dt0))
    pos_off = jax.random.randint(ks[2], (BATCH, 1), 0, 1024, dtype=jnp.int32)
    return {
        "x": nrm(ks[0], (BATCH, SEQ, D_MODEL), 1.0),
        "c": nrm(ks[1], (BATCH, D_MODEL), 1.0),
        "positions": pos_off + jnp.arange(SEQ, dtype=jnp.int32)[None, :],
        "norm1_w": gain(ks[3], (L, D_MODEL)),
        "norm2_w": gain(ks[4], (L, D_MODEL)),
        "w_ada": nrm(ks[5], (L, D_MODEL, N_MOD * D_MODEL), 0.5 * D_MODEL ** -0.5),
        "b_ada": nrm(ks[6], (L, N_MOD * D_MODEL), 0.01),
        "w_in": nrm(ks[7], (L, D_MODEL, D_IN), D_MODEL ** -0.5),
        "q_a_norm_w": gain(ks[8], (L, Q_LORA_RANK)),
        "w_q_up": nrm(ks[9], (L, Q_LORA_RANK, MLA_HEADS * QK_HEAD_DIM), Q_LORA_RANK ** -0.5),
        "kv_a_norm_w": gain(ks[10], (L, KV_LORA_RANK)),
        "w_kv_up": nrm(ks[11], (L, KV_LORA_RANK, MLA_HEADS * (QK_NOPE_DIM + V_HEAD_DIM)), KV_LORA_RANK ** -0.5),
        "q_nope_norm_w": gain(ks[12], (L, QK_NOPE_DIM)),
        "q_pe_norm_w": gain(ks[13], (L, QK_ROPE_DIM)),
        "k_nope_norm_w": gain(ks[14], (L, QK_NOPE_DIM)),
        "k_pe_norm_w": gain(ks[15], (L, QK_ROPE_DIM)),
        "conv_w": nrm(ks[16], (L, CONV_WIDTH, D_CONV), CONV_WIDTH ** -0.5),
        "conv_b": nrm(ks[17], (L, D_CONV), 0.01),
        "dt_bias": dt_bias,
        "a_log": jnp.log(jax.random.uniform(ks[19], (L, SSD_HEADS), f32, 1.0, 16.0)),
        "d_skip": 1.0 + 0.1 * jax.random.normal(ks[20], (L, SSD_HEADS), f32),
        "ssd_norm_w": gain(ks[21], (L, D_SSD)),
        "w_out": nrm(ks[22], (L, D_MIX, D_MODEL), D_MIX ** -0.5),
        "w_gate_up": nrm(ks[23], (L, D_MODEL, 2 * D_FF_2), D_MODEL ** -0.5),
        "w_down": nrm(ks[24], (L, D_FF_2, D_MODEL), D_FF_2 ** -0.5),
    }

def second_block(x, c, positions, norm1_w, norm2_w, w_ada, b_ada, w_in, q_a_norm_w, w_q_up,
              kv_a_norm_w, w_kv_up, q_nope_norm_w, q_pe_norm_w, k_nope_norm_w, k_pe_norm_w,
              conv_w, conv_b, dt_bias, a_log, d_skip, ssd_norm_w, w_out, w_gate_up, w_down):
    inv_freq = 1.0 / (ROPE_THETA ** (jnp.arange(0, QK_ROPE_DIM, 2, dtype=jnp.float32) / QK_ROPE_DIM))
    ang = positions.astype(jnp.float32)[..., None] * inv_freq
    cos = jnp.cos(ang)[:, :, None, :].astype(x.dtype)
    sin = jnp.sin(ang)[:, :, None, :].astype(x.dtype)
    c_act = jax.nn.silu(c)
    for l in range(DEPTH_2):
        mod = (c_act @ w_ada[l] + b_ada[l])[:, None, :]
        sh1, sc1, g1, sh2, sc2, g2 = jnp.split(mod, N_MOD, axis=-1)
        h = rmsnorm(x, norm1_w[l]) * (1.0 + sc1) + sh1
        x = x + g1 * hybrid_mixer(h, cos, sin, w_in[l], q_a_norm_w[l], w_q_up[l], kv_a_norm_w[l],
                                  w_kv_up[l], q_nope_norm_w[l], q_pe_norm_w[l], k_nope_norm_w[l],
                                  k_pe_norm_w[l], conv_w[l], conv_b[l], dt_bias[l], a_log[l],
                                  d_skip[l], ssd_norm_w[l], w_out[l])
        h = rmsnorm(x, norm2_w[l]) * (1.0 + sc2) + sh2
        x = x + g2 * swiglu_2(h, w_gate_up[l], w_down[l])
    return x


def setup_inputs(seed=0):
    out = dict(first_inputs(seed))
    for name, value in second_inputs(seed + 1).items():
        if name != "x":
            out[name + "_2"] = value
    return out


def reference(
    x, mix_norm_g, ffn_norm_g, final_norm_g, fox_w_in, fox_b_f, fox_w_out, s5_w_in, s5_a_re,
    s5_a_im, s5_log_dt, s5_b_re, s5_b_im, s5_c_re, s5_c_im, s5_d, s5_w_glu, pool_w, pool_b,
    pool_scale, ffn_w_gate_up, ffn_w_down, c_2, positions_2, norm1_w_2, norm2_w_2, w_ada_2,
    b_ada_2, w_in_2, q_a_norm_w_2, w_q_up_2, kv_a_norm_w_2, w_kv_up_2, q_nope_norm_w_2,
    q_pe_norm_w_2, k_nope_norm_w_2, k_pe_norm_w_2, conv_w_2, conv_b_2, dt_bias_2, a_log_2,
    d_skip_2, ssd_norm_w_2, w_out_2, w_gate_up_2, w_down_2,
):
    x = first_block(
        x, mix_norm_g, ffn_norm_g, final_norm_g, fox_w_in, fox_b_f, fox_w_out, s5_w_in, s5_a_re,
        s5_a_im, s5_log_dt, s5_b_re, s5_b_im, s5_c_re, s5_c_im, s5_d, s5_w_glu, pool_w, pool_b,
        pool_scale, ffn_w_gate_up, ffn_w_down,
    )
    return second_block(
        x, c_2, positions_2, norm1_w_2, norm2_w_2, w_ada_2, b_ada_2, w_in_2, q_a_norm_w_2,
        w_q_up_2, kv_a_norm_w_2, w_kv_up_2, q_nope_norm_w_2, q_pe_norm_w_2, k_nope_norm_w_2,
        k_pe_norm_w_2, conv_w_2, conv_b_2, dt_bias_2, a_log_2, d_skip_2, ssd_norm_w_2, w_out_2,
        w_gate_up_2, w_down_2,
    )


_drawn_inputs = setup_inputs


def setup_inputs(seed=0):
    import zlib

    import numpy as np

    out = dict(_drawn_inputs(seed))
    spreads = {}
    factors = {'s5_a_re': 8.0,
     'pool_b': 8.0,
     'norm2_w_2': 2.722,
     'b_ada_2': 3.353,
     'q_a_norm_w_2': 8.0,
     'kv_a_norm_w_2': 8.0,
     'q_nope_norm_w_2': 8.0,
     'q_pe_norm_w_2': 8.0,
     'k_nope_norm_w_2': 8.0,
     'k_pe_norm_w_2': 8.0,
     'conv_b_2': 8.0,
     'd_skip_2': 3.04,
     'ssd_norm_w_2': 3.938}
    for name, (base, spread) in spreads.items():
        noise = np.random.default_rng([zlib.crc32(name.encode()), seed]).standard_normal(out[name].shape)
        drawn = base * np.exp(spread * noise) if base else spread * noise
        out[name] = __import__('jax').numpy.asarray(drawn.astype(out[name].dtype))
    for name, factor in factors.items():
        out[name] = (out[name] * factor).astype(out[name].dtype)
    return out
```

```python
from contextlib import ExitStack, contextmanager

import numpy as np

import concourse.bass as bass
from concourse import mybir

F32 = mybir.dt.float32
BF16 = mybir.dt.bfloat16
I32 = mybir.dt.int32
ALU = mybir.AluOpType
ACT = mybir.ActivationFunctionType
AX = mybir.AxisListType

P = 128
S = 512
ST = S // P
D = 1024
DK = D // P
FF = 2816
FK = FF // P
EPS = 1e-6
FH = 16
G5, N5, C5 = 64, 64, 16
WINDOWS = (2, 4, 8, 16)
MH = 8
NOPE, ROPE = 64, 32
QH = NOPE + ROPE
Q_LORA, KV_LORA = 256, 128
D_ZI = Q_LORA + KV_LORA + ROPE
D_XBC = D_ZI + 512
D_DT = D_XBC + 1024
CONVW = 4
BIG = -1e30
SLOT = FK * 256
TWO_PI = 2 * np.pi
TURN_PARTS = (6.28125, 0.0019340515136718750, float(TWO_PI - 6.28125 - 0.0019340515136718750))
PI_IN = float(np.nextafter(np.float32(np.pi), np.float32(0)))


class Count:

    def __init__(self, sem):
        self.sem = sem
        self.done = 0

    def at(self, n):
        return n + self.done


SEMAPHORES = """
    h_ready turned sp_y sp_u sp_e sp_ln c_ready v_taken exp_ready pt_ready o_taken max_ready p_turned pv_done
    cm_ready q_staged k_staged ck_done logits_ready logits_taken quad_taken diff_ready pooled pads_clear
    biased s5_rows s5_step s5_loaded s5_act bin_ready cin_ready bt_ready bu_taken x_ready ct_ready5 y_taken
    b_turned c_turned bu_ready y_ready c_active mod_taken angles second_loaded sines conv_ready acs_ready
    cb_ready acsT_ready xdtd_ready bt_ready2 st_ready am_ready decay_ready xdt_ready l_ready sc_ready
    cth_ready y_gated ysq_ready cb_done bt_done last_spread dec_arg bc_ready bm_ready ysq_used e_ready yh_done
    a_ready rows_turned cd_ready xt_done st_done ystd_ready lsq_ready raw_taken lat_ready lv_taken stat_ready
    normed isq_ready rot_taken lsq_used raw_ready isq_used kpe_copied lv_done rot_done lstd_ready stat_std
    cos_done stat_spread ct_ready filled sq_ready sq_used std_ready h_scaled pair_taken half_ready out_taken
    x_loaded params_loaded turn_taken stored
""".split()


def due(n):
    return not isinstance(n, int) or n > 0


class Chain:

    def __init__(self, sem):
        self.sem, self.base, self.k = sem, 0, 0

    def __call__(self, eng, ins):
        self.k += 1
        ins.then_inc(self.sem, 1)
        eng.wait_ge(self.sem, self.base + self.k)

    @contextmanager
    def loop(self, eng, n, per):
        b = self.base + self.k
        with eng.Fori(0, n) as i:
            self.base, self.k = i * per + b, 0
            yield i
            assert self.k == per, (self.k, per)
        self.base, self.k = b + n * per, 0


def columns():
    at, n = {}, 0
    for name, rows in (("mix", 32), ("ffn", 32), ("final", 8), ("s5_d", 8), ("pool_b", 8), ("pool_s", 8)):
        at[name] = n
        n += rows
    n = 128
    for name, rows in (("norm1", 16), ("norm2", 16), ("b_ada", 96)):
        at[name] = n
        n += rows
    for name, rows in (("q_a", 4), ("kv_a", 2), ("conv_b", 16), ("ssd_n", 8), ("conv_w", 64), ("c", 8)):
        at[name] = n
        n += rows
    return at


COL = columns()


def shape_constants():
    ident = np.eye(P)
    rot = np.zeros((P, P))
    for i in range(ROPE // 2):
        rot[NOPE + ROPE // 2 + i, NOPE + i] = -1
        rot[NOPE + i, NOPE + ROPE // 2 + i] = 1
    last = np.zeros((P, P))
    last[P - 1] = 1
    future = np.where(np.arange(P)[None, :] > np.arange(P)[:, None], BIG, 0)
    half = (np.arange(P)[:, None] // N5 == (np.arange(P)[None, :] % 32) // C5).astype(float)
    rc = np.stack([1 / np.minimum(np.arange(16) + 1, w) for w in WINDOWS]).reshape(1, 64) * np.ones((P, 1))
    inv = (1.0 / (np.float32(10000.0) ** (np.arange(0, ROPE, 2, dtype=np.float32) / np.float32(ROPE)))).astype(np.float32)
    invc = np.zeros((P, 1))
    invc[NOPE:QH, 0] = np.tile(inv, 2)
    gather = np.zeros((P, 62))
    gather[:NOPE, 30] = 1 / NOPE
    gather[NOPE:QH, 31] = 1 / ROPE
    parts = dict(gather=gather, ident=ident, rot=rot, last=last, future=future, past=future.T, half=half, rc=rc, inv=invc)
    at, n = {}, 0
    for k, v in parts.items():
        at[k] = (n, n + v.shape[1])
        n += v.shape[1]
    return at, np.concatenate(list(parts.values()), axis=1).astype(np.float32)


CONST_AT, CONSTS = shape_constants()

SPREAD = np.zeros((32, 2 * MH, QH), np.float32)
for _n in range(2 * MH):
    SPREAD[2 * _n, _n, :NOPE] = 1
    SPREAD[2 * _n + 1, _n, NOPE:] = 1
SPREAD = SPREAD.reshape(32, -1)


class Machine:

    def __init__(self, nc, ctx, d):
        self.nc, self.d, self.ctx = nc, d, ctx

        def sb(name, shape, dt=F32):
            return ctx.enter_context(nc.sbuf_tensor(name, shape, dt))

        self.x = sb("xT", [P, DK, S])
        self.h = sb("hT", [P, DK, S])
        self.act = sb("act", [P, FK, S])
        self.w = [sb(f"w{i}", [P, SLOT]) for i in range(2)]
        self.misc = sb("misc", [P, 18 * S])
        self.sg = sb("sg", [P, 2, 2, S])
        self.sq = sb("sq", [P, 2, S])
        self.std = sb("std", [P, S])
        self.rstd = sb("rstd", [P, S])
        self.consts = sb("consts", [P, CONSTS.shape[1]])
        self.cols = sb("cols", [P, 384])
        self.mean_w = sb("mean_w", [P, P])
        self.ones = sb("ones", [P, P])
        self.identb = sb("identb", [P, P], BF16)
        self.futureb = sb("futureb", [P, P], BF16)
        self.pastb = sb("pastb", [P, P], BF16)
        self.eps = sb("eps", [P, 1])
        self.wdt = sb("wdt", [P, 2, DK, MH])
        self.heads = sb("heads", [MH, 4])
        self.qkn = sb("qkn", [P, 4])
        self.dskip = sb("dskip", [P, 8])
        self.rope = sb("rope", [P, 2, S])
        self.cact = sb("cact", [P, DK])
        self.gains = sb("gains", [P, 2, 2, DK])
        self.gather = self.c("gather")
        self.spread = sb("spread", [32, 16 * QH])
        self.rowmask = sb("rowmask", [P, 4])
        self.ones16 = sb("ones16", [FH, S])
        self.small = sb("small", [P, 512])
        self.wf = sb("wf", [P, 2, DK, FH])
        self.mod = sb("mod", [P, 2, 48])
        self.tok_v = self.act[:, 0:8, :].rearrange("p a s -> p (a s)").rearrange("p (t d) -> p t d", t=ST)
        self.tok_out = self.act[:, 8:16, :].rearrange("p a s -> p (a s)").rearrange("p (t d) -> p t d", t=ST)
        self.ps = ctx.enter_context(nc.psum_tensor("ps", [P, 8, S], F32))
        self.w_in = [ctx.enter_context(nc.semaphore(f"w_in{i}")) for i in range(2)]
        self.chunk_done = ctx.enter_context(nc.semaphore("chunk_done"))
        self.counts = {name: Count(ctx.enter_context(nc.semaphore(name))) for name in SEMAPHORES}
        self.sem = {name: c.sem for name, c in self.counts.items()}
        self.dve = Chain(ctx.enter_context(nc.semaphore("dve_chain")))
        self.acts = Chain(ctx.enter_context(nc.semaphore("act_chain")))
        self.pool = Chain(ctx.enter_context(nc.semaphore("pool_chain")))

    def c(self, name):
        a, b = CONST_AT[name]
        return self.consts[:, a:b]

    def col(self, name, k):
        return self.cols[:, COL[name] + k:COL[name] + k + 1]

    def count(self, name):
        return self.counts[name]

    def at(self, name, n):
        return n + self.counts[name].done

    def loads(self, todo):

        def run(sp):
            for load, c0, j0, j1 in todo:
                if j1 - j0 >= 6:
                    n2 = (j1 - j0) // 2
                    with sp.Fori(0, n2) as i:
                        for u in range(2):
                            self.load_one(sp, load, c0, i * 2 + (j0 + u), (c0 + j0 + u) % 2, True)
                    j0 += 2 * n2
                for j in range(j0, j1):
                    self.load_one(sp, load, c0, j, (c0 + j) % 2, c0 + j >= 2)
        return run

    def load_one(self, sp, load, c0, j, slot, wait):
        aps = load(j, self.w[slot])
        if wait:
            sp.wait_ge(self.chunk_done, j + (c0 - 1))
        for dst, src in aps:
            sp.dma_start(dst, src).then_inc(self.w_in[slot], 32 // len(aps))


def finish(m, **totals):
    for name, n in totals.items():
        m.count(name).done += n


class Stage:
    n = 0
    load = None

    def __init__(self, m):
        self.m = m

    def sync(self, e): pass
    def tensor(self, e): pass
    def vector(self, e): pass
    def scalar(self, e): pass
    def gpsimd(self, e): pass
    def end(self): pass

    def landed(self, pe, j, parity):
        if isinstance(j, int):
            pe.wait_ge(self.m.w_in[parity], 32 * ((self.c0 + j) // 2 + 1))
        else:
            i, u = j
            pe.wait_ge(self.m.w_in[parity], i * 32 + 32 * ((self.c0 + u) // 2 + 1))


def pairs(eng, n, first, body, chain=None, per=0):
    for j in range(min(first, n)):
        body(j)
    n2 = (n - first) // 2
    if n2 >= 2:
        if chain is None:
            with eng.Fori(0, n2) as i:
                for u in range(2):
                    body((i, first + u))
        else:
            with chain.loop(eng, n2, per) as i:
                for u in range(2):
                    body((i, first + u))
        first += 2 * n2
    for j in range(first, n):
        body(j)


def val(j):
    return j if isinstance(j, int) else j[0] * 2 + j[1]


def par(j):
    return (j if isinstance(j, int) else j[1]) % 2


class Norm:

    def __init__(self, m, gain, shift=None):
        self.m, self.gain, self.shift = m, gain, shift

    def scalar(self, e):
        m, nc = self.m, self.m.nc
        sq_ready, sq_used, std_ready = m.count("sq_ready"), m.count("sq_used"), m.count("std_ready")
        for k in range(DK):
            if k >= 2:
                e.wait_ge(sq_used.sem, sq_used.at(k - 1))
            nc.scalar.activation(m.sq[:, k % 2, :], m.x[:, k, :], ACT.Square).then_inc(sq_ready.sem, 1)
        e.wait_ge(sq_used.sem, sq_used.at(DK))
        nc.scalar.activation(m.std[:], m.ps[:, 7, :], ACT.Sqrt, bias=m.eps[:, 0:1]).then_inc(std_ready.sem, 1)
        if self.shift:
            pre, h_ready = m.count("h_scaled"), m.count("h_ready")
            for k in range(DK):
                e.wait_ge(pre.sem, pre.at(k + 1))
                nc.scalar.activation(m.h[:, k, :], m.h[:, k, :], ACT.Identity, bias=self.shift(k)).then_inc(h_ready.sem, 1)

    def tensor(self, e):
        m, nc = self.m, self.m.nc
        sq_ready, sq_used = m.count("sq_ready"), m.count("sq_used")
        for k in range(DK):
            e.wait_ge(sq_ready.sem, sq_ready.at(k + 1))
            nc.tensor.matmul(m.ps[:, 7, :], m.mean_w[:], m.sq[:, k % 2, :], start=k == 0, stop=k == DK - 1).then_inc(sq_used.sem, 1)

    def vector(self, e):
        m, nc = self.m, self.m.nc
        std_ready = m.count("std_ready")
        out = m.count("h_scaled" if self.shift else "h_ready")
        e.wait_ge(std_ready.sem, std_ready.at(1))
        m.dve(e, nc.vector.reciprocal(m.rstd[:], m.std[:]))
        for k in range(DK):
            nc.vector.scalar_tensor_tensor(self.dst(k), m.x[:, k, :], self.gain(k), m.rstd[:], ALU.mult, ALU.mult).then_inc(out.sem, 1)

    def dst(self, k):
        return self.m.h[:, k, :]

    def end(self):
        finish(self.m, sq_ready=DK, sq_used=DK, std_ready=1, h_ready=DK)
        if self.shift:
            finish(self.m, h_scaled=DK)


class GateUp(Stage):

    def __init__(self, m, w, width, norm, glu=False):
        super().__init__(m)
        self.wt, self.width, self.norm, self.glu = w, width, norm, glu
        self.n = width // 256
        self.rhs = m.h
        self.src = w.rearrange("(k p) n -> p k n", p=P)

    def load(self, j, slot):
        v = slot[:, 0:DK * 512].rearrange("p (k g n) -> p k g n", k=DK, g=2)
        return [(v[:, :, g, :], self.src[:, :, bass.ds(j * 256 + g * self.width, 256)]) for g in range(2)]

    def tensor(self, e):
        m, nc = self.m, self.m.nc
        h_ready, taken = m.count("h_ready"), m.count("pair_taken")
        if self.norm:
            self.norm.tensor(e)

        def chunk(j):
            slot = (self.c0 + par(j)) % 2
            self.landed(e, j, slot)
            if not (isinstance(j, int) and j < 2):
                e.wait_ge(taken.sem, val(j) + (taken.done - 1))
            v = m.w[slot][:, 0:DK * 512].rearrange("p (k b n) -> p k b n", k=DK, b=4)
            for k in range(DK):
                if self.norm and isinstance(j, int) and j == 0:
                    e.wait_ge(h_ready.sem, h_ready.at(k + 1))
                for b in range(4):
                    last = nc.tensor.matmul(m.ps[:, par(j) * 4 + b, :], v[:, k, b, :], m.h[:, k, :], start=k == 0, stop=k == DK - 1)
            last.then_inc(m.chunk_done, 1)
        pairs(e, self.n, 1, chunk)

    def scalar(self, e):
        m, nc = self.m, self.m.nc
        taken, half = m.count("pair_taken"), m.count("half_ready")
        if self.norm:
            self.norm.scalar(e)

        def chunk(j):
            if not (isinstance(j, int) and j < 2):
                e.wait_ge(taken.sem, val(j) + (taken.done - 1))
            e.wait_ge(m.chunk_done, val(j) + (self.c0 + 1))
            b = par(j) * 4 + 2 * self.glu
            nc.scalar.activation(m.sg[:, par(j)], m.ps[:, b:b + 2, :], ACT.Sigmoid if self.glu else ACT.Silu).then_inc(half.sem, 1)
        pairs(e, self.n, 1, chunk)

    def vector(self, e):
        m, nc = self.m, self.m.nc
        taken, half = m.count("pair_taken"), m.count("half_ready")
        if self.norm:
            self.norm.vector(e)

        def chunk(j):
            e.wait_ge(half.sem, val(j) + (half.done + 1))
            b = par(j) * 4 + 2 * (not self.glu)
            if self.glu:
                m.dve(e, nc.vector.tensor_tensor(m.sg[:, par(j)], m.sg[:, par(j)], m.ps[:, b:b + 2, :], ALU.mult))
                xs = m.x[:, bass.ds(val(j) * 2, 2), :]
                nc.vector.tensor_tensor(xs, xs, m.sg[:, par(j)], ALU.add).then_inc(taken.sem, 1)
            else:
                nc.vector.tensor_tensor(m.act[:, bass.ds(val(j) * 2, 2), :], m.sg[:, par(j)], m.ps[:, b:b + 2, :], ALU.mult).then_inc(taken.sem, 1)
        pairs(e, self.n, self.n if self.glu else 1, chunk)

    def end(self):
        if self.norm:
            self.norm.end()
        finish(self.m, pair_taken=self.n, half_ready=self.n)


class Project(Stage):

    def __init__(self, m, w, src, gate=None, turn=None, tok=None):
        super().__init__(m)
        self.tok = tok if tok is not None else m.tok_out
        self.srcs, self.gate, self.turn = src, gate, turn
        self.kt = w.shape[0] // P
        self.n = D // 256
        self.wv = w.rearrange("(k p) n -> p k n", p=P)

    def load(self, j, slot):
        v = slot[:, 0:self.kt * 256].rearrange("p (k n) -> p k n", k=self.kt)
        return [(v, self.wv[:, :, bass.ds(j * 256, 256)])]

    def tensor(self, e):
        m, nc = self.m, self.m.nc
        taken = m.count("out_taken")
        if self.turn:
            for k in range(self.turn):
                if due(k - 3):
                    e.wait_ge(m.sem["h_ready"], m.at("h_ready", k - 3))
                for t in range(ST):
                    last = nc.tensor.transpose(m.ps[:, 4 + k % 4, t * P:(t + 1) * P], self.tok[:, t, k * P:(k + 1) * P], m.c("ident"))
                last.then_inc(m.sem["turned"], 1)

        def chunk(j):
            slot = (self.c0 + par(j)) % 2
            self.landed(e, j, slot)
            if not (isinstance(j, int) and j < 2):
                e.wait_ge(taken.sem, val(j) + (taken.done - 1))
            v = m.w[slot][:, 0:self.kt * 256].rearrange("p (k b n) -> p k b n", k=self.kt, b=2)
            for k in range(self.kt):
                if j == 0 and k < (self.turn or 0):
                    e.wait_ge(m.sem["h_ready"], m.at("h_ready", k + 1))
                for b in range(2):
                    last = nc.tensor.matmul(m.ps[:, par(j) * 2 + b, :], v[:, k, b, :], self.srcs(k), start=k == 0, stop=k == self.kt - 1)
            last.then_inc(m.chunk_done, 1)
        pairs(e, self.n, 2, chunk)

    def vector(self, e):
        m, nc = self.m, self.m.nc
        taken = m.count("out_taken")
        for k in range(self.turn or 0):
            e.wait_ge(m.sem["turned"], m.at("turned", k + 1))
            nc.vector.tensor_copy(m.h[:, k, :], m.ps[:, 4 + k % 4, :]).then_inc(m.sem["h_ready"], 1)

        def chunk(j):
            e.wait_ge(m.chunk_done, val(j) + (self.c0 + 1))
            for b in range(2):
                xs = m.x[:, 2 * j + b, :]
                gate = self.gate(2 * j + b) if self.gate else 1.0
                last = nc.vector.scalar_tensor_tensor(xs, m.ps[:, par(j) * 2 + b, :], gate, xs, ALU.mult, ALU.add)
            last.then_inc(taken.sem, 1)
        for j in range(self.n):
            chunk(j)

    def end(self):
        finish(self.m, out_taken=self.n, h_ready=self.turn or 0, turned=self.turn or 0)


class Softplus:

    def __init__(self, m, y, a, b, out):
        self.m, self.y, self.a, self.b, self.out = m, y, a, b, out

    def scalar(self, e):
        m, nc = self.m, self.m.nc
        e.wait_ge(m.sem["sp_y"], m.at("sp_y", 1))
        m.acts(e, nc.scalar.activation(self.a, self.y, ACT.Abs))
        nc.scalar.activation(self.a, self.a, ACT.Exp, scale=-1.0).then_inc(m.sem["sp_e"], 1)
        e.wait_ge(m.sem["sp_u"], m.at("sp_u", 1))
        nc.scalar.activation(self.out, self.b, ACT.Ln).then_inc(m.sem["sp_ln"], 1)

    def vector(self, e):
        m, nc = self.m, self.m.nc
        e.wait_ge(m.sem["sp_e"], m.at("sp_e", 1))
        nc.vector.tensor_scalar(self.b, self.a, 1.0, None, ALU.add).then_inc(m.sem["sp_u"], 1)
        e.wait_ge(m.sem["sp_u"], m.at("sp_u", 1))
        e.wait_ge(m.sem["sp_ln"], m.at("sp_ln", 1))
        tt, ts = nc.vector.tensor_tensor, nc.vector.tensor_scalar
        m.dve(e, nc.vector.scalar_tensor_tensor(self.a, self.b, -1.0, self.a, ALU.add, ALU.subtract))
        m.dve(e, nc.vector.reciprocal(self.b, self.b))
        m.dve(e, nc.vector.scalar_tensor_tensor(self.a, self.a, -1.0, self.b, ALU.mult, ALU.mult))
        m.dve(e, nc.vector.scalar_tensor_tensor(self.a, self.y, 0.0, self.a, ALU.max, ALU.add))
        m.dve(e, tt(self.out, self.out, self.a, ALU.add))

    def end(self):
        finish(self.m, sp_y=1, sp_e=1, sp_u=1, sp_ln=1)


class FoxV(Stage):
    n = 2

    def __init__(self, m, l, norm):
        super().__init__(m)
        self.l, self.norm = l, norm
        self.wv = m.d["fox_w_in"][l].rearrange("(k p) n -> p k n", p=P)
        f = m.act
        self.sp = Softplus(m, f[0:FH, 16, :], f[0:FH, 17, :], f[0:FH, 18, :], f[0:FH, 19, :])

    def load(self, j, slot):
        return [(slot[:, 0:DK * 512].rearrange("p (k n) -> p k n", k=DK), self.wv[:, :, bass.ds(2 * D + j * 512, 512)])]

    def tensor(self, e):
        m, nc = self.m, self.m.nc
        self.norm.tensor(e)
        for j in range(2):
            slot = (self.c0 + j) % 2
            self.landed(e, j, slot)
            v = m.w[slot][:, 0:DK * 512].rearrange("p (k n) -> p k n", k=DK)
            if j == 1:
                e.wait_ge(m.sem["sp_y"], m.at("sp_y", 1))
            for k in range(DK):
                if j == 0:
                    e.wait_ge(m.sem["h_ready"], m.at("h_ready", k + 1))
                for t in range(ST):
                    last = nc.tensor.matmul(m.ps[:, 4 * j + t, :], m.h[:, k, t * P:(t + 1) * P], v[:, k, :], start=k == 0, stop=k == DK - 1)
                if j == 0:
                    f = nc.tensor.matmul(m.ps[0:FH, 4, :], m.wf[:, self.l, k, :], m.h[:, k, :], start=k == 0, stop=k == DK - 1)
            (f if j == 0 else last).then_inc(m.chunk_done, 1)
        e.wait_ge(m.sem["c_ready"], m.at("c_ready", 1))
        e.wait_ge(m.sem["v_taken"], m.at("v_taken", 1))
        for t in range(ST):
            last = nc.tensor.transpose(m.ps[:, 0, t * FH:(t + 1) * FH], m.misc[0:FH, 16 * S + t * P:16 * S + (t + 1) * P], m.c("ident")[0:FH, 0:FH])
        last.then_inc(m.sem["turned"], 1)

    def scalar(self, e):
        m, nc = self.m, self.m.nc
        self.norm.scalar(e)
        for j in range(2):
            e.wait_ge(m.chunk_done, self.c0 + j + 1)
            nc.scalar.activation(m.tok_v[:, :, j * 512:(j + 1) * 512], m.ps[:, 4 * j:4 * j + 4, :], ACT.Copy).then_inc(m.sem["v_taken"], 1)
            if j == 0:
                self.sp.scalar(e)

    def vector(self, e):
        m, nc = self.m, self.m.nc
        self.norm.vector(e)
        e.wait_ge(m.chunk_done, self.c0 + 1)
        nc.vector.tensor_scalar(self.sp.y, m.ps[0:FH, 4, :], m.small[0:FH, self.l:self.l + 1], -1.0, ALU.add, ALU.mult).then_inc(m.sem["sp_y"], 1)
        e.wait_ge(m.sem["sp_y"], m.at("sp_y", 1))
        self.sp.vector(e)
        nc.vector.tensor_tensor_scan(m.misc[0:FH, 16 * S:17 * S], m.ones16[0:FH, :], self.sp.out, 0.0, ALU.mult, ALU.subtract).then_inc(m.sem["c_ready"], 1)
        e.wait_ge(m.sem["turned"], m.at("turned", 1))
        nc.vector.tensor_copy(m.small[:, 16:16 + ST * FH], m.ps[:, 0, 0:ST * FH]).then_inc(m.sem["ct_ready"], 1)

    def end(self):
        self.norm.end()
        self.sp.end()
        finish(self.m, v_taken=2, c_ready=1, turned=1, ct_ready=1)


class Attention(Stage):

    taken = "exp_ready"

    def prev(self, p, j, lag):
        if j >= lag:
            return p, j - lag
        return (p - 1 if isinstance(p, int) else (p[0], p[1] - 1)), j - lag + self.per

    def s(self, p, j):
        return val(p) * self.per + j

    def setup_views(self):
        m = self.m
        v = m.misc
        self.lg = [v[:, i * S:(i + 1) * S] for i in (8, 9)]
        self.pb = [v[:, i * S:(i + 1) * S] for i in (10, 11)]
        self.pt = [v[:, i * S:(i + 1) * S] for i in (12, 13)]
        self.nm = m.small[:, 100:104]
        self.rs = m.small[:, 104:108]
        self.ri = m.small[:, 108:110]

    def logits(self, e, p, j):
        m, nc, s, t = self.m, self.m.nc, self.s(p, j), j % ST
        if due(s - 1):
            e.wait_ge(m.sem[self.taken], m.at(self.taken, s - 1))
        q, k = self.q(p, j), self.k(p, j)
        nc.tensor.matmul(m.ps[:, 4 + j % 2, 0:(t + 1) * P], q[:, t * P:(t + 1) * P], k[:, 0:(t + 1) * P], start=True, stop=False)
        nc.tensor.matmul(m.ps[:, 4 + j % 2, t * P:(t + 1) * P], m.identb[:], m.futureb[:], start=False, stop=True).then_inc(m.sem["logits_ready"], 1)

    def turn(self, e, p, j):
        m, nc, s, t = self.m, self.m.nc, self.s(p, j), j % ST
        e.wait_ge(m.sem["exp_ready"], m.at("exp_ready", s + 1))
        if due(s):
            e.wait_ge(m.sem["pt_ready"], m.at("pt_ready", s))
        for b in range(t + 1):
            last = nc.tensor.transpose(m.ps[:, 6, b * P:(b + 1) * P], self.pb[j % 2][:, b * P:(b + 1) * P], m.c("ident"))
        last.then_inc(m.sem["p_turned"], 1)

    def times_v(self, e, p, j):
        m, nc, s, t = self.m, self.m.nc, self.s(p, j), j % ST
        e.wait_ge(m.sem["pt_ready"], m.at("pt_ready", s + 1))
        if due(s):
            e.wait_ge(m.sem["o_taken"], m.at("o_taken", s))
        o = m.ps[:, 7, (j % 2) * 64:(j % 2) * 64 + 64]
        for b in range(t + 1):
            last = nc.tensor.matmul(o, self.pt[j % 2][:, b * P:(b + 1) * P], self.v(p, j, b), start=b == 0, stop=b == t)
        last.then_inc(m.sem["pv_done"], 1)

    def exp(self, e, p, j):
        m, nc, s, t = self.m, self.m.nc, self.s(p, j), j % ST
        n = (t + 1) * P
        e.wait_ge(m.sem["max_ready"], m.at("max_ready", s + 1))
        if due(s - 1):
            e.wait_ge(m.sem["p_turned"], m.at("p_turned", s - 1))
        last = nc.scalar.activation(self.pb[j % 2][:, 0:n], self.logit_src(j)[:, 0:n], ACT.Exp, bias=self.nm[:, j % 4:j % 4 + 1],
                                    scale=self.scale, accum_out=self.rs[:, j % 4:j % 4 + 1])
        last.then_inc(m.sem["exp_ready"], 1)

    def copy_turned(self, e, p, j):
        m, nc, s, t = self.m, self.m.nc, self.s(p, j), j % ST
        e.wait_ge(m.sem["p_turned"], m.at("p_turned", s + 1))
        if due(s - 1):
            e.wait_ge(m.sem["pv_done"], m.at("pv_done", s - 1))
        nc.scalar.activation(self.pt[j % 2][:, 0:(t + 1) * P], m.ps[:, 6, 0:(t + 1) * P], ACT.Copy).then_inc(m.sem["pt_ready"], 1)

    def output(self, e, p, j):
        m, nc, s, t = self.m, self.m.nc, self.s(p, j), j % ST
        e.wait_ge(m.sem["pv_done"], m.at("pv_done", s + 1))
        m.dve(e, nc.vector.reciprocal(self.ri[:, j % 2:j % 2 + 1], self.rs[:, j % 4:j % 4 + 1]))
        nc.vector.tensor_scalar(self.out(p, j), m.ps[:, 7, (j % 2) * 64:(j % 2) * 64 + 64], self.ri[:, j % 2:j % 2 + 1], None, ALU.mult).then_inc(m.sem["o_taken"], 1)

    def run(self, e, chain, per, now, later, prologue):
        prologue()

        def unit(p):
            first = isinstance(p, int) and p == 0
            for j in range(self.per):
                now(p, j)
                for lag, piece in later:
                    if not (first and j < lag):
                        piece(e, *self.prev(p, j, lag))
        unit(0)
        n2 = (self.units - 2) // 2
        if chain:
            with chain.loop(e, n2, per * 2) as i:
                for u in range(2):
                    unit((i, 1 + u))
        else:
            with e.Fori(0, n2) as i:
                for u in range(2):
                    unit((i, 1 + u))
        for p in range(1 + 2 * n2, self.units):
            unit(p)
        for j in range(max(lag for lag, _ in later)):
            for lag, piece in later:
                if j < lag:
                    piece(e, *self.prev(self.units, j, lag))

    def finish_steps(self):
        n = self.units * self.per
        finish(self.m, logits_taken=n, logits_ready=n, exp_ready=n, pt_ready=n, p_turned=n, o_taken=n, pv_done=n, max_ready=n)


class FoxAttention(Attention):
    n = units = FH // 2
    per = 2 * ST
    scale = 1.0
    taken = "logits_taken"

    def __init__(self, m, l):
        super().__init__(m)
        self.l = l
        self.wv = m.d["fox_w_in"][l].rearrange("(k p) n -> p k n", p=P)
        self.setup_views()
        v = m.misc
        self.qs = [v[:, i * S:(i + 1) * S] for i in (0, 1)]
        self.ks = [v[:, i * S:(i + 1) * S] for i in (2, 3)]
        self.ck = [[v[:, (4 + 2 * i + h) * S:(5 + 2 * i + h) * S] for h in range(2)] for i in range(2)]
        self.cm = [v[0:FH, i * S:(i + 1) * S] for i in (14, 15)]
        self.c16 = v[0:FH, 16 * S:17 * S]

    def load(self, j, slot):
        v = slot[:, 0:DK * 256].rearrange("p (k g n) -> p k g n", k=DK, g=2)
        return [(v[:, :, g, :], self.wv[:, :, bass.ds(j * P + g * D, P)]) for g in range(2)]

    def q(self, p, j):
        h = j // ST * 64
        return self.qs[par(p)][h:h + 64, :]

    def k(self, p, j):
        h = j // ST * 64
        return self.ks[par(p)][h:h + 64, :]

    def v(self, p, j, b):
        return self.m.tok_v[:, b, bass.ds(val(p) * P + (j // ST) * 64, 64)]

    def out(self, p, j):
        return self.m.tok_out[:, j % ST, bass.ds(val(p) * P + (j // ST) * 64, 64)]

    def logit_src(self, j):
        return self.lg[j % 2]

    def nxt(self, p):
        return p + 1 if isinstance(p, int) else (p[0], p[1] + 1)

    def project(self, e, p, ks):
        m, nc = self.m, self.m.nc
        slot = (self.c0 + par(p)) % 2
        v = m.w[slot][:, 0:DK * 256].rearrange("p (k g n) -> p k g n", k=DK, g=2)
        for k in ks:
            if k == 0:
                self.landed(e, p, slot)
            for g in range(2):
                last = nc.tensor.matmul(m.ps[:, g, :], v[:, k, g, :], m.h[:, k, :], start=k == 0, stop=k == DK - 1)
            if k == DK - 1:
                last.then_inc(m.chunk_done, 1)

    def spread(self, e, p):
        m, nc = self.m, self.m.nc
        e.wait_ge(m.sem["cm_ready"], m.at("cm_ready", val(p) + 1))
        for h in range(2):
            last = nc.tensor.matmul(m.ps[:, 2 + h, :], m.ones[0:FH, :], self.cm[h], start=True, stop=True)
        last.then_inc(m.sem["ck_done"], 1)

    def tensor(self, e):
        m = self.m
        split = {0: (0, 1), 1: (2, 3), 2: (4,), 3: (5,), 4: (6,), 5: (7,)}

        def prologue():
            self.project(e, 0, range(DK))
            self.spread(e, 0)

        def now(p, j):
            if j == 0:
                e.wait_ge(m.sem["q_staged"], m.at("q_staged", val(p) + 1))
                e.wait_ge(m.sem["k_staged"], m.at("k_staged", val(p) + 1))
            self.logits(e, p, j)
            if not (isinstance(p, int) and p == self.units - 1):
                self.project(e, self.nxt(p), split.get(j, ()))
                if j == 6:
                    self.spread(e, self.nxt(p))
        self.run(e, None, 0, now, [(1, self.turn), (2, self.times_v)], prologue)

    def stage_act(self, e, p):
        m, nc = self.m, self.m.nc
        e.wait_ge(m.chunk_done, val(p) + (self.c0 + 1))
        nc.scalar.activation(self.qs[par(p)], m.ps[:, 0, :], ACT.Copy, scale=64 ** -0.5)
        e.wait_ge(m.sem["ck_done"], m.at("ck_done", val(p) + 1))
        for h in range(2):
            last = nc.scalar.activation(self.ck[par(p)][h], m.ps[:, 2 + h, :], ACT.Copy)
        last.then_inc(m.sem["q_staged"], 1)

    def scalar(self, e):
        def now(p, j):
            self.exp(e, p, j)
            if j == 6 and not (isinstance(p, int) and p == self.units - 1):
                self.stage_act(e, self.nxt(p))
        self.run(e, None, 0, now, [(1, self.copy_turned)], lambda: self.stage_act(e, 0))

    def masked_c(self, e, p):
        m, nc = self.m, self.m.nc
        if due(val(p)):
            e.wait_ge(m.sem["ck_done"], m.at("ck_done", val(p)))
        for h in range(2):
            last = nc.vector.tensor_scalar(self.cm[h], self.c16, m.c("ident")[0:FH, bass.ds(val(p) * 2 + h, 1)], None, ALU.mult)
        last.then_inc(m.sem["cm_ready"], 1)

    def stage_dve(self, e, p):
        m, nc = self.m, self.m.nc
        e.wait_ge(m.chunk_done, val(p) + (self.c0 + 1))
        nc.vector.tensor_copy(self.ks[par(p)], m.ps[:, 1, :]).then_inc(m.sem["k_staged"], 1)

    def vector(self, e):
        m, nc = self.m, self.m.nc

        def prologue():
            self.masked_c(e, 0)
            self.stage_dve(e, 0)

        def now(p, j):
            s, t, n = self.s(p, j), j % ST, (j % ST + 1) * P
            if j == 0:
                e.wait_ge(m.sem["q_staged"], m.at("q_staged", val(p) + 1))
            e.wait_ge(m.sem["logits_ready"], m.at("logits_ready", s + 1))
            if due(s - 1):
                e.wait_ge(m.sem["exp_ready"], m.at("exp_ready", s - 1))
            cq = m.small[:, bass.ds(val(p) * 2 + (16 + t * FH + j // ST), 1)]
            nc.vector.scalar_tensor_tensor(self.lg[j % 2][:, 0:n], m.ps[:, 4 + j % 2, 0:n], cq, self.ck[par(p)][j // ST][:, 0:n], ALU.add, ALU.subtract).then_inc(m.sem["logits_taken"], 1)
            e.wait_ge(m.sem["logits_taken"], m.at("logits_taken", s + 1))
            nc.vector.tensor_reduce(self.nm[:, j % 4:j % 4 + 1], self.lg[j % 2][:, 0:n], AX.X, ALU.max, negate=True).then_inc(m.sem["max_ready"], 1)
            if not (isinstance(p, int) and p == self.units - 1):
                if j == 4:
                    self.masked_c(e, self.nxt(p))
                if j == 6:
                    self.stage_dve(e, self.nxt(p))
        self.run(e, m.dve, self.per, now, [(2, self.output)], prologue)

    def end(self):
        self.finish_steps()
        finish(self.m, q_staged=self.n, k_staged=self.n, cm_ready=self.n, ck_done=self.n)


class Linear(Stage):

    def __init__(self, m, w, norm, dst):
        super().__init__(m)
        self.norm, self.dst = norm, dst
        self.n = w.shape[1] // 512
        self.wv = w.rearrange("(k p) n -> p k n", p=P)

    def load(self, j, slot):
        return [(slot[:, 0:DK * 512].rearrange("p (k n) -> p k n", k=DK), self.wv[:, :, bass.ds(j * 512, 512)])]

    def tensor(self, e):
        m, nc = self.m, self.m.nc
        self.norm.tensor(e)
        for j in range(self.n):
            slot = (self.c0 + j) % 2
            self.landed(e, j, slot)
            if due(j - 1):
                e.wait_ge(m.sem["quad_taken"], m.at("quad_taken", j - 1))
            v = m.w[slot][:, 0:DK * 512].rearrange("p (k n) -> p k n", k=DK)
            for k in range(DK):
                if j == 0:
                    e.wait_ge(m.sem["h_ready"], m.at("h_ready", k + 1))
                for b in range(4):
                    last = nc.tensor.matmul(m.ps[:, 4 * (j % 2) + b, :], v[:, k, b * P:(b + 1) * P], m.h[:, k, :], start=k == 0, stop=k == DK - 1)
            last.then_inc(m.chunk_done, 1)

    def scalar(self, e):
        m, nc = self.m, self.m.nc
        self.norm.scalar(e)
        for j in range(self.n):
            e.wait_ge(m.chunk_done, self.c0 + j + 1)
            nc.scalar.activation(self.dst(j), m.ps[:, 4 * (j % 2):4 * (j % 2) + 4, :], ACT.Copy).then_inc(m.sem["quad_taken"], 1)

    def vector(self, e):
        self.norm.vector(e)

    def end(self):
        self.norm.end()
        finish(self.m, quad_taken=self.n)


class PoolMix(Stage):
    n = 1

    def __init__(self, m, norm):
        super().__init__(m)
        self.norm = norm

    def load(self, j, slot):
        return [(slot[:, 0:2048].rearrange("p (k n) -> p k n", k=8), self.m.d["pool_w"].rearrange("l g (k p) n -> p (l g k) n", p=P))]

    def gpsimd(self, e):
        m = self.m
        m.nc.gpsimd.memset(m.misc[:, 0:4 * 544], 0.0).then_inc(m.sem["pads_clear"], 1)

    def tensor(self, e):
        m, nc = self.m, self.m.nc
        self.norm.tensor(e)
        self.landed(e, 0, self.c0 % 2)
        v = m.w[self.c0 % 2][:, 0:2048].rearrange("p (k n) -> p k n", k=8)
        for o in range(DK):
            g, b = o // 2, o % 2
            if b == 0:
                e.wait_ge(m.sem["diff_ready"], m.at("diff_ready", g + 1))
            for k in range(2):
                last = nc.tensor.matmul(m.ps[:, o, :], v[:, 2 * g + k, b * P:(b + 1) * P], m.act[:, 2 * g + k, :], start=k == 0, stop=k == 1)
            if o < DK - 1:
                last.then_inc(m.sem["pooled"], 1)
        last.then_inc(m.chunk_done, 1)

    def scalar(self, e):
        m, nc = self.m, self.m.nc
        self.norm.scalar(e)
        for o in range(DK):
            if o < DK - 1:
                e.wait_ge(m.sem["pooled"], m.at("pooled", o + 1))
            else:
                e.wait_ge(m.chunk_done, self.c0 + 1)
            nc.scalar.activation(m.act[:, 8 + o, :], m.ps[:, o, :], ACT.Identity, bias=m.col("pool_b", o)).then_inc(m.sem["biased"], 1)

    def vector(self, e):
        m, nc = self.m, self.m.nc
        self.norm.vector(e)
        e.wait_ge(m.sem["h_ready"], m.at("h_ready", DK))
        e.wait_ge(m.sem["pads_clear"], m.at("pads_clear", 1))
        bufs = [m.misc[:, i * 1088:(i + 1) * 1088].rearrange("p (a n) -> p a n", a=2) for i in range(2)]
        for g, w in enumerate(WINDOWS):
            hg = m.h[:, 2 * g:2 * g + 2, :]
            a = bufs[0]
            nc.vector.tensor_copy(a[:, :, 16:17], hg[:, :, 0:1])
            m.dve(e, nc.vector.tensor_tensor(a[:, :, 17:528], hg[:, :, 1:512], hg[:, :, 0:511], ALU.add))
            lag = 2
            for i in range(g):
                a, b = bufs[i % 2], bufs[(i + 1) % 2]
                m.dve(e, nc.vector.tensor_tensor(b[:, :, 16:528], a[:, :, 16:528], a[:, :, 16 - lag:528 - lag], ALU.add))
                a, lag = b, lag * 2
            dst = m.act[:, 2 * g:2 * g + 2, :]
            m.dve(e, nc.vector.tensor_tensor(dst[:, :, 0:16], a[:, :, 16:32], m.c("rc")[:, 16 * g:16 * g + 16].rearrange("p (a n) -> p a n", a=1).broadcast_to([P, 2, 16]), ALU.mult))
            nc.vector.scalar_tensor_tensor(dst[:, :, 16:512], a[:, :, 32:528], 1.0 / w, hg[:, :, 16:512], ALU.mult, ALU.subtract)
            nc.vector.tensor_tensor(dst[:, :, 0:16], dst[:, :, 0:16], hg[:, :, 0:16], ALU.subtract).then_inc(m.sem["diff_ready"], 1)
            e.wait_ge(m.sem["diff_ready"], m.at("diff_ready", g + 1))
        for o in range(DK):
            e.wait_ge(m.sem["biased"], m.at("biased", o + 1))
            last = nc.vector.scalar_tensor_tensor(m.x[:, o, :], m.act[:, 8 + o, :], m.col("pool_s", o), m.x[:, o, :], ALU.mult, ALU.add)
        m.dve(e, last)

    def end(self):
        self.norm.end()
        finish(self.m, pads_clear=1, diff_ready=4, pooled=DK - 1, biased=DK)


class Gelu:

    def __init__(self, m):
        self.m = m

    def scalar(self, e):
        m, nc = self.m, self.m.nc
        for k in range(DK):
            nc.scalar.activation(m.h[:, k, :], m.h[:, k, :], ACT.Gelu_apprx_tanh).then_inc(m.sem["h_ready"], 1)

    def tensor(self, e): pass
    def vector(self, e): pass

    def end(self):
        finish(self.m, h_ready=DK)


def s5_buffers(m):
    v = {}
    at = 0
    for name, n in (("e2c", 2048), ("e2s", 2048), ("e1c", 256), ("e1s", 256), ("bbr", 512), ("bbi", 512), ("cr", 512), ("ci", 512),
                    ("btr", 512), ("bti", 512), ("t0", 512), ("t1", 512), ("t2", 512)):
        v[name] = m.misc[:, at:at + n]
        at += n
    for i in range(14):
        v[f"a{i}"] = m.act[:, 8 + i, :]
    return v


class S5Prepare(Stage):

    def sync(self, e):
        m, d = self.m, self.m.d
        b = s5_buffers(m)
        ld = m.count("s5_loaded")
        rows = b["a0"]
        e.dma_start(rows[0:32, 0:128], d["s5_a_re"].rearrange("l (i g) p -> (l i) (g p)", g=2)).then_inc(ld.sem, 16)
        e.dma_start(rows[0:32, 128:256], d["s5_a_im"].rearrange("l (i g) p -> (l i) (g p)", g=2)).then_inc(ld.sem, 16)
        e.dma_start(rows[0:32, 256:258], d["s5_log_dt"].rearrange("l (i g) -> (l i) g", g=2)).then_inc(ld.sem, 16)
        for k, name in (("a2", "s5_b_re"), ("a3", "s5_b_im")):
            e.dma_start(b[k].rearrange("q (i c) -> q i c", c=C5), d[name].rearrange("l g p c -> (l g p) c").rearrange("(i q) c -> q i c", q=P)).then_inc(ld.sem, 16)
        for k, name in (("cr", "s5_c_re"), ("ci", "s5_c_im")):
            e.dma_start(b[k].rearrange("r (q p) -> r q p", p=N5), d[name].rearrange("l g c p -> (l g c) p").rearrange("(q r) p -> r q p", r=P)).then_inc(ld.sem, 16)

    def tensor(self, e):
        m, nc = self.m, self.m.nc
        b = s5_buffers(m)
        e.wait_ge(m.sem["s5_rows"], m.at("s5_rows", 1))
        src = (b["a0"][0:32, 0:128], b["a0"][0:32, 128:256], b["a1"][0:32, 0:128])
        for i in range(3):
            last = nc.tensor.transpose(m.ps[:, 0, 32 * i:32 * i + 32], src[i], m.c("ident")[0:32, 0:32])
        last.then_inc(m.sem["turned"], 1)

    def scalar(self, e):
        m, nc = self.m, self.m.nc
        sm = self.cols()
        e.wait_ge(m.sem["s5_step"], m.at("s5_step", 1))
        m.acts(e, nc.scalar.activation(sm["dt"], sm["dt"], ACT.Exp))
        nc.scalar.activation(sm["z"], sm["dt"], ACT.Copy).then_inc(m.sem["s5_act"], 1)
        e.wait_ge(m.sem["s5_step"], m.at("s5_step", 2))
        nc.scalar.activation(sm["er"], sm["er"], ACT.Exp)
        nc.scalar.activation(sm["sn"], sm["sn"], ACT.Sin)
        nc.scalar.activation(sm["cs"], sm["cs"], ACT.Sin).then_inc(m.sem["s5_act"], 1)

    def cols(self):
        names = ("ar", "ai", "dt", "er", "cs", "sn", "t", "k", "den", "nr", "ni", "z")
        v = {n: self.m.small[:, 128 + 32 * i:160 + 32 * i] for i, n in enumerate(names)}
        return v

    def vector(self, e):
        m, nc = self.m, self.m.nc
        b, sm = s5_buffers(m), self.cols()
        tt, ts, stt = nc.vector.tensor_tensor, nc.vector.tensor_scalar, nc.vector.scalar_tensor_tensor
        do = lambda ins: m.dve(e, ins)
        e.wait_ge(m.sem["s5_loaded"], m.at("s5_loaded", 16 * 7))
        nc.vector.tensor_copy(b["a1"][0:32, 0:128].rearrange("p (g n) -> p g n", g=2), b["a0"][0:32, 256:258].rearrange("p (g n) -> p g n", n=1).broadcast_to([32, 2, 64])).then_inc(m.sem["s5_rows"], 1)
        e.wait_ge(m.sem["turned"], m.at("turned", 1))
        do(nc.vector.tensor_copy(m.small[:, 128:224], m.ps[:, 0, 0:96]))
        nc.vector.tensor_copy(sm["t"], sm["ar"]).then_inc(m.sem["s5_step"], 1)
        e.wait_ge(m.sem["s5_act"], m.at("s5_act", 1))
        do(tt(sm["er"], sm["ar"], sm["dt"], ALU.mult))
        do(tt(sm["t"], sm["ai"], sm["dt"], ALU.mult))
        do(ts(sm["k"], sm["t"], 1 / TWO_PI, 12582912.0, ALU.mult, ALU.add))
        do(ts(sm["k"], sm["k"], -12582912.0, None, ALU.add))
        for part in TURN_PARTS:
            do(stt(sm["t"], sm["k"], -part, sm["t"], ALU.mult, ALU.add))
        do(ts(sm["sn"], sm["t"], PI_IN, -PI_IN, ALU.min, ALU.max))
        do(ts(sm["cs"], sm["sn"], -1.0, None, ALU.mult))
        do(tt(sm["cs"], sm["cs"], sm["sn"], ALU.max))
        ts(sm["cs"], sm["cs"], -1.0, float(np.pi / 2), ALU.mult, ALU.add).then_inc(m.sem["s5_step"], 1)
        e.wait_ge(m.sem["s5_act"], m.at("s5_act", 2))
        do(tt(sm["nr"], sm["er"], sm["cs"], ALU.mult))
        do(ts(sm["nr"], sm["nr"], -1.0, None, ALU.add))
        do(tt(sm["ni"], sm["er"], sm["sn"], ALU.mult))
        do(tt(sm["den"], sm["ar"], sm["ar"], ALU.mult))
        do(tt(sm["t"], sm["ai"], sm["ai"], ALU.mult))
        do(tt(sm["den"], sm["den"], sm["t"], ALU.add))
        do(nc.vector.reciprocal(sm["den"], sm["den"]))
        do(tt(sm["t"], sm["nr"], sm["ar"], ALU.mult))
        do(tt(sm["k"], sm["ni"], sm["ai"], ALU.mult))
        do(tt(sm["t"], sm["t"], sm["k"], ALU.add))
        do(tt(sm["k"], sm["ni"], sm["ar"], ALU.mult))
        do(tt(sm["z"], sm["nr"], sm["ai"], ALU.mult))
        do(tt(sm["k"], sm["k"], sm["z"], ALU.subtract))
        do(tt(sm["t"], sm["t"], sm["den"], ALU.mult))
        do(tt(sm["k"], sm["k"], sm["den"], ALU.mult))
        wide = lambda a, n: a.rearrange("p (i a) -> p i a", a=1).broadcast_to([P, 32, n])
        three = lambda a, n: a.rearrange("p (i a) -> p i a", a=n)
        br, bi, t0 = three(b["a2"], C5), three(b["a3"], C5), three(b["a4"], C5)
        for out, p0, p1, op in (("bbr", (sm["t"], br), (sm["k"], bi), ALU.subtract), ("bbi", (sm["t"], bi), (sm["k"], br), ALU.add)):
            do(tt(three(b[out], C5), p0[1], wide(p0[0], C5), ALU.mult))
            do(tt(t0, p1[1], wide(p1[0], C5), ALU.mult))
            do(tt(three(b[out], C5), three(b[out], C5), t0, op))
        for ec, es, n, top in ((three(b["e2c"], 64), three(b["e2s"], 64), 1, 64), (three(b["e1c"], 8), three(b["e1s"], 8), 1, 8)):
            do(nc.vector.memset(ec[:, :, 0:1], 1.0))
            do(nc.vector.memset(es[:, :, 0:1], 0.0))
            while n < top:
                t = b["a5"][:, 0:32 * n] if n <= 16 else m.sg[:, :, :, :].rearrange("p a b s -> p (a b s)")[:, 0:32 * n]
                t = three(t, n)
                wc, ws = wide(sm["cs"], n), wide(sm["sn"], n)
                do(tt(ec[:, :, n:2 * n], ec[:, :, 0:n], wc, ALU.mult))
                do(tt(t, es[:, :, 0:n], ws, ALU.mult))
                do(tt(ec[:, :, n:2 * n], ec[:, :, n:2 * n], t, ALU.subtract))
                do(tt(es[:, :, n:2 * n], es[:, :, 0:n], wc, ALU.mult))
                do(tt(t, ec[:, :, 0:n], ws, ALU.mult))
                do(tt(es[:, :, n:2 * n], es[:, :, n:2 * n], t, ALU.add))
                do(tt(sm["t"], sm["cs"], sm["cs"], ALU.mult))
                do(tt(sm["k"], sm["sn"], sm["sn"], ALU.mult))
                do(stt(sm["sn"], sm["sn"], 2.0, sm["cs"], ALU.mult, ALU.mult))
                do(tt(sm["cs"], sm["t"], sm["k"], ALU.subtract))
                n *= 2

    def end(self):
        finish(self.m, s5_loaded=16 * 7, s5_rows=1, turned=1, s5_step=2, s5_act=2)


class S5Scan(Stage):

    TILES = 4

    def tensor(self, e):
        m, nc = self.m, self.m.nc
        b = s5_buffers(m)
        bt = [b[k].rearrange("p (r n) -> p r n", r=4) for k in ("btr", "bti")]
        ct = self.ct()

        def turn_b(q):
            e.wait_ge(m.sem["bin_ready"], m.at("bin_ready", q + 1))
            for i in range(2):
                last = nc.tensor.transpose(m.ps[:, 6, i * P:(i + 1) * P], self.tin()[i], m.c("ident"))
            last.then_inc(m.sem["b_turned"], 1)

        def turn_c(q):
            e.wait_ge(m.sem["cin_ready"], m.at("cin_ready", q + 1))
            for i in range(2):
                last = nc.tensor.transpose(m.ps[:, 7, i * P:(i + 1) * P], self.tin()[2 + i], m.c("ident"))
            last.then_inc(m.sem["c_turned"], 1)

        def bu(q, r):
            if r == 0:
                e.wait_ge(m.sem["bt_ready"], m.at("bt_ready", q + 1))
            if due(q * 4 + (r - 1)):
                e.wait_ge(m.sem["bu_taken"], m.at("bu_taken", q * 4 + (r - 1)))
            for i in range(2):
                last = nc.tensor.matmul(m.ps[:, 2 * (r % 2) + i, :], bt[i][:, r, :], m.act[:, bass.ds(q, 1), :].rearrange("p a s -> p (a s)"), start=True, stop=True)
            last.then_inc(m.sem["bu_ready"], 1)

        def y(q, r):
            e.wait_ge(m.sem["x_ready"], m.at("x_ready", q * 4 + (r + 1)))
            if r == 0:
                e.wait_ge(m.sem["ct_ready5"], m.at("ct_ready5", q + 1))
                if due(q):
                    e.wait_ge(m.sem["y_taken"], m.at("y_taken", q))
            for n, (prod, i) in enumerate(((0, 0), (1, 0), (2, 1), (3, 1))):
                last = nc.tensor.matmul(m.ps[32 * r:32 * r + 32, 4, :], ct[i][:, 32 * r:32 * r + 32], self.prod(r)[prod], start=n == 0, stop=n == 3)
            last.then_inc(m.sem["y_ready"], 1)

        def tile(q, final):
            turn_c(q)
            for r in range(4):
                if r < 3:
                    bu(q, r + 1)
                elif not final:
                    turn_b(q + 1)
                    bu(q + 1, 0)
                y(q, r)
        turn_b(0)
        bu(0, 0)
        tile(0, False)
        with e.Fori(0, DK - 2) as i:
            tile(i + 1, False)
        tile(DK - 1, True)

    def tin(self):
        b = s5_buffers(self.m)
        return [b["t0"][:, i * P:(i + 1) * P] for i in range(4)]

    def ct(self):
        b = s5_buffers(self.m)
        return [b["t1"][:, i * P:(i + 1) * P] for i in range(2)]

    def prod(self, r):
        b = s5_buffers(self.m)
        return [b[f"a{4 * (r % 2) + i}"] for i in range(4)]

    def tab(self, r):
        b = s5_buffers(self.m)
        return [b[f"a{8 + 2 * (r % 2) + i}"] for i in range(2)]

    def gpsimd(self, e):
        m, nc = self.m, self.m.nc
        b = s5_buffers(m)
        tt = nc.gpsimd.tensor_tensor
        tmp = m.sg[:, 0, :, :]
        v3 = lambda a: a.rearrange("p (a b) -> p a b", a=8)

        def table(q, r):
            if due(q * 4 + (r - 1)):
                e.wait_ge(m.sem["x_ready"], m.at("x_ready", q * 4 + (r - 1)))
            c, s = (v3(t) for t in self.tab(r))
            t0, t1 = v3(tmp[:, 0, :]), v3(tmp[:, 1, :])
            at = q * 4 + r
            e2 = [b[k].rearrange("p (i b a) -> p i a b", i=32, a=1)[:, bass.ds(at, 1), :, :].rearrange("p i a b -> p (i a) b").broadcast_to([P, 8, 64]) for k in ("e2c", "e2s")]
            e1 = [b[k].rearrange("p (i a b) -> p i a b", i=32, b=1)[:, bass.ds(at, 1), :, :].rearrange("p i a b -> p (i a) b").broadcast_to([P, 8, 64]) for k in ("e1c", "e1s")]
            tt(m.small[:, 121:122], m.eps[:], m.eps[:], ALU.add)
            tt(c, e1[0], e2[0], ALU.mult)
            tt(t0, e1[1], e2[1], ALU.mult)
            tt(s, e1[1], e2[0], ALU.mult)
            m.pool(e, tt(t1, e1[0], e2[1], ALU.mult))
            tt(c, c, t0, ALU.subtract)
            m.pool(e, tt(s, s, t1, ALU.add))

        for r in range(4):
            table(0, r)
        with m.pool.loop(e, DK - 1, 4 * 2) as i:
            for r in range(4):
                table(i + 1, r)

    def vector(self, e):
        m, nc = self.m, self.m.nc
        b = s5_buffers(m)
        tt, ts, stt = nc.vector.tensor_tensor, nc.vector.tensor_scalar, nc.vector.scalar_tensor_tensor
        tin, ct = self.tin(), self.ct()
        half = m.c("half").rearrange("p (r g c) -> p r g c", r=4, g=2)
        rowm = m.rowmask[:, :].rearrange("p (r a) -> p r a", a=1).broadcast_to([P, 4, P])
        t = [m.sg[:, 1, 0, :], m.sg[:, 1, 1, :], m.sq[:, 0, :], m.sq[:, 1, :]]
        er = S5Prepare.cols(self)["er"]

        def prep_b(q):
            for i, k in enumerate(("bbr", "bbi")):
                src = b[k].rearrange("p (i g c) -> p i g c", i=32, g=1)[:, bass.ds(q * 4, 4), :, :].broadcast_to([P, 4, 2, C5])
                last = tt(tin[i].rearrange("p (r g c) -> p r g c", r=4, g=2), src, half, ALU.mult)
            last.then_inc(m.sem["bin_ready"], 1)
            e.wait_ge(m.sem["b_turned"], m.at("b_turned", q + 1))
            for i, k in enumerate(("btr", "bti")):
                src = m.ps[:, 6, i * P:(i + 1) * P].rearrange("p (a n) -> p a n", a=1).broadcast_to([P, 4, P])
                last = tt(b[k].rearrange("p (r n) -> p r n", r=4), rowm, src, ALU.mult)
            last.then_inc(m.sem["bt_ready"], 1)

        def prep_c(q):
            for i, k in enumerate(("cr", "ci")):
                src = b[k].rearrange("p (q a n) -> p q a n", q=8, a=1)[:, bass.ds(q, 1), :, :].rearrange("p q a n -> p (q a) n").broadcast_to([P, 2, N5])
                last = ts(tin[2 + i].rearrange("p (a n) -> p a n", a=2), src, 1.0, None, ALU.mult)
            last.then_inc(m.sem["cin_ready"], 1)
            e.wait_ge(m.sem["c_turned"], m.at("c_turned", q + 1))
            stt(ct[0], m.ps[:, 7, 0:P], 1.0, m.c("half"), ALU.mult, ALU.mult)
            stt(ct[1], m.ps[:, 7, P:2 * P], -1.0, m.c("half"), ALU.mult, ALU.mult).then_inc(m.sem["ct_ready5"], 1)

        def scan(q, r):
            c, s = self.tab(r)
            o = self.prod(r)
            n = 2 * (r % 2)
            br, bi = m.ps[:, n, :], m.ps[:, n + 1, :]
            e.wait_ge(m.sem["bu_ready"], m.at("bu_ready", q * 4 + (r + 1)))
            e.wait_ge(m.pool.sem, (q * 4 + (r + 1)) * 2 + self.pool0)
            if due(q * 4 + r):
                e.wait_ge(m.sem["x_ready"], m.at("x_ready", q * 4 + r))
            tt(t[0], br, c, ALU.mult)
            tt(t[1], bi, s, ALU.mult)
            tt(t[2], bi, c, ALU.mult)
            m.dve(e, tt(t[3], br, s, ALU.mult))
            tt(t[0], t[0], t[1], ALU.add).then_inc(m.sem["bu_taken"], 1)
            m.dve(e, tt(t[2], t[2], t[3], ALU.subtract))
            rr = er[:, bass.ds(q * 4 + r, 1)].broadcast_to([P, S])
            nc.vector.tensor_tensor_scan(t[1], rr, t[0], 0.0, ALU.mult, ALU.add)
            m.dve(e, nc.vector.tensor_tensor_scan(t[3], rr, t[2], 0.0, ALU.mult, ALU.add))
            if due(q * 4 + (r - 1)):
                e.wait_ge(m.sem["y_ready"], m.at("y_ready", q * 4 + (r - 1)))
            tt(o[0], t[1], c, ALU.mult)
            stt(o[1], t[3], -1.0, s, ALU.mult, ALU.mult)
            tt(o[2], t[1], s, ALU.mult)
            tt(o[3], t[3], c, ALU.mult).then_inc(m.sem["x_ready"], 1)

        def tile(q, final):
            for r in range(4):
                scan(q, r)
                if r == 2 and not final:
                    e.wait_ge(m.sem["bu_ready"], m.at("bu_ready", q * 4 + 4))
                    prep_b(q + 1)
            e.wait_ge(m.sem["y_ready"], m.at("y_ready", q * 4 + 4))
            dcol = m.cols[:, bass.ds(q + COL["s5_d"], 1)]
            one = lambda a: a[:, bass.ds(q, 1), :].rearrange("p a s -> p (a s)")
            stt(one(m.h), one(m.act), dcol, m.ps[:, 4, :], ALU.mult, ALU.add).then_inc(m.sem["y_taken"], 1)

        prep_b(0)
        prep_c(0)
        tile(0, False)
        with m.dve.loop(e, DK - 2, 4 * 3) as i:
            prep_c(i + 1)
            tile(i + 1, False)
        prep_c(DK - 1)
        tile(DK - 1, True)

    def end(self):
        n = 4 * DK
        finish(self.m, bin_ready=DK, cin_ready=DK, b_turned=DK, c_turned=DK, bt_ready=DK, ct_ready5=DK, bu_ready=n, bu_taken=n,
               x_ready=n, y_ready=n, y_taken=DK)


class Ada(Stage):
    n = 6 * D // 512

    def __init__(self, m, l):
        super().__init__(m)
        self.l = l
        self.wv = m.d["w_ada_2"][l].rearrange("(k p) n -> p k n", p=P)

    def load(self, j, slot):
        return [(slot[:, 0:DK * 512].rearrange("p (k n) -> p k n", k=DK), self.wv[:, :, bass.ds(j * 512, 512)])]

    def sync(self, e):
        m, d = self.m, self.m.d
        if self.l:
            return
        ld = m.count("second_loaded")
        with m.nc.allow_non_contiguous_dma(reason="short parameter vectors"):
            e.dma_start(m.wdt[:, 0], d["w_in_2"][0][:, D_DT:].rearrange("(k p) n -> p k n", p=P)).then_inc(ld.sem, 16)
            e.dma_start(m.wdt[:, 1], d["w_in_2"][1][:, D_DT:].rearrange("(k p) n -> p k n", p=P)).then_inc(ld.sem, 16)
            for l in range(2):
                for i, name in enumerate(("dt_bias_2", "a_log_2")):
                    e.dma_start(m.heads[0:MH, 2 * l + i:2 * l + i + 1], d[name][l].rearrange("(h a) -> h a", a=1)).then_inc(ld.sem, 16)
                for i, name in enumerate(("q", "k")):
                    e.dma_start(m.qkn[0:NOPE, 2 * l + i:2 * l + i + 1], d[name + "_nope_norm_w_2"][l].rearrange("(h a) -> h a", a=1)).then_inc(ld.sem, 16)
                    e.dma_start(m.qkn[NOPE:QH, 2 * l + i:2 * l + i + 1], d[name + "_pe_norm_w_2"][l].rearrange("(h a) -> h a", a=1)).then_inc(ld.sem, 16)
            for h in range(2):
                src = d["d_skip_2"].rearrange("l (t h) -> h (l t)", h=2)[h:h + 1, :].broadcast_to([64, 8])
                e.dma_start(m.dskip[64 * h:64 * h + 64, :], src).then_inc(ld.sem, 16)
            e.dma_start(m.misc.bitcast(I32)[0:QH, 0:S], d["positions_2"].broadcast_to([QH, S])).then_inc(ld.sem, 16)

    def tensor(self, e):
        m, nc = self.m, self.m.nc
        e.wait_ge(m.sem["c_active"], m.at("c_active", 1))

        def chunk(j):
            slot = (self.c0 + par(j)) % 2
            self.landed(e, j, slot)
            if not (isinstance(j, int) and j < 2):
                e.wait_ge(m.sem["mod_taken"], m.at("mod_taken", val(j) - 1))
            v = m.w[slot][:, 0:DK * 512].rearrange("p (k n) -> p k n", k=DK)
            for b in range(4):
                for k in range(DK):
                    last = nc.tensor.matmul(m.ps[:, par(j), b:b + 1], v[:, k, b * P:(b + 1) * P], m.cact[:, k:k + 1], start=k == 0, stop=k == DK - 1)
            last.then_inc(m.chunk_done, 1)
        pairs(e, self.n, 2, chunk)

    def scalar(self, e):
        m, nc = self.m, self.m.nc
        nc.scalar.activation(m.cact[:], m.cols[:, COL["c"]:COL["c"] + DK], ACT.Silu).then_inc(m.sem["c_active"], 1)
        if self.l == 0:
            e.wait_ge(m.sem["angles"], m.at("angles", 1))
            for i in range(2):
                nc.scalar.activation(m.rope[0:QH, i, :], m.rope[0:QH, i, :], ACT.Sin).then_inc(m.sem["sines"], 1)

    def vector(self, e):
        m, nc = self.m, self.m.nc
        tt, ts, stt = nc.vector.tensor_tensor, nc.vector.tensor_scalar, nc.vector.scalar_tensor_tensor
        if self.l == 0:
            do = lambda ins: m.dve(e, ins)
            a, k = m.sg[0:QH, 0, 0, :], m.sg[0:QH, 0, 1, :]
            c, s = m.rope[0:QH, 0, :], m.rope[0:QH, 1, :]
            e.wait_ge(m.sem["second_loaded"], m.at("second_loaded", 16 * 17))
            do(nc.vector.tensor_copy(a, m.misc.bitcast(I32)[0:QH, 0:S]))
            do(ts(a, a, m.c("inv")[0:QH, :], None, ALU.mult))
            do(ts(k, a, 1 / TWO_PI, 12582912.0, ALU.mult, ALU.add))
            do(ts(k, k, -12582912.0, None, ALU.add))
            for part in TURN_PARTS:
                do(stt(a, k, -part, a, ALU.mult, ALU.add))
            do(ts(s, a, PI_IN, -PI_IN, ALU.min, ALU.max))
            do(ts(c, s, -1.0, None, ALU.mult))
            do(tt(c, c, s, ALU.max))
            ts(c, c, -1.0, float(np.pi / 2), ALU.mult, ALU.add).then_inc(m.sem["angles"], 1)
            e.wait_ge(m.sem["sines"], m.at("sines", 2))
            nc.vector.memset(m.rope[0:NOPE, 0, :], 1.0)
            do(nc.vector.memset(m.rope[0:NOPE, 1, :], 0.0))
        b0 = COL["b_ada"] + 48 * self.l

        def chunk(j):
            e.wait_ge(m.chunk_done, val(j) + (self.c0 + 1))
            tt(m.mod[:, self.l, bass.ds(val(j) * 4, 4)], m.ps[:, par(j), 0:4], m.cols[:, bass.ds(val(j) * 4 + b0, 4)], ALU.add).then_inc(m.sem["mod_taken"], 1)
        pairs(e, self.n, 2, chunk)
        e.wait_ge(m.sem["mod_taken"], m.at("mod_taken", self.n))
        for i, name in enumerate(("norm1", "norm2")):
            last = stt(m.gains[:, self.l, i, :], m.mod[:, self.l, 24 * i + 8:24 * i + 16], 1.0,
                       m.cols[:, COL[name] + 8 * self.l:COL[name] + 8 * self.l + 8], ALU.add, ALU.mult)
        m.dve(e, last)

    def end(self):
        finish(self.m, c_active=1, mod_taken=self.n)
        if self.l == 0:
            finish(self.m, second_loaded=16 * 17, angles=1, sines=2)


class SecondIn(Stage):
    n = 4

    def __init__(self, m, l, norm):
        super().__init__(m)
        self.l, self.norm = l, norm
        self.wv = m.d["w_in_2"][l].rearrange("(k p) n -> p k n", p=P)
        g = m.sg
        self.sp = Softplus(m, g[0:MH, 0, 0, :], g[0:MH, 0, 1, :], g[0:MH, 1, 0, :], g[0:MH, 1, 1, :])
        self.span = [(0, D_ZI), (D_ZI, 512), (D_XBC, 512), (D_XBC + 512, 512)]
        self.tiles = [[(0, P), (P, P), (2 * P, P), (D_ZI - QH, QH)]] + [[(b * P, P) for b in range(4)]] * 3
        self.pad = m.act[:, 4:13, :].rearrange("p a s -> p (a s)")[:, 0:8 * 515].rearrange("p (a n) -> p a n", a=8)

    def load(self, j, slot):
        a, n = self.span[j]
        return [(slot[:, 0:DK * n].rearrange("p (k n) -> p k n", k=DK), self.wv[:, :, a:a + n])]

    def gpsimd(self, e):
        m = self.m
        m.nc.gpsimd.memset(self.pad[:, :, 0:3], 0.0).then_inc(m.sem["pads_clear"], 1)

    def tensor(self, e):
        m, nc = self.m, self.m.nc
        self.norm.tensor(e)
        for j in range(4):
            slot = (self.c0 + j) % 2
            self.landed(e, j, slot)
            if j == 1:
                e.wait_ge(m.sem["sp_y"], m.at("sp_y", 1))
            if due(j - 1):
                e.wait_ge(m.sem["quad_taken"], m.at("quad_taken", j - 1))
            n = self.span[j][1]
            v = m.w[slot][:, 0:DK * n].rearrange("p (k n) -> p k n", k=DK)
            for k in range(DK):
                if j == 0:
                    e.wait_ge(m.sem["h_ready"], m.at("h_ready", k + 1))
                for b, (c, w) in enumerate(self.tiles[j]):
                    last = nc.tensor.matmul(m.ps[0:w, 4 * (j % 2) + b, :], v[:, k, c:c + w], m.h[:, k, :], start=k == 0, stop=k == DK - 1)
                if j == 0:
                    last = nc.tensor.matmul(m.ps[0:MH, 4, :], m.wdt[:, self.l, k, :], m.h[:, k, :], start=k == 0, stop=k == DK - 1)
            last.then_inc(m.chunk_done, 1)

    def scalar(self, e):
        m, nc = self.m, self.m.nc
        self.norm.scalar(e)
        q = m.count("quad_taken")
        e.wait_ge(m.chunk_done, self.c0 + 1)
        nc.scalar.activation(m.misc[:, 0:3 * S].rearrange("p (a s) -> p a s", a=3), m.ps[:, 0:3, :], ACT.Copy)
        nc.scalar.activation(m.misc[NOPE:QH, 3 * S:4 * S], m.ps[NOPE:QH, 3, :], ACT.Copy).then_inc(q.sem, 1)
        self.sp.scalar(e)
        e.wait_ge(m.chunk_done, self.c0 + 2)
        nc.scalar.activation(m.act[:, 0:4, :], m.ps[:, 4:8, :], ACT.Silu).then_inc(q.sem, 1)
        e.wait_ge(m.sem["pads_clear"], m.at("pads_clear", 1))
        for j in range(2):
            e.wait_ge(m.chunk_done, self.c0 + 3 + j)
            nc.scalar.activation(self.pad[:, 4 * j:4 * j + 4, 3:515], m.ps[:, 4 * j:4 * j + 4, :], ACT.Copy).then_inc(q.sem, 1)
        for t in range(8):
            e.wait_ge(m.sem["conv_ready"], m.at("conv_ready", t + 1))
            last = nc.scalar.activation(m.act[:, 13 + t, :], m.act[:, 13 + t, :], ACT.Silu, bias=m.col("conv_b", 8 * self.l + t))
        m.acts(e, last)

    def vector(self, e):
        m, nc = self.m, self.m.nc
        self.norm.vector(e)
        e.wait_ge(m.chunk_done, self.c0 + 1)
        nc.vector.tensor_scalar(self.sp.y, m.ps[0:MH, 4, :], m.heads[0:MH, 2 * self.l:2 * self.l + 1], None, ALU.add).then_inc(m.sem["sp_y"], 1)
        e.wait_ge(m.sem["sp_y"], m.at("sp_y", 1))
        self.sp.vector(e)
        for t in range(8):
            if t % 4 == 0:
                e.wait_ge(m.sem["quad_taken"], m.at("quad_taken", 3 + t // 4))
            w = lambda i: m.col("conv_w", (CONVW * self.l + i) * 8 + t)
            o = m.act[:, 13 + t, :]
            m.dve(e, nc.vector.tensor_scalar(o, self.pad[:, t, 0:S], w(0), None, ALU.mult))
            for i in range(1, CONVW):
                ins = nc.vector.scalar_tensor_tensor(o, self.pad[:, t, i:i + S], w(i), o, ALU.mult, ALU.add)
                if i < CONVW - 1:
                    m.dve(e, ins)
            ins.then_inc(m.sem["conv_ready"], 1)

    def end(self):
        self.norm.end()
        self.sp.end()
        finish(self.m, quad_taken=4, conv_ready=8, pads_clear=1)


class Ssd(Stage):

    def __init__(self, m, l):
        super().__init__(m)
        self.l = l
        mi, ac = m.misc, m.act
        sl = lambda i: mi[:, i * S:(i + 1) * S]
        self.adt, self.acs, self.cmask = m.sg[0:MH, 0, 0, :], m.sg[0:MH, 0, 1, :], m.sg[0:MH, 1, 0, :]
        self.dt = m.sg[0:MH, 1, 1, :]
        self.am = [ac[0:MH, 21, :], m.rstd[0:MH, :]]
        self.btok = mi[:, 4 * S:6 * S].rearrange("p (g c n) -> p g c n", g=2, c=ST)
        self.cb = [sl(6), sl(7)]
        self.eh, self.lh, self.sc, self.cth = [sl(8), sl(9)], [sl(10), sl(11)], [sl(12), sl(13)], [sl(14), sl(15)]
        self.st = [None, sl(16), sl(17), ac[:, 12, :]]
        self.xdt, self.xdtd = [ac[:, 4 + t, :] for t in range(4)], [ac[:, 8 + t, :] for t in range(4)]
        self.xs = lambda t: ac[:, 13 + t, :]
        self.bT = lambda g: ac[:, 17 + g, :]
        self.cT = lambda g: ac[:, 19 + g, :]
        sm = m.small
        self.dtT, self.acsT = sm[:, 0:32], sm[:, 32:64]
        self.nacs, self.dec, self.cd = sm[:, 64:96], sm[:, 96:128], sm[:, 128:160]
        self.na = sm[0:MH, 160:161]

    def tensor(self, e):
        m, nc = self.m, self.m.nc
        ident = m.c("ident")
        tr, mm = nc.tensor.transpose, nc.tensor.matmul
        ps = m.ps
        for g in range(2):
            for c in range(ST):
                cs = slice(c * P, (c + 1) * P)
                last = mm(ps[:, g, cs], self.bT(g)[:, cs], self.cT(g)[:, cs], start=True, stop=True)
            last.then_inc(m.sem["cb_done"], 1)
        for g in range(2):
            for c in range(ST):
                last = tr(ps[:, 2 + g, c * P:(c + 1) * P], self.bT(g)[:, c * P:(c + 1) * P], ident)
            last.then_inc(m.sem["bt_done"], 1)
        for c in range(ST):
            for t in range(4):
                last = tr(ps[:, 4 + c, t * P:(t + 1) * P], self.xs(t)[:, c * P:(c + 1) * P], ident)
            last.then_inc(m.sem["xt_done"], 1)
        e.wait_ge(m.sem["acs_ready"], m.at("acs_ready", 1))
        e.wait_ge(m.sem["cb_ready"], m.at("cb_ready", 1))
        for i, src in enumerate((self.dt, self.acs)):
            for c in range(ST):
                last = tr(ps[:, 0, 32 * i + 8 * c:32 * i + 8 * c + 8], src[:, c * P:(c + 1) * P], ident[0:MH, 0:MH])
        last.then_inc(m.sem["rows_turned"], 1)
        e.wait_ge(m.sem["acsT_ready"], m.at("acsT_ready", 1))
        e.wait_ge(m.sem["cb_ready"], m.at("cb_ready", 2))
        mm(ps[:, 1, 0:32], m.c("last"), self.acsT, start=True, stop=True).then_inc(m.sem["last_spread"], 1)
        for c in range(ST - 1):
            e.wait_ge(m.sem["xdtd_ready"], m.at("xdtd_ready", c + 1))
            e.wait_ge(m.sem["bt_ready2"], m.at("bt_ready2", 2))
            if due(c - 1):
                e.wait_ge(m.sem["st_ready"], m.at("st_ready", c - 1))
            for g in range(2):
                last = mm(ps[:, 2 + c % 2, g * 256:(g + 1) * 256], self.btok[:, g, c, :], self.xdtd[c][:, g * 256:(g + 1) * 256], start=True, stop=True)
            last.then_inc(m.sem["st_done"], 1)

        def spread(h):
            b = 6 if h % 2 else 0
            e.wait_ge(m.sem["am_ready"], m.at("am_ready", h + 1))
            if h == 0:
                e.wait_ge(m.sem["decay_ready"], m.at("decay_ready", 1))
            if h == 1:
                e.wait_ge(m.sem["xdt_ready"], m.at("xdt_ready", ST))
            if due(h - 1):
                e.wait_ge(m.sem["l_ready"], m.at("l_ready", h - 1))
            mm(ps[:, b, :], m.ones[0:MH, :], self.am[h % 2], start=True, stop=True).then_inc(m.sem["bc_ready"], 1)
            mm(ps[:, b + 1, :], m.ones[0:MH, :], self.am[h % 2], start=True, stop=False)
            mm(ps[:, b + 1, :], m.identb[:], m.pastb[:].rearrange("p (a n) -> p a n", a=1).broadcast_to([P, ST, P]), start=False, stop=True).then_inc(m.sem["bm_ready"], 1)

        def out(h):
            bank = 4 + (h // 2) % 2
            e.wait_ge(m.sem["sc_ready"], m.at("sc_ready", h + 1))
            e.wait_ge(m.sem["cth_ready"], m.at("cth_ready", h + 1))
            e.wait_ge(m.sem["st_ready"], m.at("st_ready", ST - 1))
            if h == 0:
                e.wait_ge(m.sem["xdt_ready"], m.at("xdt_ready", ST))
            if due(h // 2 - 1):
                e.wait_ge(m.sem["y_gated"], m.at("y_gated", h // 2 - 1))
            r = 64 * (h % 2)
            for c in range(ST):
                cs, hs = slice(c * P, (c + 1) * P), slice(h * 64, (h + 1) * 64)
                last = mm(ps[r:r + 64, bank, cs], self.xdt[c][:, hs], self.sc[h % 2][:, cs], start=True, stop=c == 0)
                if c:
                    last = mm(ps[r:r + 64, bank, cs], self.st[c][:, hs], self.cth[h % 2][:, cs], start=False, stop=True)
            last.then_inc(m.sem["yh_done"], 1)

        spread(0)
        for h in range(MH):
            if h + 1 < MH:
                spread(h + 1)
            out(h)
        for t in range(4):
            e.wait_ge(m.sem["ysq_ready"], m.at("ysq_ready", t + 1))
            last = mm(ps[:, 2 + t // 2, :], m.ones[:], m.sq[:, t % 2, :], start=t % 2 == 0, stop=t % 2 == 1)
            last.then_inc(m.sem["ysq_used"], 1)

    def scalar(self, e):
        m, nc = self.m, self.m.nc
        act = nc.scalar.activation
        act(self.na, m.heads[0:MH, 2 * self.l + 1:2 * self.l + 2], ACT.Exp).then_inc(m.sem["a_ready"], 1)
        for g in range(2):
            e.wait_ge(m.sem["cb_done"], m.at("cb_done", g + 1))
            act(self.cb[g], m.ps[:, g, :], ACT.Copy).then_inc(m.sem["cb_ready"], 1)
        for g in range(2):
            e.wait_ge(m.sem["bt_done"], m.at("bt_done", g + 1))
            act(self.btok[:, g], m.ps[:, 2 + g, :].rearrange("p (c n) -> p c n", c=ST), ACT.Copy).then_inc(m.sem["bt_ready2"], 1)
        e.wait_ge(m.sem["last_spread"], m.at("last_spread", 1))
        act(self.cd, m.ps[:, 1, 0:32], ACT.Exp).then_inc(m.sem["cd_ready"], 1)
        e.wait_ge(m.sem["dec_arg"], m.at("dec_arg", 1))
        act(self.dec, self.dec, ACT.Exp).then_inc(m.sem["decay_ready"], 1)
        for h in range(MH):
            b = 6 if h % 2 else 0
            e.wait_ge(m.sem["bc_ready"], m.at("bc_ready", h + 1))
            if due(h - 1):
                e.wait_ge(m.sem["cth_ready"], m.at("cth_ready", h - 1))
            act(self.eh[h % 2], m.ps[:, b, :], ACT.Exp).then_inc(m.sem["e_ready"], 1)
            e.wait_ge(m.sem["bm_ready"], m.at("bm_ready", h + 1))
            if due(h - 1):
                e.wait_ge(m.sem["sc_ready"], m.at("sc_ready", h - 1))
            for c in range(ST):
                last = act(self.lh[h % 2][:, c * P:(c + 1) * P], m.ps[:, b + 1, c * P:(c + 1) * P], ACT.Exp, bias=self.nacs[:, 8 * c + h:8 * c + h + 1])
            last.then_inc(m.sem["l_ready"], 1)
        for t in range(4):
            e.wait_ge(m.sem["y_gated"], m.at("y_gated", t + 1))
            if due(t - 1):
                e.wait_ge(m.sem["ysq_used"], m.at("ysq_used", t - 1))
            act(m.sq[:, t % 2, :], m.h[:, 4 + t, :], ACT.Square).then_inc(m.sem["ysq_ready"], 1)
            if t % 2:
                e.wait_ge(m.sem["ysq_used"], m.at("ysq_used", t + 1))
                act(self.eh[t // 2], m.ps[:, 2 + t // 2, :], ACT.Sqrt, bias=m.eps[:, 0:1], scale=1 / 256).then_inc(m.sem["ystd_ready"], 1)

    def gpsimd(self, e):
        m, nc = self.m, self.m.nc
        tt = nc.gpsimd.tensor_tensor
        for h in range(MH):
            g = h // 4
            e.wait_ge(m.sem["e_ready"], m.at("e_ready", h + 1))
            if due(h - 1):
                e.wait_ge(m.sem["yh_done"], m.at("yh_done", h - 1))
            tt(self.cth[h % 2], self.cT(g), self.eh[h % 2], ALU.mult).then_inc(m.sem["cth_ready"], 1)

    def vector(self, e):
        m, nc = self.m, self.m.nc
        tt, ts, stt = nc.vector.tensor_tensor, nc.vector.tensor_scalar, nc.vector.scalar_tensor_tensor
        do = lambda ins: m.dve(e, ins)
        e.wait_ge(m.sem["a_ready"], m.at("a_ready", 1))
        do(nc.vector.memset(self.cmask, 1.0))
        do(nc.vector.memset(self.cmask.rearrange("p (c n) -> p c n", c=ST)[:, :, 0:1], 0.0))
        do(ts(self.na, self.na, -1.0, None, ALU.mult))
        do(ts(self.adt, self.dt, self.na, None, ALU.mult))
        nc.vector.tensor_tensor_scan(self.acs, self.cmask, self.adt, 0.0, ALU.mult, ALU.add).then_inc(m.sem["acs_ready"], 1)
        e.wait_ge(m.sem["rows_turned"], m.at("rows_turned", 1))
        nc.vector.tensor_copy(m.small[:, 0:64], m.ps[:, 0, 0:64]).then_inc(m.sem["acsT_ready"], 1)
        e.wait_ge(m.sem["acsT_ready"], m.at("acsT_ready", 1))
        do(ts(self.nacs, self.acsT, -1.0, None, ALU.mult))
        e.wait_ge(m.sem["cd_ready"], m.at("cd_ready", 1))
        tt(self.dec, m.ps[:, 1, 0:32], self.acsT, ALU.subtract).then_inc(m.sem["dec_arg"], 1)
        wide = lambda a: a.rearrange("p (h a) -> p h a", a=1).broadcast_to([P, MH, 64])
        three = lambda a: a.rearrange("p (h n) -> p h n", h=MH)

        def am(h):
            if due(h - 1):
                e.wait_ge(m.sem["bm_ready"], m.at("bm_ready", h - 1))
            ts(self.am[h % 2], self.acs, m.c("ident")[0:MH, h:h + 1], None, ALU.mult).then_inc(m.sem["am_ready"], 1)
        am(0)
        am(1)
        for c in range(ST):
            e.wait_ge(m.sem["xt_done"], m.at("xt_done", c + 1))
            tt(three(self.xdt[c]), three(m.ps[:, 4 + c, :]), wide(self.dtT[:, 8 * c:8 * c + 8]), ALU.mult).then_inc(m.sem["xdt_ready"], 1)
        e.wait_ge(m.sem["decay_ready"], m.at("decay_ready", 1))
        e.wait_ge(m.sem["xdt_ready"], m.at("xdt_ready", ST))
        for c in range(ST - 1):
            tt(three(self.xdtd[c]), three(self.xdt[c]), wide(self.dec[:, 8 * c:8 * c + 8]), ALU.mult).then_inc(m.sem["xdtd_ready"], 1)
        for c in range(ST - 1):
            e.wait_ge(m.sem["st_done"], m.at("st_done", c + 1))
            bank = m.ps[:, 2 + c % 2, :]
            if c == 0:
                nc.vector.tensor_copy(self.st[1], bank).then_inc(m.sem["st_ready"], 1)
            else:
                e.wait_ge(m.sem["st_ready"], m.at("st_ready", c))
                do(tt(three(self.st[c + 1]), three(self.st[c]), wide(self.cd[:, 8 * c:8 * c + 8]), ALU.mult))
                tt(self.st[c + 1], self.st[c + 1], bank, ALU.add).then_inc(m.sem["st_ready"], 1)

        def gate(t):
            e.wait_ge(m.sem["yh_done"], m.at("yh_done", 2 * t + 2))
            y = m.h[:, 4 + t, :]
            do(stt(y, self.xs(t), m.dskip[:, 4 * self.l + t:4 * self.l + t + 1], m.ps[:, 4 + t % 2, :], ALU.mult, ALU.add))
            tt(y, y, m.act[:, t, :], ALU.mult).then_inc(m.sem["y_gated"], 1)

        for h in range(MH):
            e.wait_ge(m.sem["l_ready"], m.at("l_ready", h + 1))
            if due(h - 1):
                e.wait_ge(m.sem["yh_done"], m.at("yh_done", h - 1))
            tt(self.sc[h % 2], self.lh[h % 2], self.cb[h // 4], ALU.mult).then_inc(m.sem["sc_ready"], 1)
            if h + 2 < MH:
                am(h + 2)
            if h % 2 == 0 and h:
                gate(h // 2 - 1)
        gate(3)
        for g in range(2):
            e.wait_ge(m.sem["ystd_ready"], m.at("ystd_ready", g + 1))
            do(nc.vector.reciprocal(self.eh[g], self.eh[g]))
            for t in (2 * g, 2 * g + 1):
                last = stt(m.h[:, 4 + t, :], m.h[:, 4 + t, :], m.col("ssd_n", 4 * self.l + t), self.eh[g], ALU.mult, ALU.mult)
        do(last)

    def end(self):
        finish(self.m, cb_done=2, bt_done=2, xt_done=ST, acs_ready=1, cb_ready=2, rows_turned=1, acsT_ready=1, last_spread=1,
               xdtd_ready=ST - 1, bt_ready2=2, st_ready=ST - 1, st_done=ST - 1, am_ready=MH, decay_ready=1, xdt_ready=ST, l_ready=MH,
               bc_ready=MH, bm_ready=MH, sc_ready=MH, cth_ready=MH, y_gated=4, yh_done=MH, ysq_ready=4, ysq_used=4,
               a_ready=1, cd_ready=1, dec_arg=1, e_ready=MH, ystd_ready=2)


class LatentUp(Stage):
    n = 1
    ITEMS = 2 * MH

    def __init__(self, m, l):
        super().__init__(m)
        self.l = l
        mi = m.misc
        self.qa = [mi[:, i * S:(i + 1) * S] for i in range(3)]
        self.kpe = mi[NOPE:QH, 3 * S:4 * S]
        self.tok_v = mi[:, 4 * S:8 * S].rearrange("p (t n) -> p t n", t=ST)
        self.rs = [m.std, m.rstd]
        self.tmp = [mi[0:QH, 8 * S:9 * S], mi[0:QH, 9 * S:10 * S]]
        self.stat = mi[0:32, 10 * S:11 * S]
        self.item = lambda n: m.act[0:QH, 4 + n, :]

    def load(self, j, slot):
        d = self.m.d
        return [(slot[:, 0:1536].rearrange("p (k n) -> p k n", k=2), d["w_q_up_2"][self.l].rearrange("(k p) n -> p k n", p=P)),
                (slot[:, 1536:2560], d["w_kv_up_2"][self.l])]

    def tensor(self, e):
        m, nc = self.m, self.m.nc
        mm, ps = nc.tensor.matmul, m.ps
        for i in range(3):
            e.wait_ge(m.sem["lsq_ready"], m.at("lsq_ready", i + 1))
            mm(ps[:, i // 2, :], m.ones[:], m.sg[:, i // 2, i % 2, :], start=i != 1, stop=i != 0).then_inc(m.sem["lsq_used"], 1)
        slot = self.c0 % 2
        self.landed(e, 0, slot)
        wq = m.w[slot][:, 0:1536].rearrange("p (k n) -> p k n", k=2)
        wkv = m.w[slot][:, 1536:2560].rearrange("p (h n) -> p h n", h=MH)
        for n in range(self.ITEMS):
            h, bank = n % MH, 2 + n % 4
            if due(n - 3):
                e.wait_ge(m.sem["raw_taken"], m.at("raw_taken", n - 3))
            if n < MH:
                if n == 0:
                    e.wait_ge(m.sem["lat_ready"], m.at("lat_ready", 2))
                for k in range(2):
                    last = mm(ps[0:QH, bank, :], wq[:, k, h * QH:(h + 1) * QH], self.qa[k], start=k == 0, stop=k == 1)
            else:
                if n == MH:
                    e.wait_ge(m.sem["lat_ready"], m.at("lat_ready", 3))
                last = mm(ps[0:NOPE, bank, :], wkv[:, h, 0:NOPE], self.qa[2], start=True, stop=True)
            last.then_inc(m.sem["raw_ready"], 1)
            if n >= 1:
                self.stats(e, n - 1)
        self.stats(e, self.ITEMS - 1)
        for t in range(ST):
            if due(t - 1):
                e.wait_ge(m.sem["lv_taken"], m.at("lv_taken", t - 1))
            if t < 2:
                e.wait_ge(m.sem["lat_ready"], m.at("lat_ready", 3))
            last = mm(ps[:, t % 2, :], self.qa[2][:, t * P:(t + 1) * P], wkv[:, :, NOPE:P], start=True, stop=True)
            if t < ST - 1:
                last.then_inc(m.sem["lv_done"], 1)
        last.then_inc(m.chunk_done, 1)
        e.wait_ge(m.sem["stat_ready"], m.at("stat_ready", 1))
        for n in range(self.ITEMS):
            if due(n - 1):
                e.wait_ge(m.sem["normed"], m.at("normed", n - 1))
            if n < 2:
                e.wait_ge(m.sem["raw_taken"], m.at("raw_taken", self.ITEMS))
            mm(ps[0:QH, 2 + n % 2, :], m.spread[:, n * QH:(n + 1) * QH], self.stat, start=True, stop=True).then_inc(m.sem["stat_spread"], 1)
            if n >= 1:
                self.rotate(e, n - 1)
        self.rotate(e, self.ITEMS - 1)

    def stats(self, e, n):
        m = self.m
        e.wait_ge(m.sem["isq_ready"], m.at("isq_ready", n + 1))
        m.nc.tensor.matmul(m.ps[0:32, 6, :], m.gather[0:QH, 30 - 2 * n:62 - 2 * n], m.sg[0:QH, n % 2, 0, :], start=n == 0, stop=n == self.ITEMS - 1).then_inc(m.sem["isq_used"], 1)

    def rotate(self, e, n):
        m = self.m
        e.wait_ge(m.sem["normed"], m.at("normed", n + 1))
        if due(n - 1):
            e.wait_ge(m.sem["rot_taken"], m.at("rot_taken", n - 1))
        m.nc.tensor.matmul(m.ps[0:QH, 4 + n % 2, :], m.c("rot")[0:QH, 0:QH], self.item(n), start=True, stop=True).then_inc(m.sem["rot_done"], 1)

    def scalar(self, e):
        m, nc = self.m, self.m.nc
        act = nc.scalar.activation
        for i in range(3):
            act(m.sg[:, i // 2, i % 2, :], self.qa[i], ACT.Square).then_inc(m.sem["lsq_ready"], 1)
        for i, (n, w) in enumerate(((2, Q_LORA), (3, KV_LORA))):
            e.wait_ge(m.sem["lsq_used"], m.at("lsq_used", n))
            act(self.rs[i][:], m.ps[:, i, :], ACT.Sqrt, bias=m.eps[:, 0:1], scale=1 / w).then_inc(m.sem["lstd_ready"], 1)
        for n in range(self.ITEMS):
            rows = QH if n < MH else NOPE
            e.wait_ge(m.sem["raw_ready"], m.at("raw_ready", n + 1))
            if n < MH:
                act(self.item(n), m.ps[0:rows, 2 + n % 4, :], ACT.Copy).then_inc(m.sem["raw_taken"], 1)
            else:
                act(self.item(n)[0:NOPE], m.ps[0:rows, 2 + n % 4, :], ACT.Copy).then_inc(m.sem["raw_taken"], 1)
            e.wait_ge(m.sem["raw_taken"], m.at("raw_taken", n + 1))
            if due(n - 1):
                e.wait_ge(m.sem["isq_used"], m.at("isq_used", n - 1))
            if n >= MH:
                e.wait_ge(m.sem["kpe_copied"], m.at("kpe_copied", n - MH + 1))
            act(m.sg[0:QH, n % 2, 0, :], self.item(n), ACT.Square).then_inc(m.sem["isq_ready"], 1)
        for t in range(ST):
            if t < ST - 1:
                e.wait_ge(m.sem["lv_done"], m.at("lv_done", t + 1))
            else:
                e.wait_ge(m.chunk_done, self.c0 + 1)
            act(self.tok_v[:, t, :], m.ps[:, t % 2, :], ACT.Copy).then_inc(m.sem["lv_taken"], 1)
        e.wait_ge(m.sem["isq_used"], m.at("isq_used", self.ITEMS))
        act(self.stat, m.ps[0:32, 6, :], ACT.Sqrt, bias=m.eps[0:32, 0:1]).then_inc(m.sem["stat_std"], 1)

    def gpsimd(self, e):
        m, nc = self.m, self.m.nc
        for h in range(MH):
            nc.gpsimd.tensor_copy(self.item(MH + h)[NOPE:QH], self.kpe).then_inc(m.sem["kpe_copied"], 1)
        for n in range(self.ITEMS):
            e.wait_ge(m.sem["rot_done"], m.at("rot_done", n + 1))
            nc.gpsimd.tensor_tensor(self.item(n), self.item(n), m.rope[0:QH, 0, :], ALU.mult).then_inc(m.sem["cos_done"], 1)

    def vector(self, e):
        m, nc = self.m, self.m.nc
        tt, ts, stt = nc.vector.tensor_tensor, nc.vector.tensor_scalar, nc.vector.scalar_tensor_tensor
        for i, (tiles, name) in enumerate((((0, 1), "q_a"), ((2,), "kv_a"))):
            e.wait_ge(m.sem["lstd_ready"], m.at("lstd_ready", i + 1))
            m.dve(e, nc.vector.reciprocal(self.rs[i][:], self.rs[i][:]))
            for t in tiles:
                col = m.col(name, 2 * self.l + t) if i == 0 else m.col(name, self.l)
                stt(self.qa[t], self.qa[t], col, self.rs[i][:], ALU.mult, ALU.mult).then_inc(m.sem["lat_ready"], 1)
        e.wait_ge(m.sem["stat_std"], m.at("stat_std", 1))
        nc.vector.reciprocal(self.stat, self.stat).then_inc(m.sem["stat_ready"], 1)

        def rotated(n):
            e.wait_ge(m.sem["rot_done"], m.at("rot_done", n + 1))
            tt(self.tmp[n % 2], m.rope[0:QH, 1, :], m.ps[0:QH, 4 + n % 2, :], ALU.mult).then_inc(m.sem["rot_taken"], 1)
            e.wait_ge(m.sem["rot_taken"], m.at("rot_taken", n + 1))
            e.wait_ge(m.sem["cos_done"], m.at("cos_done", n + 1))
            m.dve(e, tt(self.item(n), self.item(n), self.tmp[n % 2], ALU.add))
        for n in range(self.ITEMS):
            e.wait_ge(m.sem["stat_spread"], m.at("stat_spread", n + 1))
            w = m.qkn[0:QH, 2 * self.l + n // MH:2 * self.l + n // MH + 1]
            stt(self.item(n), self.item(n), w, m.ps[0:QH, 2 + n % 2, :], ALU.mult, ALU.mult).then_inc(m.sem["normed"], 1)
            if n >= 1:
                rotated(n - 1)
        rotated(self.ITEMS - 1)

    def end(self):
        n = self.ITEMS
        finish(self.m, lsq_ready=3, lsq_used=3, raw_taken=n, raw_ready=n, lat_ready=3, lv_taken=ST, lv_done=ST - 1, stat_ready=1, normed=n,
               stat_spread=n, isq_ready=n, isq_used=n, rot_taken=n, rot_done=n, lstd_ready=2, kpe_copied=MH, stat_std=1, cos_done=n)


class LatentAttention(Attention):
    units = MH
    per = ST
    scale = 1.0
    n = 0

    def __init__(self, m, up):
        super().__init__(m)
        self.up = up
        self.setup_views()
        self.qs = [m.misc[0:QH, i * S:(i + 1) * S] for i in (8, 9)]
        self.tok = m.misc[:, 14 * S:18 * S].rearrange("p (t n) -> p t n", t=ST)

    def q(self, p, j):
        return self.qs[par(p)]

    def k(self, p, j):
        return self.m.act[0:QH, bass.ds(val(p) + 12, 1), :].rearrange("p a s -> p (a s)")

    def v(self, p, j, b):
        return self.up.tok_v[:, b, bass.ds(val(p) * 64, 64)]

    def out(self, p, j):
        return self.tok[:, j, bass.ds(val(p) * 64, 64)]

    def tensor(self, e):
        m = self.m

        def now(p, j):
            if j == 0:
                e.wait_ge(m.sem["q_staged"], m.at("q_staged", val(p) + 1))
            self.logits(e, p, j)
        self.run(e, None, 0, now, [(1, self.turn), (2, self.times_v)], lambda: None)

    def logit_src(self, j):
        return self.m.ps[:, 4 + j % 2, :]

    def stage(self, e, p):
        m, nc = self.m, self.m.nc
        src = m.act[0:QH, bass.ds(val(p) + 4, 1), :].rearrange("p a s -> p (a s)")
        nc.scalar.activation(self.qs[par(p)], src, ACT.Copy, scale=QH ** -0.5).then_inc(m.sem["q_staged"], 1)

    def scalar(self, e):
        def now(p, j):
            self.exp(e, p, j)
            if j == 2 and not (isinstance(p, int) and p == self.units - 1):
                self.stage(e, p + 1 if isinstance(p, int) else (p[0], p[1] + 1))
        self.run(e, None, 0, now, [(1, self.copy_turned)], lambda: self.stage(e, 0))

    def vector(self, e):
        m, nc = self.m, self.m.nc

        def now(p, j):
            s, n = self.s(p, j), (j + 1) * P
            e.wait_ge(m.sem["logits_ready"], m.at("logits_ready", s + 1))
            nc.vector.tensor_reduce(self.nm[:, j % 4:j % 4 + 1], m.ps[:, 4 + j % 2, 0:n], AX.X, ALU.max, negate=True).then_inc(m.sem["max_ready"], 1)
        self.run(e, m.dve, self.per, now, [(2, self.output)], lambda: None)

    def end(self):
        self.finish_steps()
        finish(self.m, q_staged=self.units)


class Setup(Stage):

    def sync(self, e):
        m, d = self.m, self.m.d
        self.loaded = m.count("x_loaded")
        self.par = m.count("params_loaded")
        e.dma_start(m.consts[:], d["consts"]).then_inc(self.par.sem, 16)
        e.dma_start(m.spread[:], d["spread"]).then_inc(self.par.sem, 16)
        e.dma_start(m.act[:, 0:8, :].rearrange("p a s -> p (a s)").rearrange("p (t d) -> p t d", t=ST),
                    d["x"].rearrange("a (t p) d -> p (a t) d", p=P)).then_inc(self.loaded.sem, 16)
        e.wait_ge(m.sem["filled"], 1)
        rows = m.act[:, 8, 0:384].rearrange("p (a n) -> p a n", a=3)

        def put(a, name, src):
            r = COL[name] % 128 if a < 2 else COL[name] - 256
            n = src.shape[0]
            e.dma_start(rows[r:r + n, a, :], src).then_inc(self.par.sem, 16)

        put(0, "mix", d["mix_norm_g"].rearrange("l (k p) -> (l k) p", p=P))
        put(0, "ffn", d["ffn_norm_g"].rearrange("l (k p) -> (l k) p", p=P))
        put(0, "final", d["final_norm_g"].rearrange("(k p) -> k p", p=P))
        put(0, "s5_d", d["s5_d"].rearrange("l (k p) -> (l k) p", p=P))
        put(0, "pool_b", d["pool_b"].rearrange("l (k p) -> (l k) p", p=P))
        put(0, "pool_s", d["pool_scale"].rearrange("l (k p) -> (l k) p", p=P))
        put(1, "norm1", d["norm1_w_2"].rearrange("l (k p) -> (l k) p", p=P))
        put(1, "norm2", d["norm2_w_2"].rearrange("l (k p) -> (l k) p", p=P))
        put(1, "b_ada", d["b_ada_2"].rearrange("l (k p) -> (l k) p", p=P))
        put(2, "q_a", d["q_a_norm_w_2"].rearrange("l (k p) -> (l k) p", p=P))
        put(2, "kv_a", d["kv_a_norm_w_2"].rearrange("l (k p) -> (l k) p", p=P))
        put(2, "conv_b", d["conv_b_2"].rearrange("l (k p) -> (l k) p", p=P))
        put(2, "ssd_n", d["ssd_norm_w_2"].rearrange("l (k p) -> (l k) p", p=P))
        put(2, "conv_w", d["conv_w_2"].rearrange("l w (k p) -> (l w k) p", p=P))
        put(2, "c", d["c_2"].rearrange("l (k p) -> (l k) p", p=P))
        for l in range(2):
            e.dma_start(m.wf[:, l], d["fox_w_in"][l, :, 3 * D:3 * D + FH].rearrange("(k p) n -> p k n", p=P)).then_inc(self.par.sem, 16)
        with m.nc.allow_non_contiguous_dma(reason="sixteen biases of heads"):
            for l in range(2):
                e.dma_start(m.small[0:FH, l:l + 1], d["fox_b_f"][l].rearrange("(h a) -> h a", a=1)).then_inc(self.par.sem, 16)

    def gpsimd(self, e):
        m, nc = self.m, self.m.nc
        r = m.count("filled")
        nc.gpsimd.memset(m.act[:, 8, 0:384], 0.0).then_inc(r.sem, 1)
        for n, (buf, value) in enumerate(((m.mean_w, 1.0 / D), (m.ones, 1.0), (m.eps, EPS), (m.ones16, 1.0))):
            e.wait_ge(r.sem, n + 1)
            nc.gpsimd.memset(buf[:], value).then_inc(r.sem, 1)

    def tensor(self, e):
        m, nc = self.m, self.m.nc
        moved, taken = m.count("turned"), m.count("turn_taken")
        e.wait_ge(self.loaded.sem, 16)
        e.wait_ge(self.par.sem, 16 * 21)
        e.wait_ge(m.sem["filled"], 5)
        xt = m.act[:, 0:8, :].rearrange("p a s -> p (a s)").rearrange("p (t d) -> p t d", t=ST)
        for k in range(DK):
            if k >= 4:
                e.wait_ge(taken.sem, taken.at(k - 3))
            for t in range(ST):
                last = nc.tensor.transpose(m.ps[:, k % 4, t * P:(t + 1) * P], xt[:, t, k * P:(k + 1) * P], m.c("ident"))
            last.then_inc(moved.sem, 1)
        for a in range(3):
            last = nc.tensor.transpose(m.ps[:, 4, a * P:(a + 1) * P], m.act[:, 8, a * P:(a + 1) * P], m.c("ident"))
        last.then_inc(moved.sem, 1)

    def vector(self, e):
        m, nc = self.m, self.m.nc
        moved, taken = m.count("turned"), m.count("turn_taken")
        e.wait_ge(self.par.sem, 16 * 21)
        nc.vector.tensor_reduce(m.rowmask[:], m.c("ident").rearrange("p (r n) -> p r n", r=4), AX.X, ALU.add)
        nc.vector.tensor_copy(m.identb[:], m.c("ident"))
        nc.vector.tensor_copy(m.futureb[:], m.c("future"))
        nc.vector.tensor_copy(m.pastb[:], m.c("past"))
        for k in range(DK):
            e.wait_ge(moved.sem, moved.at(k + 1))
            nc.vector.tensor_copy(m.x[:, k, :], m.ps[:, k % 4, :]).then_inc(taken.sem, 1)
        e.wait_ge(moved.sem, moved.at(DK + 1))
        nc.vector.tensor_copy(m.cols[:], m.ps[:, 4, 0:384]).then_inc(taken.sem, 1)

    def end(self):
        finish(self.m, turned=DK + 1, turn_taken=DK + 1, x_loaded=16, params_loaded=16 * 21, filled=5)


class Store(Stage):

    def tensor(self, e):
        m, nc = self.m, self.m.nc
        moved, taken = m.count("turned"), m.count("turn_taken")
        for t in range(ST):
            for f in range(2):
                n = 2 * t + f
                if n >= 4:
                    e.wait_ge(taken.sem, taken.at(n - 3))
                for k in range(4):
                    last = nc.tensor.transpose(m.ps[:, n % 4, k * P:(k + 1) * P], m.x[:, 4 * f + k, t * P:(t + 1) * P], m.c("ident"))
                last.then_inc(moved.sem, 1)

    def vector(self, e):
        m, nc = self.m, self.m.nc
        moved, taken = m.count("turned"), m.count("turn_taken")
        for n in range(8):
            e.wait_ge(moved.sem, moved.at(n + 1))
            nc.vector.tensor_copy(m.act[:, n, :], m.ps[:, n % 4, :]).then_inc(taken.sem, 1)

    def sync(self, e):
        m = self.m
        taken, stored = m.count("turn_taken"), m.count("stored")
        out = m.d["out"].rearrange("a (t p) (f n) -> (a t) f p n", p=P, f=2)
        for n in range(8):
            e.wait_ge(taken.sem, taken.at(n + 1))
            e.dma_start(out[n // 2, n % 2], m.act[:, n, :]).then_inc(stored.sem, 16)
        e.wait_ge(stored.sem, stored.at(128))


class FinalNorm(Stage):

    def __init__(self, m, norm):
        super().__init__(m)
        self.norm = norm
        norm.dst = lambda k: m.x[:, k, :]

    def tensor(self, e): self.norm.tensor(e)
    def scalar(self, e): self.norm.scalar(e)
    def vector(self, e): self.norm.vector(e)
    def end(self): self.norm.end()


def build(nc, d):
    with ExitStack() as ctx:
        m = Machine(nc, ctx, d)
        stages = [Setup(m)]
        stages += plan(m, d)
        stages.append(Store(m))
        n = 0
        for s in stages:
            s.c0 = n
            n += s.n
        issued = 0
        for s in stages:
            want = min(n, s.c0 + s.n + 2)
            todo = []
            for t in stages:
                a, b = max(issued, t.c0), min(want, t.c0 + t.n)
                if b > a:
                    todo.append((t.load, t.c0, a - t.c0, b - t.c0))
            issued = max(issued, want)
            stream = m.loads(todo)
            s.pool0 = m.pool.base + m.pool.k
            with nc.Block() as block:
                @block.sync
                def _(sp):
                    s.sync(sp)
                    stream(sp)

                @block.gpsimd
                def _(pool):
                    s.gpsimd(pool)

                @block.tensor
                def _(pe):
                    s.tensor(pe)

                @block.scalar
                def _(act):
                    s.scalar(act)

                @block.vector
                def _(dve):
                    s.vector(dve)
            s.end()


def plan(m, d):
    out = []
    for l in range(4):
        mix = Norm(m, lambda k, l=l: m.col("mix", 8 * l + k))
        if l % 3 == 0:
            out.append(FoxV(m, l // 3, mix))
            out.append(FoxAttention(m, l // 3))
            out.append(Project(m, d["fox_w_out"][l // 3], lambda k: m.h[:, k, :], turn=DK))
        elif l == 1:
            four = lambda j: m.act[:, 4 * j:4 * j + 4, :]
            out.append(Linear(m, d["s5_w_in"][0], mix, four))
            out.append(S5Prepare(m))
            out.append(S5Scan(m))
            out.append(GateUp(m, d["s5_w_glu"][0], D, Gelu(m), glu=True))
        else:
            out.append(PoolMix(m, mix))
        out.append(GateUp(m, d["ffn_w_gate_up"][l], FF, Norm(m, lambda k, l=l: m.col("ffn", 8 * l + k))))
        out.append(Project(m, d["ffn_w_down"][l], lambda k: m.act[:, k, :]))
    out.append(FinalNorm(m, Norm(m, lambda k: m.col("final", k))))
    for l in range(2):
        mod = lambda i, k, l=l: m.mod[:, l, 8 * i + k:8 * i + k + 1]
        gain = lambda i, k, l=l: m.gains[:, l, i, k:k + 1]
        out.append(Ada(m, l))
        out.append(SecondIn(m, l, Norm(m, lambda k, g=gain: g(0, k), lambda k, mod=mod: mod(0, k))))
        out.append(Ssd(m, l))
        up = LatentUp(m, l)
        out.append(up)
        att = LatentAttention(m, up)
        out.append(att)
        out.append(Project(m, d["w_out_2"][l], lambda k: m.h[:, k, :], turn=4, gate=lambda k, mod=mod: mod(2, k), tok=att.tok))
        out.append(GateUp(m, d["w_gate_up_2"][l], FF, Norm(m, lambda k, g=gain: g(1, k), lambda k, mod=mod: mod(3, k))))
        out.append(Project(m, d["w_down_2"][l], lambda k: m.act[:, k, :], gate=lambda k, mod=mod: mod(5, k)))
    return out


NAMES = ["x", "mix_norm_g", "ffn_norm_g", "final_norm_g", "fox_w_in", "fox_b_f", "fox_w_out", "s5_w_in", "s5_a_re",
         "s5_a_im", "s5_log_dt", "s5_b_re", "s5_b_im", "s5_c_re", "s5_c_im", "s5_d", "s5_w_glu", "pool_w", "pool_b",
         "pool_scale", "ffn_w_gate_up", "ffn_w_down", "c_2", "positions_2", "norm1_w_2", "norm2_w_2", "w_ada_2",
         "b_ada_2", "w_in_2", "q_a_norm_w_2", "w_q_up_2", "kv_a_norm_w_2", "w_kv_up_2", "q_nope_norm_w_2",
         "q_pe_norm_w_2", "k_nope_norm_w_2", "k_pe_norm_w_2", "conv_w_2", "conv_b_2", "dt_bias_2", "a_log_2",
         "d_skip_2", "ssd_norm_w_2", "w_out_2", "w_gate_up_2", "w_down_2"]


def kernel(**inputs):
    import concourse.bacc as _bacc
    from concourse.bass_utils import run_bass_kernel_spmd as _run

    nc = _bacc.Bacc("TRN2", target_bir_lowering=False, num_devices=1)
    arrays, d = {}, {}
    for name in NAMES:
        a = np.ascontiguousarray(inputs[name])
        arrays[f"in_{name}"] = a
        d[name] = nc.dram_tensor(f"in_{name}", a.shape, mybir.dt.from_np(a.dtype), kind="ExternalInput").ap()
    arrays["in_consts"] = CONSTS
    arrays["in_spread"] = SPREAD
    d["spread"] = nc.dram_tensor("in_spread", SPREAD.shape, F32, kind="ExternalInput").ap()
    d["consts"] = nc.dram_tensor("in_consts", CONSTS.shape, F32, kind="ExternalInput").ap()
    d["out"] = nc.dram_tensor("out_0", (1, S, D), F32, kind="ExternalOutput").ap()
    build(nc, d)
    r = _run(nc, [arrays], core_ids=[0])
    return r.results[0]["out_0"]
```

```python
from contextlib import ExitStack, contextmanager

import numpy as np

import concourse.bass as bass
from concourse import mybir

F32 = mybir.dt.float32
F32R = mybir.dt.float32r
BF16 = mybir.dt.bfloat16
I32 = mybir.dt.int32
ALU = mybir.AluOpType
ACT = mybir.ActivationFunctionType
AX = mybir.AxisListType

P = 128
S = 512
ST = S // P
D = 1024
DK = D // P
FF = 2816
FK = FF // P
EPS = 1e-6
FH = 16
G5, N5, C5 = 64, 64, 16
WINDOWS = (2, 4, 8, 16)
MH = 8
NOPE, ROPE = 64, 32
QH = NOPE + ROPE
Q_LORA, KV_LORA = 256, 128
D_ZI = Q_LORA + KV_LORA + ROPE
D_XBC = D_ZI + 512
D_DT = D_XBC + 1024
CONVW = 4
BIG = -1e30
SLOT = DK * 512
FH_K = FK // 2
HALF_SLOT = DK * 256
TWO_PI = 2 * np.pi
TURN_PARTS = (6.28125, 0.0019340515136718750, float(TWO_PI - 6.28125 - 0.0019340515136718750))
PI_IN = float(np.nextafter(np.float32(np.pi), np.float32(0)))


class Count:

    def __init__(self, sem):
        self.sem = sem
        self.done = 0

    def at(self, n):
        return n + self.done


SEMAPHORES = """
    diag_ready rms_spread ada_in ada_summed ada_done 
    w_hi_ready prod_done hi_ready
    h_ready turned sp_y sp_u sp_e sp_ln c_ready v_taken exp_ready pt_ready o_taken max_ready p_turned pv_done
    cm_ready q_staged k_staged ck_done logits_ready logits_taken quad_taken diff_ready pooled pads_clear
    biased s5_rows s5_step s5_loaded s5_act bin_ready cin_ready bt_ready bu_taken x_ready ct_ready5 y_taken
    b_turned c_turned bu_ready y_ready angles second_loaded sines conv_ready acs_ready
    cb_ready acsT_ready xdtd_ready bt_ready2 st_ready am_ready decay_ready xdt_ready l_ready sc_ready
    cth_ready y_gated ysq_ready cb_done bt_done last_spread dec_arg bc_ready bm_ready ysq_used e_ready yh_done
    a_ready rows_turned cd_ready xt_done st_done ystd_ready lsq_ready raw_taken lat_ready lv_taken stat_ready
    normed isq_ready rot_taken lsq_used raw_ready isq_used kpe_copied lv_done rot_done lstd_ready stat_std
    cos_done stat_spread ct_ready filled sq_ready sq_used std_ready h_scaled pair_taken half_ready out_taken
    x_loaded params_loaded turn_taken stored
""".split()


def due(n):
    return not isinstance(n, int) or n > 0


class Chain:

    def __init__(self, sem):
        self.sem, self.base, self.k = sem, 0, 0

    def __call__(self, eng, ins):
        self.k += 1
        ins.then_inc(self.sem, 1)
        eng.wait_ge(self.sem, self.base + self.k)

    @contextmanager
    def loop(self, eng, n, per):
        b = self.base + self.k
        with eng.Fori(0, n) as i:
            self.base, self.k = i * per + b, 0
            yield i
            assert self.k == per, (self.k, per)
        self.base, self.k = b + n * per, 0


def columns():
    at, n = {}, 0
    for name, rows in (("mix", 32), ("ffn", 32), ("final", 8), ("s5_d", 8), ("pool_b", 8), ("pool_s", 8)):
        at[name] = n
        n += rows
    n = 128
    for name, rows in (("norm1", 16), ("norm2", 16), ("b_ada", 96)):
        at[name] = n
        n += rows
    for name, rows in (("q_a", 4), ("kv_a", 2), ("conv_b", 16), ("ssd_n", 8), ("conv_w", 64), ("c", 8)):
        at[name] = n
        n += rows
    return at


COL = columns()


def shape_constants():
    ident = np.eye(P)
    rot = np.zeros((P, P))
    for i in range(ROPE // 2):
        rot[NOPE + ROPE // 2 + i, NOPE + i] = -1
        rot[NOPE + i, NOPE + ROPE // 2 + i] = 1
    last = np.zeros((P, P))
    last[P - 1] = 1
    future = np.where(np.arange(P)[None, :] > np.arange(P)[:, None], BIG, 0)
    half = (np.arange(P)[:, None] // N5 == (np.arange(P)[None, :] % 32) // C5).astype(float)
    rc = np.stack([1 / np.minimum(np.arange(16) + 1, w) for w in WINDOWS]).reshape(1, 64) * np.ones((P, 1))
    inv = (1.0 / (np.float32(10000.0) ** (np.arange(0, ROPE, 2, dtype=np.float32) / np.float32(ROPE)))).astype(np.float32)
    invc = np.zeros((P, 1))
    invc[NOPE:QH, 0] = np.tile(inv, 2)
    gather = np.zeros((P, 62))
    gather[:NOPE, 30] = 1 / NOPE
    gather[NOPE:QH, 31] = 1 / ROPE
    parts = dict(gather=gather, ident=ident, rot=rot, last=last, future=future, past=future.T, half=half, rc=rc, inv=invc)
    at, n = {}, 0
    for k, v in parts.items():
        at[k] = (n, n + v.shape[1])
        n += v.shape[1]
    return at, np.concatenate(list(parts.values()), axis=1).astype(np.float32)


CONST_AT, CONSTS = shape_constants()

SPREAD = np.zeros((32, 2 * MH, QH), np.float32)
for _n in range(2 * MH):
    SPREAD[2 * _n, _n, :NOPE] = 1
    SPREAD[2 * _n + 1, _n, NOPE:] = 1
SPREAD = SPREAD.reshape(32, -1)


class Machine:

    def __init__(self, nc, ctx, d):
        self.nc, self.d, self.ctx = nc, d, ctx

        def sb(name, shape, dt=F32):
            return ctx.enter_context(nc.sbuf_tensor(name, shape, dt))

        base = nc.sbuf_base
        base = ((base() if callable(base) else base) + 31) // 32 * 32
        sb("arena", [P, (2 * DK + FK) * S + 4 * HALF_SLOT])

        def at(name, floats, shape, dt=F32):
            return nc.alloc_sbuf_tensor_at(name, shape, dt, offset=base + 4 * floats)

        self.h = at("hT", 0, [P, DK, S])
        self.act = at("act", DK * S, [P, FK, S])
        self.misc = at("misc", (DK + FK) * S, [P, 18 * S])
        self.h_hi = at("h_hi", 0, [P, DK, S], F32R)
        self.h_lo = at("h_lo", DK * S, [P, DK, S], F32R)
        self.a_hi = at("a_hi", 2 * DK * S, [P, FH_K, S], F32R)
        self.a_lo = at("a_lo", (2 * DK + FH_K) * S, [P, FH_K, S], F32R)
        w0 = (2 * DK + FK) * S
        self.w_hi = [at(f"w_hi{i}", w0 + i * HALF_SLOT, [P, HALF_SLOT], F32R) for i in range(2)]
        self.w_lo = [at(f"w_lo{i}", w0 + (2 + i) * HALF_SLOT, [P, HALF_SLOT], F32R) for i in range(2)]
        self.x = sb("xT", [P, DK, S])
        self.w = [sb(f"w{i}", [P, SLOT]) for i in range(2)]
        self.sg = sb("sg", [P, 2, 2, S])
        self.sq = sb("sq", [P, 2, S])
        self.std = sb("std", [P, S])
        self.rstd = sb("rstd", [P, S])
        self.consts = sb("consts", [P, CONSTS.shape[1]])
        self.cols = sb("cols", [P, 384])
        self.mean_w = sb("mean_w", [P, P])
        self.ones = sb("ones", [P, P])
        self.identb = sb("identb", [P, P], BF16)
        self.futureb = sb("futureb", [P, P], BF16)
        self.pastb = sb("pastb", [P, P], BF16)
        self.eps = sb("eps", [P, 1])
        self.rms = sb("rms", [P, ST])
        self.diag = sb("diag", [P, ST, P])
        self.ada_w, self.ada_p = (w[:, HALF_SLOT:HALF_SLOT + 2 * DK * P].rearrange("p (b n) -> p b n", b=2) for w in self.w)
        self.wdt = sb("wdt", [P, 2, DK, MH])
        self.heads = sb("heads", [MH, 4])
        self.qkn = sb("qkn", [P, 4])
        self.dskip = sb("dskip", [P, 8])
        self.rope = sb("rope", [P, 2, S])
        self.cact = sb("cact", [P, DK])
        self.gains = sb("gains", [P, 2, 2, DK])
        self.gather = self.c("gather")
        self.spread = sb("spread", [32, 16 * QH])
        self.rowmask = sb("rowmask", [P, 4])
        self.ones16 = sb("ones16", [FH, S])
        self.small = sb("small", [P, 512])
        self.wf = sb("wf", [P, 2, DK, FH])
        self.mod = sb("mod", [P, 2, 48])
        self.tok_v = self.act[:, 0:8, :].rearrange("p a s -> p (a s)").rearrange("p (t d) -> p t d", t=ST)
        self.tok_out = self.act[:, 8:16, :].rearrange("p a s -> p (a s)").rearrange("p (t d) -> p t d", t=ST)
        self.ps = ctx.enter_context(nc.psum_tensor("ps", [P, 8, S], F32))
        self.w_in = [ctx.enter_context(nc.semaphore(f"w_in{i}")) for i in range(2)]
        self.chunk_done = ctx.enter_context(nc.semaphore("chunk_done"))
        self.counts = {name: Count(ctx.enter_context(nc.semaphore(name))) for name in SEMAPHORES}
        self.sem = {name: c.sem for name, c in self.counts.items()}
        self.dve = Chain(ctx.enter_context(nc.semaphore("dve_chain")))
        self.acts = Chain(ctx.enter_context(nc.semaphore("act_chain")))
        self.pool = Chain(ctx.enter_context(nc.semaphore("pool_chain")))

    def c(self, name):
        a, b = CONST_AT[name]
        return self.consts[:, a:b]

    def col(self, name, k):
        return self.cols[:, COL[name] + k:COL[name] + k + 1]

    def count(self, name):
        return self.counts[name]

    def at(self, name, n):
        return n + self.counts[name].done

    def loads(self, todo):

        def run(sp):
            for load, c0, j0, j1 in todo:
                if j1 - j0 >= 6:
                    n2 = (j1 - j0) // 2
                    with sp.Fori(0, n2) as i:
                        for u in range(2):
                            self.load_one(sp, load, c0, i * 2 + (j0 + u), (c0 + j0 + u) % 2, True)
                    j0 += 2 * n2
                for j in range(j0, j1):
                    self.load_one(sp, load, c0, j, (c0 + j) % 2, c0 + j >= 2)
        return run

    def load_one(self, sp, load, c0, j, slot, wait):
        aps = load(j, self.w[slot])
        if wait:
            sp.wait_ge(self.chunk_done, j + (c0 - 1))
        for dst, src in aps:
            sp.dma_start(dst, src).then_inc(self.w_in[slot], 32 // len(aps))


def finish(m, **totals):
    for name, n in totals.items():
        m.count(name).done += n


class Stage:
    n = 0
    load = None

    def __init__(self, m):
        self.m = m

    def sync(self, e): pass
    def tensor(self, e): pass
    def vector(self, e): pass
    def scalar(self, e): pass
    def gpsimd(self, e): pass
    def end(self): pass

    def landed(self, pe, j, parity):
        if isinstance(j, int):
            pe.wait_ge(self.m.w_in[parity], 32 * ((self.c0 + j) // 2 + 1))
        else:
            i, u = j
            pe.wait_ge(self.m.w_in[parity], i * 32 + 32 * ((self.c0 + u) // 2 + 1))


def pairs(eng, n, first, body, chain=None, per=0, tail=0):
    for j in range(min(first, n)):
        body(j)
    n2 = (n - first - tail) // 2
    if n2 >= 2:
        if chain is None:
            with eng.Fori(0, n2) as i:
                for u in range(2):
                    body((i, first + u))
        else:
            with chain.loop(eng, n2, per) as i:
                for u in range(2):
                    body((i, first + u))
        first += 2 * n2
    for j in range(first, n):
        body(j)


def val(j):
    return j if isinstance(j, int) else j[0] * 2 + j[1]


def par(j):
    return (j if isinstance(j, int) else j[1]) % 2


class Stats:

    def __init__(self, m):
        self.m = m

    def tensor(self, e):
        m, nc = self.m, self.m.nc
        for k in range(DK):
            e.wait_ge(m.sem["sq_ready"], m.at("sq_ready", k + 1))
            for t in range(ST):
                last = nc.tensor.matmul(m.ps[:, 7, t:t + 1], m.sq[:, k % 2, t * P:(t + 1) * P], m.mean_w[:, 0:1],
                                        start=k == 0 and t == 0, stop=k == DK - 1, skip_group_check=True)
            last.then_inc(m.sem["sq_used"], 1)
        for t in range(ST):
            e.wait_ge(m.sem["diag_ready"], m.at("diag_ready", t + 1))
            last = nc.tensor.matmul(m.ps[:, 6, t * P:(t + 1) * P], m.ones[:], m.diag[:, t, :], start=True, stop=True)
        last.then_inc(m.sem["rms_spread"], 1)

    def scalar(self, e):
        m, nc = self.m, self.m.nc
        for k in range(DK):
            if k >= 2:
                e.wait_ge(m.sem["sq_used"], m.at("sq_used", k - 1))
            nc.scalar.activation(m.sq[:, k % 2, :], m.x[:, k, :], ACT.Square).then_inc(m.sem["sq_ready"], 1)
        e.wait_ge(m.sem["sq_used"], m.at("sq_used", DK))
        nc.scalar.activation(m.rms[:], m.ps[:, 7, 0:ST], ACT.Sqrt, bias=m.eps[:, 0:1]).then_inc(m.sem["std_ready"], 1)

    def vector(self, e):
        m, nc = self.m, self.m.nc
        e.wait_ge(m.sem["std_ready"], m.at("std_ready", 1))
        m.dve(e, nc.vector.reciprocal(m.rms[:], m.rms[:]))
        for t in range(ST):
            nc.vector.tensor_scalar(m.diag[:, t, :], m.c("ident"), m.rms[:, t:t + 1], None, ALU.mult).then_inc(m.sem["diag_ready"], 1)
        e.wait_ge(m.sem["rms_spread"], m.at("rms_spread", 1))

    def end(self):
        finish(self.m, sq_ready=DK, sq_used=DK, std_ready=1, diag_ready=ST, rms_spread=1)


class Norm:

    def __init__(self, m, gain, shift=None):
        self.m, self.gain, self.shift, self.stats = m, gain, shift, Stats(m)

    def scalar(self, e):
        m, nc = self.m, self.m.nc
        self.stats.scalar(e)
        if self.shift:
            for k in range(DK):
                e.wait_ge(m.sem["h_scaled"], m.at("h_scaled", k + 1))
                nc.scalar.activation(m.h[:, k, :], m.h[:, k, :], ACT.Identity, bias=self.shift(k)).then_inc(m.sem["h_ready"], 1)

    def tensor(self, e):
        self.stats.tensor(e)

    def vector(self, e):
        m, nc = self.m, self.m.nc
        self.stats.vector(e)
        out = m.sem["h_scaled" if self.shift else "h_ready"]
        for k in range(DK):
            nc.vector.scalar_tensor_tensor(self.dst(k), m.x[:, k, :], self.gain(k), m.ps[:, 6, :], ALU.mult, ALU.mult).then_inc(out, 1)

    def dst(self, k):
        return self.m.h[:, k, :]

    def end(self):
        self.stats.end()
        finish(self.m, h_ready=DK)
        if self.shift:
            finish(self.m, h_scaled=DK)


class GateUp(Stage):

    def __init__(self, m, w, width, norm, glu=False):
        super().__init__(m)
        self.wt, self.width, self.norm, self.glu = w, width, norm, glu
        self.n = width // 256
        self.rhs = m.h
        self.src = w.rearrange("(k p) n -> p k n", p=P)

    def load(self, j, slot):
        v = slot[:, 0:DK * 512].rearrange("p (k g n) -> p k g n", k=DK, g=2)
        return [(v[:, :, g, :], self.src[:, :, bass.ds(j * 256 + g * self.width, 256)]) for g in range(2)]

    def tensor(self, e):
        m, nc = self.m, self.m.nc
        h_ready, taken = m.count("h_ready"), m.count("pair_taken")
        if self.norm:
            self.norm.tensor(e)

        def chunk(j):
            slot = (self.c0 + par(j)) % 2
            self.landed(e, j, slot)
            if not (isinstance(j, int) and j < 2):
                e.wait_ge(taken.sem, val(j) + (taken.done - 1))
            v = m.w[slot][:, 0:DK * 512].rearrange("p (k b n) -> p k b n", k=DK, b=4)
            for k in range(DK):
                if self.norm and isinstance(j, int) and j == 0:
                    e.wait_ge(h_ready.sem, h_ready.at(k + 1))
                for b in range(4):
                    last = nc.tensor.matmul(m.ps[:, par(j) * 4 + b, :], v[:, k, b, :], m.h[:, k, :], start=k == 0, stop=k == DK - 1)
            last.then_inc(m.chunk_done, 1)
        pairs(e, self.n, 1, chunk)

    def scalar(self, e):
        m, nc = self.m, self.m.nc
        taken, half = m.count("pair_taken"), m.count("half_ready")
        if self.norm:
            self.norm.scalar(e)

        def chunk(j):
            if not (isinstance(j, int) and j < 2):
                e.wait_ge(taken.sem, val(j) + (taken.done - 1))
            e.wait_ge(m.chunk_done, val(j) + (self.c0 + 1))
            b = par(j) * 4 + 2 * self.glu
            nc.scalar.activation(m.sg[:, par(j)], m.ps[:, b:b + 2, :], ACT.Sigmoid if self.glu else ACT.Silu).then_inc(half.sem, 1)
        pairs(e, self.n, 1, chunk)

    def vector(self, e):
        m, nc = self.m, self.m.nc
        taken, half = m.count("pair_taken"), m.count("half_ready")
        if self.norm:
            self.norm.vector(e)

        def chunk(j):
            e.wait_ge(half.sem, val(j) + (half.done + 1))
            b = par(j) * 4 + 2 * (not self.glu)
            if self.glu:
                m.dve(e, nc.vector.tensor_tensor(m.sg[:, par(j)], m.sg[:, par(j)], m.ps[:, b:b + 2, :], ALU.mult))
                xs = m.x[:, bass.ds(val(j) * 2, 2), :]
                nc.vector.tensor_tensor(xs, xs, m.sg[:, par(j)], ALU.add).then_inc(taken.sem, 1)
            else:
                nc.vector.tensor_tensor(m.act[:, bass.ds(val(j) * 2, 2), :], m.sg[:, par(j)], m.ps[:, b:b + 2, :], ALU.mult).then_inc(taken.sem, 1)
        pairs(e, self.n, self.n if self.glu else 1, chunk)

    def end(self):
        if self.norm:
            self.norm.end()
        finish(self.m, pair_taken=self.n, half_ready=self.n)


class Project(Stage):

    def __init__(self, m, w, src, gate=None, turn=None, tok=None):
        super().__init__(m)
        self.tok = tok if tok is not None else m.tok_out
        self.srcs, self.gate, self.turn = src, gate, turn
        self.kt = w.shape[0] // P
        self.n = D // 256
        self.wv = w.rearrange("(k p) n -> p k n", p=P)

    def load(self, j, slot):
        v = slot[:, 0:self.kt * 256].rearrange("p (k n) -> p k n", k=self.kt)
        return [(v, self.wv[:, :, bass.ds(j * 256, 256)])]

    def tensor(self, e):
        m, nc = self.m, self.m.nc
        taken = m.count("out_taken")
        if self.turn:
            for k in range(self.turn):
                if due(k - 3):
                    e.wait_ge(m.sem["h_ready"], m.at("h_ready", k - 3))
                for t in range(ST):
                    last = nc.tensor.transpose(m.ps[:, 4 + k % 4, t * P:(t + 1) * P], self.tok[:, t, k * P:(k + 1) * P], m.c("ident"))
                last.then_inc(m.sem["turned"], 1)

        def chunk(j):
            slot = (self.c0 + par(j)) % 2
            self.landed(e, j, slot)
            if not (isinstance(j, int) and j < 2):
                e.wait_ge(taken.sem, val(j) + (taken.done - 1))
            v = m.w[slot][:, 0:self.kt * 256].rearrange("p (k b n) -> p k b n", k=self.kt, b=2)
            for k in range(self.kt):
                if j == 0 and k < (self.turn or 0):
                    e.wait_ge(m.sem["h_ready"], m.at("h_ready", k + 1))
                for b in range(2):
                    last = nc.tensor.matmul(m.ps[:, par(j) * 2 + b, :], v[:, k, b, :], self.srcs(k), start=k == 0, stop=k == self.kt - 1)
            last.then_inc(m.chunk_done, 1)
        pairs(e, self.n, 2, chunk)

    def vector(self, e):
        m, nc = self.m, self.m.nc
        taken = m.count("out_taken")
        for k in range(self.turn or 0):
            e.wait_ge(m.sem["turned"], m.at("turned", k + 1))
            nc.vector.tensor_copy(m.h[:, k, :], m.ps[:, 4 + k % 4, :]).then_inc(m.sem["h_ready"], 1)

        def chunk(j):
            e.wait_ge(m.chunk_done, val(j) + (self.c0 + 1))
            for b in range(2):
                xs = m.x[:, 2 * j + b, :]
                gate = self.gate(2 * j + b) if self.gate else 1.0
                last = nc.vector.scalar_tensor_tensor(xs, m.ps[:, par(j) * 2 + b, :], gate, xs, ALU.mult, ALU.add)
            last.then_inc(taken.sem, 1)
        for j in range(self.n):
            chunk(j)

    def end(self):
        finish(self.m, out_taken=self.n, h_ready=self.turn or 0, turned=self.turn or 0)


class Softplus:

    def __init__(self, m, y, a, b, out):
        self.m, self.y, self.a, self.b, self.out = m, y, a, b, out

    def scalar(self, e):
        m, nc = self.m, self.m.nc
        e.wait_ge(m.sem["sp_y"], m.at("sp_y", 1))
        m.acts(e, nc.scalar.activation(self.a, self.y, ACT.Abs))
        nc.scalar.activation(self.a, self.a, ACT.Exp, scale=-1.0).then_inc(m.sem["sp_e"], 1)
        e.wait_ge(m.sem["sp_u"], m.at("sp_u", 1))
        nc.scalar.activation(self.out, self.b, ACT.Ln).then_inc(m.sem["sp_ln"], 1)

    def vector(self, e):
        m, nc = self.m, self.m.nc
        e.wait_ge(m.sem["sp_e"], m.at("sp_e", 1))
        nc.vector.tensor_scalar(self.b, self.a, 1.0, None, ALU.add).then_inc(m.sem["sp_u"], 1)
        e.wait_ge(m.sem["sp_u"], m.at("sp_u", 1))
        e.wait_ge(m.sem["sp_ln"], m.at("sp_ln", 1))
        tt, ts = nc.vector.tensor_tensor, nc.vector.tensor_scalar
        m.dve(e, nc.vector.scalar_tensor_tensor(self.a, self.b, -1.0, self.a, ALU.add, ALU.subtract))
        m.dve(e, nc.vector.reciprocal(self.b, self.b))
        m.dve(e, nc.vector.scalar_tensor_tensor(self.a, self.a, -1.0, self.b, ALU.mult, ALU.mult))
        m.dve(e, nc.vector.scalar_tensor_tensor(self.a, self.y, 0.0, self.a, ALU.max, ALU.add))
        m.dve(e, tt(self.out, self.out, self.a, ALU.add))

    def end(self):
        finish(self.m, sp_y=1, sp_e=1, sp_u=1, sp_ln=1)


class FoxV(Stage):
    n = 2

    def __init__(self, m, l, norm):
        super().__init__(m)
        self.l, self.norm = l, norm
        self.wv = m.d["fox_w_in"][l].rearrange("(k p) n -> p k n", p=P)
        f = m.act
        self.sp = Softplus(m, f[0:FH, 16, :], f[0:FH, 17, :], f[0:FH, 18, :], f[0:FH, 19, :])

    def load(self, j, slot):
        return [(slot[:, 0:DK * 512].rearrange("p (k n) -> p k n", k=DK), self.wv[:, :, bass.ds(2 * D + j * 512, 512)])]

    def tensor(self, e):
        m, nc = self.m, self.m.nc
        self.norm.tensor(e)
        for j in range(2):
            slot = (self.c0 + j) % 2
            self.landed(e, j, slot)
            v = m.w[slot][:, 0:DK * 512].rearrange("p (k n) -> p k n", k=DK)
            if j == 1:
                e.wait_ge(m.sem["sp_y"], m.at("sp_y", 1))
            for k in range(DK):
                if j == 0:
                    e.wait_ge(m.sem["h_ready"], m.at("h_ready", k + 1))
                for t in range(ST):
                    last = nc.tensor.matmul(m.ps[:, 4 * j + t, :], m.h[:, k, t * P:(t + 1) * P], v[:, k, :], start=k == 0, stop=k == DK - 1)
                if j == 0:
                    f = nc.tensor.matmul(m.ps[0:FH, 4, :], m.wf[:, self.l, k, :], m.h[:, k, :], start=k == 0, stop=k == DK - 1)
            (f if j == 0 else last).then_inc(m.chunk_done, 1)
        e.wait_ge(m.sem["c_ready"], m.at("c_ready", 1))
        e.wait_ge(m.sem["v_taken"], m.at("v_taken", 1))
        for t in range(ST):
            last = nc.tensor.transpose(m.ps[:, 0, t * FH:(t + 1) * FH], m.misc[0:FH, 16 * S + t * P:16 * S + (t + 1) * P], m.c("ident")[0:FH, 0:FH])
        last.then_inc(m.sem["turned"], 1)

    def scalar(self, e):
        m, nc = self.m, self.m.nc
        self.norm.scalar(e)
        for j in range(2):
            e.wait_ge(m.chunk_done, self.c0 + j + 1)
            nc.scalar.activation(m.tok_v[:, :, j * 512:(j + 1) * 512], m.ps[:, 4 * j:4 * j + 4, :], ACT.Copy).then_inc(m.sem["v_taken"], 1)
            if j == 0:
                self.sp.scalar(e)

    def vector(self, e):
        m, nc = self.m, self.m.nc
        self.norm.vector(e)
        e.wait_ge(m.chunk_done, self.c0 + 1)
        nc.vector.tensor_scalar(self.sp.y, m.ps[0:FH, 4, :], m.small[0:FH, self.l:self.l + 1], -1.0, ALU.add, ALU.mult).then_inc(m.sem["sp_y"], 1)
        e.wait_ge(m.sem["sp_y"], m.at("sp_y", 1))
        self.sp.vector(e)
        nc.vector.tensor_tensor_scan(m.misc[0:FH, 16 * S:17 * S], m.ones16[0:FH, :], self.sp.out, 0.0, ALU.mult, ALU.subtract).then_inc(m.sem["c_ready"], 1)
        e.wait_ge(m.sem["turned"], m.at("turned", 1))
        nc.vector.tensor_copy(m.small[:, 16:16 + ST * FH], m.ps[:, 0, 0:ST * FH]).then_inc(m.sem["ct_ready"], 1)

    def end(self):
        self.norm.end()
        self.sp.end()
        finish(self.m, v_taken=2, c_ready=1, turned=1, ct_ready=1)


class Attention(Stage):

    taken = "exp_ready"

    def prev(self, p, j, lag):
        if j >= lag:
            return p, j - lag
        return (p - 1 if isinstance(p, int) else (p[0], p[1] - 1)), j - lag + self.per

    def s(self, p, j):
        return val(p) * self.per + j

    def setup_views(self):
        m = self.m
        v = m.misc
        self.lg = [v[:, i * S:(i + 1) * S] for i in (8, 9)]
        self.pb = [v[:, i * S:(i + 1) * S] for i in (10, 11)]
        self.pt = [v[:, i * S:(i + 1) * S] for i in (12, 13)]
        self.nm = m.small[:, 100:104]
        self.rs = m.small[:, 104:108]
        self.ri = m.small[:, 108:110]

    def logits(self, e, p, j):
        m, nc, s, t = self.m, self.m.nc, self.s(p, j), j % ST
        if due(s - 1):
            e.wait_ge(m.sem[self.taken], m.at(self.taken, s - 1))
        q, k = self.q(p, j), self.k(p, j)
        nc.tensor.matmul(m.ps[:, 4 + j % 2, 0:(t + 1) * P], q[:, t * P:(t + 1) * P], k[:, 0:(t + 1) * P], start=True, stop=False)
        nc.tensor.matmul(m.ps[:, 4 + j % 2, t * P:(t + 1) * P], m.identb[:], m.futureb[:], start=False, stop=True).then_inc(m.sem["logits_ready"], 1)

    def turn(self, e, p, j):
        m, nc, s, t = self.m, self.m.nc, self.s(p, j), j % ST
        e.wait_ge(m.sem["exp_ready"], m.at("exp_ready", s + 1))
        if due(s):
            e.wait_ge(m.sem["pt_ready"], m.at("pt_ready", s))
        for b in range(t + 1):
            last = nc.tensor.transpose(m.ps[:, 6, b * P:(b + 1) * P], self.pb[j % 2][:, b * P:(b + 1) * P], m.c("ident"))
        last.then_inc(m.sem["p_turned"], 1)

    def times_v(self, e, p, j):
        m, nc, s, t = self.m, self.m.nc, self.s(p, j), j % ST
        e.wait_ge(m.sem["pt_ready"], m.at("pt_ready", s + 1))
        if due(s):
            e.wait_ge(m.sem["o_taken"], m.at("o_taken", s))
        o = m.ps[:, 7, (j % 2) * 64:(j % 2) * 64 + 64]
        for b in range(t + 1):
            last = nc.tensor.matmul(o, self.pt[j % 2][:, b * P:(b + 1) * P], self.v(p, j, b), start=b == 0, stop=b == t)
        last.then_inc(m.sem["pv_done"], 1)

    def exp(self, e, p, j):
        m, nc, s, t = self.m, self.m.nc, self.s(p, j), j % ST
        n = (t + 1) * P
        e.wait_ge(m.sem["max_ready"], m.at("max_ready", s + 1))
        if due(s - 1):
            e.wait_ge(m.sem["p_turned"], m.at("p_turned", s - 1))
        last = nc.scalar.activation(self.pb[j % 2][:, 0:n], self.logit_src(j)[:, 0:n], ACT.Exp, bias=self.nm[:, j % 4:j % 4 + 1],
                                    scale=self.scale, accum_out=self.rs[:, j % 4:j % 4 + 1])
        last.then_inc(m.sem["exp_ready"], 1)

    def copy_turned(self, e, p, j):
        m, nc, s, t = self.m, self.m.nc, self.s(p, j), j % ST
        e.wait_ge(m.sem["p_turned"], m.at("p_turned", s + 1))
        if due(s - 1):
            e.wait_ge(m.sem["pv_done"], m.at("pv_done", s - 1))
        nc.scalar.activation(self.pt[j % 2][:, 0:(t + 1) * P], m.ps[:, 6, 0:(t + 1) * P], ACT.Copy).then_inc(m.sem["pt_ready"], 1)

    def output(self, e, p, j):
        m, nc, s, t = self.m, self.m.nc, self.s(p, j), j % ST
        e.wait_ge(m.sem["pv_done"], m.at("pv_done", s + 1))
        m.dve(e, nc.vector.reciprocal(self.ri[:, j % 2:j % 2 + 1], self.rs[:, j % 4:j % 4 + 1]))
        nc.vector.tensor_scalar(self.out(p, j), m.ps[:, 7, (j % 2) * 64:(j % 2) * 64 + 64], self.ri[:, j % 2:j % 2 + 1], None, ALU.mult).then_inc(m.sem["o_taken"], 1)

    def run(self, e, chain, per, now, later, prologue):
        prologue()

        def unit(p):
            first = isinstance(p, int) and p == 0
            for j in range(self.per):
                now(p, j)
                for lag, piece in later:
                    if not (first and j < lag):
                        piece(e, *self.prev(p, j, lag))
        unit(0)
        n2 = (self.units - 2) // 2
        if chain:
            with chain.loop(e, n2, per * 2) as i:
                for u in range(2):
                    unit((i, 1 + u))
        else:
            with e.Fori(0, n2) as i:
                for u in range(2):
                    unit((i, 1 + u))
        for p in range(1 + 2 * n2, self.units):
            unit(p)
        for j in range(max(lag for lag, _ in later)):
            for lag, piece in later:
                if j < lag:
                    piece(e, *self.prev(self.units, j, lag))

    def finish_steps(self):
        n = self.units * self.per
        finish(self.m, logits_taken=n, logits_ready=n, exp_ready=n, pt_ready=n, p_turned=n, o_taken=n, pv_done=n, max_ready=n)


class FoxAttention(Attention):
    n = units = FH // 2
    per = 2 * ST
    scale = 1.0
    taken = "logits_taken"

    def __init__(self, m, l):
        super().__init__(m)
        self.l = l
        self.wv = m.d["fox_w_in"][l].rearrange("(k p) n -> p k n", p=P)
        self.setup_views()
        v = m.misc
        self.qs = [v[:, i * S:(i + 1) * S] for i in (0, 1)]
        self.ks = [v[:, i * S:(i + 1) * S] for i in (2, 3)]
        self.ck = [[v[:, (4 + 2 * i + h) * S:(5 + 2 * i + h) * S] for h in range(2)] for i in range(2)]
        self.cm = [v[0:FH, i * S:(i + 1) * S] for i in (14, 15)]
        self.c16 = v[0:FH, 16 * S:17 * S]

    def load(self, j, slot):
        v = slot[:, 0:DK * 256].rearrange("p (k g n) -> p k g n", k=DK, g=2)
        return [(v[:, :, g, :], self.wv[:, :, bass.ds(j * P + g * D, P)]) for g in range(2)]

    def q(self, p, j):
        h = j // ST * 64
        return self.qs[par(p)][h:h + 64, :]

    def k(self, p, j):
        h = j // ST * 64
        return self.ks[par(p)][h:h + 64, :]

    def v(self, p, j, b):
        return self.m.tok_v[:, b, bass.ds(val(p) * P + (j // ST) * 64, 64)]

    def out(self, p, j):
        return self.m.tok_out[:, j % ST, bass.ds(val(p) * P + (j // ST) * 64, 64)]

    def logit_src(self, j):
        return self.lg[j % 2]

    def nxt(self, p):
        return p + 1 if isinstance(p, int) else (p[0], p[1] + 1)

    def project(self, e, p, ks):
        m, nc = self.m, self.m.nc
        slot = (self.c0 + par(p)) % 2
        v = m.w[slot][:, 0:DK * 256].rearrange("p (k g n) -> p k g n", k=DK, g=2)
        for k in ks:
            if k == 0:
                self.landed(e, p, slot)
            for g in range(2):
                last = nc.tensor.matmul(m.ps[:, g, :], v[:, k, g, :], m.h[:, k, :], start=k == 0, stop=k == DK - 1)
            if k == DK - 1:
                last.then_inc(m.chunk_done, 1)

    def spread(self, e, p):
        m, nc = self.m, self.m.nc
        e.wait_ge(m.sem["cm_ready"], m.at("cm_ready", val(p) + 1))
        for h in range(2):
            last = nc.tensor.matmul(m.ps[:, 2 + h, :], m.ones[0:FH, :], self.cm[h], start=True, stop=True)
        last.then_inc(m.sem["ck_done"], 1)

    def tensor(self, e):
        m = self.m
        split = {0: (0, 1), 1: (2, 3), 2: (4,), 3: (5,), 4: (6,), 5: (7,)}

        def prologue():
            self.project(e, 0, range(DK))
            self.spread(e, 0)

        def now(p, j):
            if j == 0:
                e.wait_ge(m.sem["q_staged"], m.at("q_staged", val(p) + 1))
                e.wait_ge(m.sem["k_staged"], m.at("k_staged", val(p) + 1))
            self.logits(e, p, j)
            if not (isinstance(p, int) and p == self.units - 1):
                self.project(e, self.nxt(p), split.get(j, ()))
                if j == 6:
                    self.spread(e, self.nxt(p))
        self.run(e, None, 0, now, [(1, self.turn), (2, self.times_v)], prologue)

    def stage_act(self, e, p):
        m, nc = self.m, self.m.nc
        e.wait_ge(m.chunk_done, val(p) + (self.c0 + 1))
        nc.scalar.activation(self.qs[par(p)], m.ps[:, 0, :], ACT.Copy, scale=64 ** -0.5)
        e.wait_ge(m.sem["ck_done"], m.at("ck_done", val(p) + 1))
        for h in range(2):
            last = nc.scalar.activation(self.ck[par(p)][h], m.ps[:, 2 + h, :], ACT.Copy)
        last.then_inc(m.sem["q_staged"], 1)

    def scalar(self, e):
        def now(p, j):
            self.exp(e, p, j)
            if j == 6 and not (isinstance(p, int) and p == self.units - 1):
                self.stage_act(e, self.nxt(p))
        self.run(e, None, 0, now, [(1, self.copy_turned)], lambda: self.stage_act(e, 0))

    def masked_c(self, e, p):
        m, nc = self.m, self.m.nc
        if due(val(p)):
            e.wait_ge(m.sem["ck_done"], m.at("ck_done", val(p)))
        for h in range(2):
            last = nc.vector.tensor_scalar(self.cm[h], self.c16, m.c("ident")[0:FH, bass.ds(val(p) * 2 + h, 1)], None, ALU.mult)
        last.then_inc(m.sem["cm_ready"], 1)

    def stage_dve(self, e, p):
        m, nc = self.m, self.m.nc
        e.wait_ge(m.chunk_done, val(p) + (self.c0 + 1))
        nc.vector.tensor_copy(self.ks[par(p)], m.ps[:, 1, :]).then_inc(m.sem["k_staged"], 1)

    def vector(self, e):
        m, nc = self.m, self.m.nc

        def prologue():
            self.masked_c(e, 0)
            self.stage_dve(e, 0)

        def now(p, j):
            s, t, n = self.s(p, j), j % ST, (j % ST + 1) * P
            if j == 0:
                e.wait_ge(m.sem["q_staged"], m.at("q_staged", val(p) + 1))
            e.wait_ge(m.sem["logits_ready"], m.at("logits_ready", s + 1))
            if due(s - 1):
                e.wait_ge(m.sem["exp_ready"], m.at("exp_ready", s - 1))
            cq = m.small[:, bass.ds(val(p) * 2 + (16 + t * FH + j // ST), 1)]
            nc.vector.scalar_tensor_tensor(self.lg[j % 2][:, 0:n], m.ps[:, 4 + j % 2, 0:n], cq, self.ck[par(p)][j // ST][:, 0:n], ALU.add, ALU.subtract).then_inc(m.sem["logits_taken"], 1)
            e.wait_ge(m.sem["logits_taken"], m.at("logits_taken", s + 1))
            nc.vector.tensor_reduce(self.nm[:, j % 4:j % 4 + 1], self.lg[j % 2][:, 0:n], AX.X, ALU.max, negate=True).then_inc(m.sem["max_ready"], 1)
            if not (isinstance(p, int) and p == self.units - 1):
                if j == 4:
                    self.masked_c(e, self.nxt(p))
                if j == 6:
                    self.stage_dve(e, self.nxt(p))
        self.run(e, m.dve, self.per, now, [(2, self.output)], prologue)

    def end(self):
        self.finish_steps()
        finish(self.m, q_staged=self.n, k_staged=self.n, cm_ready=self.n, ck_done=self.n)


class Linear(Stage):

    def __init__(self, m, w, norm, dst):
        super().__init__(m)
        self.norm, self.dst = norm, dst
        self.n = w.shape[1] // 512
        self.wv = w.rearrange("(k p) n -> p k n", p=P)

    def load(self, j, slot):
        return [(slot[:, 0:DK * 512].rearrange("p (k n) -> p k n", k=DK), self.wv[:, :, bass.ds(j * 512, 512)])]

    def tensor(self, e):
        m, nc = self.m, self.m.nc
        self.norm.tensor(e)
        for j in range(self.n):
            slot = (self.c0 + j) % 2
            self.landed(e, j, slot)
            if j == 1:
                e.wait_ge(m.sem["s5_step"], m.at("s5_step", 1))
            v = m.w[slot][:, 0:DK * 512].rearrange("p (k n) -> p k n", k=DK)
            for k in range(DK):
                if j == 0:
                    e.wait_ge(m.sem["h_ready"], m.at("h_ready", k + 1))
                for b in range(4):
                    last = nc.tensor.matmul(m.ps[:, 4 * (j % 2) + b, :], v[:, k, b * P:(b + 1) * P], m.h[:, k, :], start=k == 0, stop=k == DK - 1)
            last.then_inc(m.chunk_done, 1)

    def scalar(self, e):
        self.norm.scalar(e)
        self.copies(e)

    def copies(self, e):
        m, nc = self.m, self.m.nc
        for j in range(self.n):
            e.wait_ge(m.chunk_done, self.c0 + j + 1)
            nc.scalar.activation(self.dst(j), m.ps[:, 4 * (j % 2):4 * (j % 2) + 4, :], ACT.Copy).then_inc(m.sem["quad_taken"], 1)

    def vector(self, e):
        self.norm.vector(e)

    def end(self):
        self.norm.end()
        finish(self.m, quad_taken=self.n)


class PoolMix(Stage):
    n = 1

    def __init__(self, m, norm):
        super().__init__(m)
        self.norm = norm

    def load(self, j, slot):
        return [(slot[:, 0:2048].rearrange("p (k n) -> p k n", k=8), self.m.d["pool_w"].rearrange("l g (k p) n -> p (l g k) n", p=P))]

    def gpsimd(self, e):
        m = self.m
        m.nc.gpsimd.memset(m.misc[:, 0:4 * 544], 0.0).then_inc(m.sem["pads_clear"], 1)

    def tensor(self, e):
        m, nc = self.m, self.m.nc
        self.norm.tensor(e)
        self.landed(e, 0, self.c0 % 2)
        v = m.w[self.c0 % 2][:, 0:2048].rearrange("p (k n) -> p k n", k=8)
        for o in range(DK):
            g, b = o // 2, o % 2
            if b == 0:
                e.wait_ge(m.sem["diff_ready"], m.at("diff_ready", g + 1))
            for k in range(2):
                last = nc.tensor.matmul(m.ps[:, o, :], v[:, 2 * g + k, b * P:(b + 1) * P], m.act[:, 2 * g + k, :], start=k == 0, stop=k == 1)
            if o < DK - 1:
                last.then_inc(m.sem["pooled"], 1)
        last.then_inc(m.chunk_done, 1)

    def scalar(self, e):
        m, nc = self.m, self.m.nc
        self.norm.scalar(e)
        for o in range(DK):
            if o < DK - 1:
                e.wait_ge(m.sem["pooled"], m.at("pooled", o + 1))
            else:
                e.wait_ge(m.chunk_done, self.c0 + 1)
            nc.scalar.activation(m.act[:, 8 + o, :], m.ps[:, o, :], ACT.Identity, bias=m.col("pool_b", o)).then_inc(m.sem["biased"], 1)

    def vector(self, e):
        m, nc = self.m, self.m.nc
        self.norm.vector(e)
        e.wait_ge(m.sem["h_ready"], m.at("h_ready", DK))
        e.wait_ge(m.sem["pads_clear"], m.at("pads_clear", 1))
        bufs = [m.misc[:, i * 1088:(i + 1) * 1088].rearrange("p (a n) -> p a n", a=2) for i in range(2)]
        for g, w in enumerate(WINDOWS):
            hg = m.h[:, 2 * g:2 * g + 2, :]
            a = bufs[0]
            nc.vector.tensor_copy(a[:, :, 16:17], hg[:, :, 0:1])
            m.dve(e, nc.vector.tensor_tensor(a[:, :, 17:528], hg[:, :, 1:512], hg[:, :, 0:511], ALU.add))
            lag = 2
            for i in range(g):
                a, b = bufs[i % 2], bufs[(i + 1) % 2]
                m.dve(e, nc.vector.tensor_tensor(b[:, :, 16:528], a[:, :, 16:528], a[:, :, 16 - lag:528 - lag], ALU.add))
                a, lag = b, lag * 2
            dst = m.act[:, 2 * g:2 * g + 2, :]
            m.dve(e, nc.vector.tensor_tensor(dst[:, :, 0:16], a[:, :, 16:32], m.c("rc")[:, 16 * g:16 * g + 16].rearrange("p (a n) -> p a n", a=1).broadcast_to([P, 2, 16]), ALU.mult))
            nc.vector.scalar_tensor_tensor(dst[:, :, 16:512], a[:, :, 32:528], 1.0 / w, hg[:, :, 16:512], ALU.mult, ALU.subtract)
            nc.vector.tensor_tensor(dst[:, :, 0:16], dst[:, :, 0:16], hg[:, :, 0:16], ALU.subtract).then_inc(m.sem["diff_ready"], 1)
            e.wait_ge(m.sem["diff_ready"], m.at("diff_ready", g + 1))
        for o in range(DK):
            e.wait_ge(m.sem["biased"], m.at("biased", o + 1))
            last = nc.vector.scalar_tensor_tensor(m.x[:, o, :], m.act[:, 8 + o, :], m.col("pool_s", o), m.x[:, o, :], ALU.mult, ALU.add)
        m.dve(e, last)

    def end(self):
        self.norm.end()
        finish(self.m, pads_clear=1, diff_ready=4, pooled=DK - 1, biased=DK)


class Gelu:

    def __init__(self, m):
        self.m = m

    def scalar(self, e):
        m, nc = self.m, self.m.nc
        for k in range(DK):
            nc.scalar.activation(m.h[:, k, :], m.h[:, k, :], ACT.Gelu_apprx_tanh).then_inc(m.sem["h_ready"], 1)

    def tensor(self, e): pass
    def vector(self, e): pass

    def end(self):
        finish(self.m, h_ready=DK)


def s5_buffers(m):
    v = {}
    at = 0
    for name, n in (("e2c", 2048), ("e2s", 2048), ("e1c", 256), ("e1s", 256), ("bbr", 512), ("bbi", 512), ("cr", 512), ("ci", 512),
                    ("btr", 512), ("bti", 512), ("t0", 512), ("t1", 512), ("t2", 512)):
        v[name] = m.misc[:, at:at + n]
        at += n
    for i in range(14):
        v[f"a{i}"] = m.act[:, 8 + i, :]
    return v


class S5Prepare(Stage):

    def sync(self, e):
        m, d = self.m, self.m.d
        b = s5_buffers(m)
        ld = m.count("s5_loaded")
        rows = b["a0"]
        e.dma_start(rows[0:32, 0:128], d["s5_a_re"].rearrange("l (i g) p -> (l i) (g p)", g=2)).then_inc(ld.sem, 16)
        e.dma_start(rows[0:32, 128:256], d["s5_a_im"].rearrange("l (i g) p -> (l i) (g p)", g=2)).then_inc(ld.sem, 16)
        e.dma_start(rows[0:32, 256:258], d["s5_log_dt"].rearrange("l (i g) -> (l i) g", g=2)).then_inc(ld.sem, 16)
        for k, name in (("a2", "s5_b_re"), ("a3", "s5_b_im")):
            e.dma_start(b[k].rearrange("q (i c) -> q i c", c=C5), d[name].rearrange("l g p c -> (l g p) c").rearrange("(i q) c -> q i c", q=P)).then_inc(ld.sem, 16)
        for k, name in (("cr", "s5_c_re"), ("ci", "s5_c_im")):
            e.dma_start(b[k].rearrange("r (q p) -> r q p", p=N5), d[name].rearrange("l g c p -> (l g c) p").rearrange("(q r) p -> r q p", r=P)).then_inc(ld.sem, 16)

    def tensor(self, e):
        m, nc = self.m, self.m.nc
        b = s5_buffers(m)
        e.wait_ge(m.sem["s5_rows"], m.at("s5_rows", 1))
        src = (b["a0"][0:32, 0:128], b["a0"][0:32, 128:256], b["a1"][0:32, 0:128])
        for i in range(3):
            last = nc.tensor.transpose(m.ps[:, 5, 32 * i:32 * i + 32], src[i], m.c("ident")[0:32, 0:32])
        last.then_inc(m.sem["turned"], 1)

    def scalar(self, e):
        m, nc = self.m, self.m.nc
        sm = self.cols()
        e.wait_ge(m.sem["s5_step"], m.at("s5_step", 1))
        m.acts(e, nc.scalar.activation(sm["dt"], sm["dt"], ACT.Exp))
        nc.scalar.activation(sm["z"], sm["dt"], ACT.Copy).then_inc(m.sem["s5_act"], 1)
        e.wait_ge(m.sem["s5_step"], m.at("s5_step", 2))
        nc.scalar.activation(sm["er"], sm["er"], ACT.Exp)
        nc.scalar.activation(sm["sn"], sm["sn"], ACT.Sin)
        nc.scalar.activation(sm["cs"], sm["cs"], ACT.Sin).then_inc(m.sem["s5_act"], 1)

    def cols(self):
        names = ("ar", "ai", "dt", "er", "cs", "sn", "t", "k", "den", "nr", "ni", "z")
        v = {n: self.m.small[:, 128 + 32 * i:160 + 32 * i] for i, n in enumerate(names)}
        return v

    def rows(self, e):
        m, nc = self.m, self.m.nc
        b = s5_buffers(m)
        e.wait_ge(m.sem["s5_loaded"], m.at("s5_loaded", 16 * 7))
        nc.vector.tensor_copy(b["a1"][0:32, 0:128].rearrange("p (g n) -> p g n", g=2), b["a0"][0:32, 256:258].rearrange("p (g n) -> p g n", n=1).broadcast_to([32, 2, 64])).then_inc(m.sem["s5_rows"], 1)

    def vector(self, e):
        m, nc = self.m, self.m.nc
        b, sm = s5_buffers(m), self.cols()
        tt, ts, stt = nc.vector.tensor_tensor, nc.vector.tensor_scalar, nc.vector.scalar_tensor_tensor
        do = lambda ins: m.dve(e, ins)
        e.wait_ge(m.sem["turned"], m.at("turned", 1))
        do(nc.vector.tensor_copy(m.small[:, 128:224], m.ps[:, 5, 0:96]))
        nc.vector.tensor_copy(sm["t"], sm["ar"]).then_inc(m.sem["s5_step"], 1)
        e.wait_ge(m.sem["s5_act"], m.at("s5_act", 1))
        do(tt(sm["er"], sm["ar"], sm["dt"], ALU.mult))
        do(tt(sm["t"], sm["ai"], sm["dt"], ALU.mult))
        do(ts(sm["k"], sm["t"], 1 / TWO_PI, 12582912.0, ALU.mult, ALU.add))
        do(ts(sm["k"], sm["k"], -12582912.0, None, ALU.add))
        for part in TURN_PARTS:
            do(stt(sm["t"], sm["k"], -part, sm["t"], ALU.mult, ALU.add))
        do(ts(sm["sn"], sm["t"], PI_IN, -PI_IN, ALU.min, ALU.max))
        do(ts(sm["cs"], sm["sn"], -1.0, None, ALU.mult))
        do(tt(sm["cs"], sm["cs"], sm["sn"], ALU.max))
        ts(sm["cs"], sm["cs"], -1.0, float(np.pi / 2), ALU.mult, ALU.add).then_inc(m.sem["s5_step"], 1)
        e.wait_ge(m.sem["s5_act"], m.at("s5_act", 2))
        do(tt(sm["nr"], sm["er"], sm["cs"], ALU.mult))
        do(ts(sm["nr"], sm["nr"], -1.0, None, ALU.add))
        do(tt(sm["ni"], sm["er"], sm["sn"], ALU.mult))
        do(tt(sm["den"], sm["ar"], sm["ar"], ALU.mult))
        do(tt(sm["t"], sm["ai"], sm["ai"], ALU.mult))
        do(tt(sm["den"], sm["den"], sm["t"], ALU.add))
        do(nc.vector.reciprocal(sm["den"], sm["den"]))
        do(tt(sm["t"], sm["nr"], sm["ar"], ALU.mult))
        do(tt(sm["k"], sm["ni"], sm["ai"], ALU.mult))
        do(tt(sm["t"], sm["t"], sm["k"], ALU.add))
        do(tt(sm["k"], sm["ni"], sm["ar"], ALU.mult))
        do(tt(sm["z"], sm["nr"], sm["ai"], ALU.mult))
        do(tt(sm["k"], sm["k"], sm["z"], ALU.subtract))
        do(tt(sm["t"], sm["t"], sm["den"], ALU.mult))
        do(tt(sm["k"], sm["k"], sm["den"], ALU.mult))
        wide = lambda a, n: a.rearrange("p (i a) -> p i a", a=1).broadcast_to([P, 32, n])
        three = lambda a, n: a.rearrange("p (i a) -> p i a", a=n)
        br, bi, t0 = three(b["a2"], C5), three(b["a3"], C5), three(b["a4"], C5)
        for out, p0, p1, op in (("bbr", (sm["t"], br), (sm["k"], bi), ALU.subtract), ("bbi", (sm["t"], bi), (sm["k"], br), ALU.add)):
            do(tt(three(b[out], C5), p0[1], wide(p0[0], C5), ALU.mult))
            do(tt(t0, p1[1], wide(p1[0], C5), ALU.mult))
            do(tt(three(b[out], C5), three(b[out], C5), t0, op))
        for ec, es, n, top in ((three(b["e2c"], 64), three(b["e2s"], 64), 1, 64), (three(b["e1c"], 8), three(b["e1s"], 8), 1, 8)):
            do(nc.vector.memset(ec[:, :, 0:1], 1.0))
            do(nc.vector.memset(es[:, :, 0:1], 0.0))
            while n < top:
                t = b["a5"][:, 0:32 * n] if n <= 16 else m.sg[:, :, :, :].rearrange("p a b s -> p (a b s)")[:, 0:32 * n]
                t = three(t, n)
                wc, ws = wide(sm["cs"], n), wide(sm["sn"], n)
                do(tt(ec[:, :, n:2 * n], ec[:, :, 0:n], wc, ALU.mult))
                do(tt(t, es[:, :, 0:n], ws, ALU.mult))
                do(tt(ec[:, :, n:2 * n], ec[:, :, n:2 * n], t, ALU.subtract))
                do(tt(es[:, :, n:2 * n], es[:, :, 0:n], wc, ALU.mult))
                do(tt(t, ec[:, :, 0:n], ws, ALU.mult))
                do(tt(es[:, :, n:2 * n], es[:, :, n:2 * n], t, ALU.add))
                do(tt(sm["t"], sm["cs"], sm["cs"], ALU.mult))
                do(tt(sm["k"], sm["sn"], sm["sn"], ALU.mult))
                do(stt(sm["sn"], sm["sn"], 2.0, sm["cs"], ALU.mult, ALU.mult))
                do(tt(sm["cs"], sm["t"], sm["k"], ALU.subtract))
                n *= 2

    def end(self):
        finish(self.m, s5_loaded=16 * 7, s5_rows=1, turned=1, s5_step=2, s5_act=2)


class S5In(Linear):

    def __init__(self, m, w, norm, dst):
        super().__init__(m, w, norm, dst)
        self.prepare = S5Prepare(m)

    def sync(self, e):
        self.prepare.sync(e)

    def tensor(self, e):
        self.prepare.tensor(e)
        super().tensor(e)

    def scalar(self, e):
        self.norm.scalar(e)
        self.prepare.scalar(e)
        self.copies(e)

    def vector(self, e):
        self.prepare.rows(e)
        self.norm.vector(e)
        self.prepare.vector(e)

    def end(self):
        super().end()
        self.prepare.end()


class S5Scan(Stage):

    TILES = 4

    def tensor(self, e):
        m, nc = self.m, self.m.nc
        b = s5_buffers(m)
        bt = [b[k].rearrange("p (r n) -> p r n", r=4) for k in ("btr", "bti")]
        ct = self.ct()

        def turn_b(q):
            e.wait_ge(m.sem["bin_ready"], m.at("bin_ready", q + 1))
            for i in range(2):
                last = nc.tensor.transpose(m.ps[:, 6, i * P:(i + 1) * P], self.tin()[i], m.c("ident"))
            last.then_inc(m.sem["b_turned"], 1)

        def turn_c(q):
            e.wait_ge(m.sem["cin_ready"], m.at("cin_ready", q + 1))
            for i in range(2):
                last = nc.tensor.transpose(m.ps[:, 7, i * P:(i + 1) * P], self.tin()[2 + i], m.c("ident"))
            last.then_inc(m.sem["c_turned"], 1)

        def bu(q, r):
            if r == 0:
                e.wait_ge(m.sem["bt_ready"], m.at("bt_ready", q + 1))
            if due(q * 4 + (r - 1)):
                e.wait_ge(m.sem["bu_taken"], m.at("bu_taken", q * 4 + (r - 1)))
            for i in range(2):
                last = nc.tensor.matmul(m.ps[:, 2 * (r % 2) + i, :], bt[i][:, r, :], m.act[:, bass.ds(q, 1), :].rearrange("p a s -> p (a s)"), start=True, stop=True)
            last.then_inc(m.sem["bu_ready"], 1)

        def y(q, r):
            e.wait_ge(m.sem["x_ready"], m.at("x_ready", q * 4 + (r + 1)))
            if r == 0:
                e.wait_ge(m.sem["ct_ready5"], m.at("ct_ready5", q + 1))
                if due(q):
                    e.wait_ge(m.sem["y_taken"], m.at("y_taken", q))
            for n, (prod, i) in enumerate(((0, 0), (1, 0), (2, 1), (3, 1))):
                last = nc.tensor.matmul(m.ps[32 * r:32 * r + 32, 4, :], ct[i][:, 32 * r:32 * r + 32], self.prod(r)[prod], start=n == 0, stop=n == 3)
            last.then_inc(m.sem["y_ready"], 1)

        def tile(q, final):
            turn_c(q)
            for r in range(4):
                if r < 3:
                    bu(q, r + 1)
                elif not final:
                    turn_b(q + 1)
                    bu(q + 1, 0)
                y(q, r)
        turn_b(0)
        bu(0, 0)
        tile(0, False)
        with e.Fori(0, DK - 2) as i:
            tile(i + 1, False)
        tile(DK - 1, True)

    def tin(self):
        b = s5_buffers(self.m)
        return [b["t0"][:, i * P:(i + 1) * P] for i in range(4)]

    def ct(self):
        b = s5_buffers(self.m)
        return [b["t1"][:, i * P:(i + 1) * P] for i in range(2)]

    def prod(self, r):
        b = s5_buffers(self.m)
        return [b[f"a{4 * (r % 2) + i}"] for i in range(4)]

    def tab(self, r):
        b = s5_buffers(self.m)
        return [b[f"a{8 + 2 * (r % 2) + i}"] for i in range(2)]

    def gpsimd(self, e):
        m, nc = self.m, self.m.nc
        b = s5_buffers(m)
        tt = nc.gpsimd.tensor_tensor
        tmp = m.sg[:, 0, :, :]
        v3 = lambda a: a.rearrange("p (a b) -> p a b", a=8)

        def table(q, r):
            if due(q * 4 + (r - 1)):
                e.wait_ge(m.sem["x_ready"], m.at("x_ready", q * 4 + (r - 1)))
            c, s = (v3(t) for t in self.tab(r))
            t0, t1 = v3(tmp[:, 0, :]), v3(tmp[:, 1, :])
            at = q * 4 + r
            e2 = [b[k].rearrange("p (i b a) -> p i a b", i=32, a=1)[:, bass.ds(at, 1), :, :].rearrange("p i a b -> p (i a) b").broadcast_to([P, 8, 64]) for k in ("e2c", "e2s")]
            e1 = [b[k].rearrange("p (i a b) -> p i a b", i=32, b=1)[:, bass.ds(at, 1), :, :].rearrange("p i a b -> p (i a) b").broadcast_to([P, 8, 64]) for k in ("e1c", "e1s")]
            tt(m.small[:, 121:122], m.eps[:], m.eps[:], ALU.add)
            tt(c, e1[0], e2[0], ALU.mult)
            tt(t0, e1[1], e2[1], ALU.mult)
            tt(s, e1[1], e2[0], ALU.mult)
            m.pool(e, tt(t1, e1[0], e2[1], ALU.mult))
            tt(c, c, t0, ALU.subtract)
            m.pool(e, tt(s, s, t1, ALU.add))

        for r in range(4):
            table(0, r)
        with m.pool.loop(e, DK - 1, 4 * 2) as i:
            for r in range(4):
                table(i + 1, r)

    def vector(self, e):
        m, nc = self.m, self.m.nc
        b = s5_buffers(m)
        tt, ts, stt = nc.vector.tensor_tensor, nc.vector.tensor_scalar, nc.vector.scalar_tensor_tensor
        tin, ct = self.tin(), self.ct()
        half = m.c("half").rearrange("p (r g c) -> p r g c", r=4, g=2)
        rowm = m.rowmask[:, :].rearrange("p (r a) -> p r a", a=1).broadcast_to([P, 4, P])
        t = [m.sg[:, 1, 0, :], m.sg[:, 1, 1, :], m.sq[:, 0, :], m.sq[:, 1, :]]
        er = S5Prepare.cols(self)["er"]

        def prep_b(q):
            for i, k in enumerate(("bbr", "bbi")):
                src = b[k].rearrange("p (i g c) -> p i g c", i=32, g=1)[:, bass.ds(q * 4, 4), :, :].broadcast_to([P, 4, 2, C5])
                last = tt(tin[i].rearrange("p (r g c) -> p r g c", r=4, g=2), src, half, ALU.mult)
            last.then_inc(m.sem["bin_ready"], 1)
            e.wait_ge(m.sem["b_turned"], m.at("b_turned", q + 1))
            for i, k in enumerate(("btr", "bti")):
                src = m.ps[:, 6, i * P:(i + 1) * P].rearrange("p (a n) -> p a n", a=1).broadcast_to([P, 4, P])
                last = tt(b[k].rearrange("p (r n) -> p r n", r=4), rowm, src, ALU.mult)
            last.then_inc(m.sem["bt_ready"], 1)

        def prep_c(q):
            for i, k in enumerate(("cr", "ci")):
                src = b[k].rearrange("p (q a n) -> p q a n", q=8, a=1)[:, bass.ds(q, 1), :, :].rearrange("p q a n -> p (q a) n").broadcast_to([P, 2, N5])
                last = ts(tin[2 + i].rearrange("p (a n) -> p a n", a=2), src, 1.0, None, ALU.mult)
            last.then_inc(m.sem["cin_ready"], 1)
            e.wait_ge(m.sem["c_turned"], m.at("c_turned", q + 1))
            stt(ct[0], m.ps[:, 7, 0:P], 1.0, m.c("half"), ALU.mult, ALU.mult)
            stt(ct[1], m.ps[:, 7, P:2 * P], -1.0, m.c("half"), ALU.mult, ALU.mult).then_inc(m.sem["ct_ready5"], 1)

        def scan(q, r):
            c, s = self.tab(r)
            o = self.prod(r)
            n = 2 * (r % 2)
            br, bi = m.ps[:, n, :], m.ps[:, n + 1, :]
            e.wait_ge(m.sem["bu_ready"], m.at("bu_ready", q * 4 + (r + 1)))
            e.wait_ge(m.pool.sem, (q * 4 + (r + 1)) * 2 + self.pool0)
            if due(q * 4 + r):
                e.wait_ge(m.sem["x_ready"], m.at("x_ready", q * 4 + r))
            tt(t[0], br, c, ALU.mult)
            tt(t[1], bi, s, ALU.mult)
            tt(t[2], bi, c, ALU.mult)
            m.dve(e, tt(t[3], br, s, ALU.mult))
            tt(t[0], t[0], t[1], ALU.add).then_inc(m.sem["bu_taken"], 1)
            m.dve(e, tt(t[2], t[2], t[3], ALU.subtract))
            rr = er[:, bass.ds(q * 4 + r, 1)].broadcast_to([P, S])
            nc.vector.tensor_tensor_scan(t[1], rr, t[0], 0.0, ALU.mult, ALU.add)
            m.dve(e, nc.vector.tensor_tensor_scan(t[3], rr, t[2], 0.0, ALU.mult, ALU.add))
            if due(q * 4 + (r - 1)):
                e.wait_ge(m.sem["y_ready"], m.at("y_ready", q * 4 + (r - 1)))
            tt(o[0], t[1], c, ALU.mult)
            stt(o[1], t[3], -1.0, s, ALU.mult, ALU.mult)
            tt(o[2], t[1], s, ALU.mult)
            tt(o[3], t[3], c, ALU.mult).then_inc(m.sem["x_ready"], 1)

        def tile(q, final):
            for r in range(4):
                scan(q, r)
                if r == 2 and not final:
                    e.wait_ge(m.sem["bu_ready"], m.at("bu_ready", q * 4 + 4))
                    prep_b(q + 1)
            e.wait_ge(m.sem["y_ready"], m.at("y_ready", q * 4 + 4))
            dcol = m.cols[:, bass.ds(q + COL["s5_d"], 1)]
            one = lambda a: a[:, bass.ds(q, 1), :].rearrange("p a s -> p (a s)")
            stt(one(m.h), one(m.act), dcol, m.ps[:, 4, :], ALU.mult, ALU.add).then_inc(m.sem["y_taken"], 1)

        prep_b(0)
        prep_c(0)
        tile(0, False)
        with m.dve.loop(e, DK - 2, 4 * 3) as i:
            prep_c(i + 1)
            tile(i + 1, False)
        prep_c(DK - 1)
        tile(DK - 1, True)

    def end(self):
        n = 4 * DK
        finish(self.m, bin_ready=DK, cin_ready=DK, b_turned=DK, c_turned=DK, bt_ready=DK, ct_ready5=DK, bu_ready=n, bu_taken=n,
               x_ready=n, y_ready=n, y_taken=DK)


class AdaUnits:

    def __init__(self, m, first, n):
        self.m, self.first, self.n = m, first, n

    def source(self, u):
        l, c = divmod(self.first + u, 6 * DK)
        return self.m.d["w_ada_2"][l].rearrange("(k p) n -> p k n", p=P)[:, :, c * P:(c + 1) * P]

    def gpsimd(self, e):
        m, nc = self.m, self.m.nc
        tt = nc.gpsimd.tensor_tensor
        c = m.cact[:, :].rearrange("p (k a) -> p k a", a=1).broadcast_to([P, DK, P])
        three = lambda a: a.rearrange("p (k n) -> p k n", k=DK)

        def load(u):
            nc.gpsimd.dma_start(three(m.ada_w[:, u % 2, :]), self.source(u)).then_inc(m.sem["ada_in"], 16)
        load(0)
        for u in range(self.n):
            e.wait_ge(m.sem["ada_in"], m.at("ada_in", 16 * (u + 1)))
            if u + 1 < self.n:
                load(u + 1)
            if due(u - 1):
                e.wait_ge(m.sem["ada_done"], m.at("ada_done", u - 1))
            p = m.ada_p[:, u % 2, :]
            m.pool(e, tt(three(p), three(m.ada_w[:, u % 2, :]), c, ALU.mult))
            for n in (4 * P, 2 * P):
                m.pool(e, tt(p[:, 0:n], p[:, 0:n], p[:, n:2 * n], ALU.add))
            tt(p[:, 0:P], p[:, 0:P], p[:, P:2 * P], ALU.add).then_inc(m.sem["ada_summed"], 1)
            e.wait_ge(m.sem["ada_summed"], m.at("ada_summed", u + 1))

    def tensor(self, e, u):
        m, nc = self.m, self.m.nc
        e.wait_ge(m.sem["ada_summed"], m.at("ada_summed", u + 1))
        nc.tensor.matmul(m.ps[:, 4, u:u + 1], m.ada_p[:, u % 2, 0:P], m.ones[:, 0:1], start=True, stop=True).then_inc(m.sem["ada_done"], 1)

    def vector(self, e):
        m, nc = self.m, self.m.nc
        e.wait_ge(m.sem["ada_done"], m.at("ada_done", self.n))
        flat = m.mod[:, :, :].rearrange("p l n -> p (l n)")[:, self.first:self.first + self.n]
        b = COL["b_ada"] + self.first
        m.dve(e, nc.vector.tensor_tensor(flat, m.ps[:, 4, 0:self.n], m.cols[:, b:b + self.n], ALU.add))

    def end(self):
        finish(self.m, ada_in=16 * self.n, ada_summed=self.n, ada_done=self.n)


class SecondSetup(Stage):

    def sync(self, e):
        m, d = self.m, self.m.d
        ld = m.count("second_loaded")
        with m.nc.allow_non_contiguous_dma(reason="short parameter vectors"):
            e.dma_start(m.wdt[:, 0], d["w_in_2"][0][:, D_DT:].rearrange("(k p) n -> p k n", p=P)).then_inc(ld.sem, 16)
            e.dma_start(m.wdt[:, 1], d["w_in_2"][1][:, D_DT:].rearrange("(k p) n -> p k n", p=P)).then_inc(ld.sem, 16)
            for l in range(2):
                for i, name in enumerate(("dt_bias_2", "a_log_2")):
                    e.dma_start(m.heads[0:MH, 2 * l + i:2 * l + i + 1], d[name][l].rearrange("(h a) -> h a", a=1)).then_inc(ld.sem, 16)
                for i, name in enumerate(("q", "k")):
                    e.dma_start(m.qkn[0:NOPE, 2 * l + i:2 * l + i + 1], d[name + "_nope_norm_w_2"][l].rearrange("(h a) -> h a", a=1)).then_inc(ld.sem, 16)
                    e.dma_start(m.qkn[NOPE:QH, 2 * l + i:2 * l + i + 1], d[name + "_pe_norm_w_2"][l].rearrange("(h a) -> h a", a=1)).then_inc(ld.sem, 16)
            for h in range(2):
                src = d["d_skip_2"].rearrange("l (t h) -> h (l t)", h=2)[h:h + 1, :].broadcast_to([64, 8])
                e.dma_start(m.dskip[64 * h:64 * h + 64, :], src).then_inc(ld.sem, 16)
            e.dma_start(m.misc.bitcast(I32)[0:QH, 0:S], d["positions_2"].broadcast_to([QH, S])).then_inc(ld.sem, 16)

    def scalar(self, e):
        m, nc = self.m, self.m.nc
        e.wait_ge(m.sem["angles"], m.at("angles", 1))
        for i in range(2):
            nc.scalar.activation(m.rope[0:QH, i, :], m.rope[0:QH, i, :], ACT.Sin).then_inc(m.sem["sines"], 1)

    def vector(self, e):
        m, nc = self.m, self.m.nc
        tt, ts, stt = nc.vector.tensor_tensor, nc.vector.tensor_scalar, nc.vector.scalar_tensor_tensor
        do = lambda ins: m.dve(e, ins)
        a, k = m.sg[0:QH, 0, 0, :], m.sg[0:QH, 0, 1, :]
        c, s = m.rope[0:QH, 0, :], m.rope[0:QH, 1, :]
        e.wait_ge(m.sem["second_loaded"], m.at("second_loaded", 16 * 17))
        do(nc.vector.tensor_copy(a, m.misc.bitcast(I32)[0:QH, 0:S]))
        do(ts(a, a, m.c("inv")[0:QH, :], None, ALU.mult))
        do(ts(k, a, 1 / TWO_PI, 12582912.0, ALU.mult, ALU.add))
        do(ts(k, k, -12582912.0, None, ALU.add))
        for part in TURN_PARTS:
            do(stt(a, k, -part, a, ALU.mult, ALU.add))
        do(ts(s, a, PI_IN, -PI_IN, ALU.min, ALU.max))
        do(ts(c, s, -1.0, None, ALU.mult))
        do(tt(c, c, s, ALU.max))
        ts(c, c, -1.0, float(np.pi / 2), ALU.mult, ALU.add).then_inc(m.sem["angles"], 1)
        e.wait_ge(m.sem["sines"], m.at("sines", 2))
        nc.vector.memset(m.rope[0:NOPE, 0, :], 1.0)
        do(nc.vector.memset(m.rope[0:NOPE, 1, :], 0.0))
        for l in range(2):
            for i, name in enumerate(("norm1", "norm2")):
                last = stt(m.gains[:, l, i, :], m.mod[:, l, 24 * i + 8:24 * i + 16], 1.0,
                           m.cols[:, COL[name] + 8 * l:COL[name] + 8 * l + 8], ALU.add, ALU.mult)
        m.dve(e, last)

    def end(self):
        finish(self.m, second_loaded=16 * 17, angles=1, sines=2)


class SecondIn(Stage):
    n = 4

    def __init__(self, m, l, norm):
        super().__init__(m)
        self.l, self.norm = l, norm
        self.wv = m.d["w_in_2"][l].rearrange("(k p) n -> p k n", p=P)
        g = m.sg
        self.sp = Softplus(m, g[0:MH, 0, 0, :], g[0:MH, 0, 1, :], g[0:MH, 1, 0, :], g[0:MH, 1, 1, :])
        self.span = [(0, D_ZI), (D_ZI, 512), (D_XBC, 512), (D_XBC + 512, 512)]
        self.tiles = [[(0, P), (P, P), (2 * P, P), (D_ZI - QH, QH)]] + [[(b * P, P) for b in range(4)]] * 3
        self.pad = m.act[:, 4:13, :].rearrange("p a s -> p (a s)")[:, 0:8 * 515].rearrange("p (a n) -> p a n", a=8)

    def load(self, j, slot):
        a, n = self.span[j]
        return [(slot[:, 0:DK * n].rearrange("p (k n) -> p k n", k=DK), self.wv[:, :, a:a + n])]

    def gpsimd(self, e):
        m = self.m
        m.nc.gpsimd.memset(self.pad[:, :, 0:3], 0.0).then_inc(m.sem["pads_clear"], 1)

    def tensor(self, e):
        m, nc = self.m, self.m.nc
        self.norm.tensor(e)
        for j in range(4):
            slot = (self.c0 + j) % 2
            self.landed(e, j, slot)
            if j == 1:
                e.wait_ge(m.sem["sp_y"], m.at("sp_y", 1))
            if due(j - 1):
                e.wait_ge(m.sem["quad_taken"], m.at("quad_taken", j - 1))
            n = self.span[j][1]
            v = m.w[slot][:, 0:DK * n].rearrange("p (k n) -> p k n", k=DK)
            for k in range(DK):
                if j == 0:
                    e.wait_ge(m.sem["h_ready"], m.at("h_ready", k + 1))
                for b, (c, w) in enumerate(self.tiles[j]):
                    last = nc.tensor.matmul(m.ps[0:w, 4 * (j % 2) + b, :], v[:, k, c:c + w], m.h[:, k, :], start=k == 0, stop=k == DK - 1)
                if j == 0:
                    last = nc.tensor.matmul(m.ps[0:MH, 4, :], m.wdt[:, self.l, k, :], m.h[:, k, :], start=k == 0, stop=k == DK - 1)
            last.then_inc(m.chunk_done, 1)

    def scalar(self, e):
        m, nc = self.m, self.m.nc
        self.norm.scalar(e)
        q = m.count("quad_taken")
        e.wait_ge(m.chunk_done, self.c0 + 1)
        nc.scalar.activation(m.misc[:, 0:3 * S].rearrange("p (a s) -> p a s", a=3), m.ps[:, 0:3, :], ACT.Copy)
        nc.scalar.activation(m.misc[NOPE:QH, 3 * S:4 * S], m.ps[NOPE:QH, 3, :], ACT.Copy).then_inc(q.sem, 1)
        self.sp.scalar(e)
        e.wait_ge(m.chunk_done, self.c0 + 2)
        nc.scalar.activation(m.act[:, 0:4, :], m.ps[:, 4:8, :], ACT.Silu).then_inc(q.sem, 1)
        e.wait_ge(m.sem["pads_clear"], m.at("pads_clear", 1))
        for j in range(2):
            e.wait_ge(m.chunk_done, self.c0 + 3 + j)
            nc.scalar.activation(self.pad[:, 4 * j:4 * j + 4, 3:515], m.ps[:, 4 * j:4 * j + 4, :], ACT.Copy).then_inc(q.sem, 1)
        for t in range(8):
            e.wait_ge(m.sem["conv_ready"], m.at("conv_ready", t + 1))
            last = nc.scalar.activation(m.act[:, 13 + t, :], m.act[:, 13 + t, :], ACT.Silu, bias=m.col("conv_b", 8 * self.l + t))
        m.acts(e, last)

    def vector(self, e):
        m, nc = self.m, self.m.nc
        self.norm.vector(e)
        e.wait_ge(m.chunk_done, self.c0 + 1)
        nc.vector.tensor_scalar(self.sp.y, m.ps[0:MH, 4, :], m.heads[0:MH, 2 * self.l:2 * self.l + 1], None, ALU.add).then_inc(m.sem["sp_y"], 1)
        e.wait_ge(m.sem["sp_y"], m.at("sp_y", 1))
        self.sp.vector(e)
        for t in range(8):
            if t % 4 == 0:
                e.wait_ge(m.sem["quad_taken"], m.at("quad_taken", 3 + t // 4))
            w = lambda i: m.col("conv_w", (CONVW * self.l + i) * 8 + t)
            o = m.act[:, 13 + t, :]
            m.dve(e, nc.vector.tensor_scalar(o, self.pad[:, t, 0:S], w(0), None, ALU.mult))
            for i in range(1, CONVW):
                ins = nc.vector.scalar_tensor_tensor(o, self.pad[:, t, i:i + S], w(i), o, ALU.mult, ALU.add)
                if i < CONVW - 1:
                    m.dve(e, ins)
            ins.then_inc(m.sem["conv_ready"], 1)

    def end(self):
        self.norm.end()
        self.sp.end()
        finish(self.m, quad_taken=4, conv_ready=8, pads_clear=1)


class Ssd(Stage):

    def __init__(self, m, l):
        super().__init__(m)
        self.l = l
        mi, ac = m.misc, m.act
        sl = lambda i: mi[:, i * S:(i + 1) * S]
        self.adt, self.acs, self.cmask = m.sg[0:MH, 0, 0, :], m.sg[0:MH, 0, 1, :], m.sg[0:MH, 1, 0, :]
        self.dt = m.sg[0:MH, 1, 1, :]
        self.am = [ac[0:MH, 21, :], m.rstd[0:MH, :]]
        self.btok = mi[:, 4 * S:6 * S].rearrange("p (g c n) -> p g c n", g=2, c=ST)
        self.cb = [sl(6), sl(7)]
        self.eh, self.lh, self.sc, self.cth = [sl(8), sl(9)], [sl(10), sl(11)], [sl(12), sl(13)], [sl(14), sl(15)]
        self.st = [None, sl(16), sl(17), ac[:, 12, :]]
        self.xdt, self.xdtd = [ac[:, 4 + t, :] for t in range(4)], [ac[:, 8 + t, :] for t in range(4)]
        self.xs = lambda t: ac[:, 13 + t, :]
        self.bT = lambda g: ac[:, 17 + g, :]
        self.cT = lambda g: ac[:, 19 + g, :]
        sm = m.small
        self.dtT, self.acsT = sm[:, 0:32], sm[:, 32:64]
        self.nacs, self.dec, self.cd = sm[:, 64:96], sm[:, 96:128], sm[:, 128:160]
        self.na = sm[0:MH, 160:161]

    def tensor(self, e):
        m, nc = self.m, self.m.nc
        ident = m.c("ident")
        tr, mm = nc.tensor.transpose, nc.tensor.matmul
        ps = m.ps
        for g in range(2):
            for c in range(ST):
                cs = slice(c * P, (c + 1) * P)
                last = mm(ps[:, g, cs], self.bT(g)[:, cs], self.cT(g)[:, cs], start=True, stop=True)
            last.then_inc(m.sem["cb_done"], 1)
        for g in range(2):
            for c in range(ST):
                last = tr(ps[:, 2 + g, c * P:(c + 1) * P], self.bT(g)[:, c * P:(c + 1) * P], ident)
            last.then_inc(m.sem["bt_done"], 1)
        for c in range(ST):
            for t in range(4):
                last = tr(ps[:, 4 + c, t * P:(t + 1) * P], self.xs(t)[:, c * P:(c + 1) * P], ident)
            last.then_inc(m.sem["xt_done"], 1)
        e.wait_ge(m.sem["acs_ready"], m.at("acs_ready", 1))
        e.wait_ge(m.sem["cb_ready"], m.at("cb_ready", 1))
        for i, src in enumerate((self.dt, self.acs)):
            for c in range(ST):
                last = tr(ps[:, 0, 32 * i + 8 * c:32 * i + 8 * c + 8], src[:, c * P:(c + 1) * P], ident[0:MH, 0:MH])
        last.then_inc(m.sem["rows_turned"], 1)
        e.wait_ge(m.sem["acsT_ready"], m.at("acsT_ready", 1))
        e.wait_ge(m.sem["cb_ready"], m.at("cb_ready", 2))
        mm(ps[:, 1, 0:32], m.c("last"), self.acsT, start=True, stop=True).then_inc(m.sem["last_spread"], 1)
        for c in range(ST - 1):
            e.wait_ge(m.sem["xdtd_ready"], m.at("xdtd_ready", c + 1))
            e.wait_ge(m.sem["bt_ready2"], m.at("bt_ready2", 2))
            if due(c - 1):
                e.wait_ge(m.sem["st_ready"], m.at("st_ready", c - 1))
            for g in range(2):
                last = mm(ps[:, 2 + c % 2, g * 256:(g + 1) * 256], self.btok[:, g, c, :], self.xdtd[c][:, g * 256:(g + 1) * 256], start=True, stop=True)
            last.then_inc(m.sem["st_done"], 1)

        def spread(h):
            b = 6 if h % 2 else 0
            e.wait_ge(m.sem["am_ready"], m.at("am_ready", h + 1))
            if h == 0:
                e.wait_ge(m.sem["decay_ready"], m.at("decay_ready", 1))
            if h == 1:
                e.wait_ge(m.sem["xdt_ready"], m.at("xdt_ready", ST))
            if due(h - 1):
                e.wait_ge(m.sem["l_ready"], m.at("l_ready", h - 1))
            mm(ps[:, b, :], m.ones[0:MH, :], self.am[h % 2], start=True, stop=True).then_inc(m.sem["bc_ready"], 1)
            mm(ps[:, b + 1, :], m.ones[0:MH, :], self.am[h % 2], start=True, stop=False)
            mm(ps[:, b + 1, :], m.identb[:], m.pastb[:].rearrange("p (a n) -> p a n", a=1).broadcast_to([P, ST, P]), start=False, stop=True).then_inc(m.sem["bm_ready"], 1)

        def out(h):
            bank = 4 + (h // 2) % 2
            e.wait_ge(m.sem["sc_ready"], m.at("sc_ready", h + 1))
            e.wait_ge(m.sem["cth_ready"], m.at("cth_ready", h + 1))
            e.wait_ge(m.sem["st_ready"], m.at("st_ready", ST - 1))
            if h == 0:
                e.wait_ge(m.sem["xdt_ready"], m.at("xdt_ready", ST))
            if due(h // 2 - 1):
                e.wait_ge(m.sem["y_gated"], m.at("y_gated", h // 2 - 1))
            r = 64 * (h % 2)
            for c in range(ST):
                cs, hs = slice(c * P, (c + 1) * P), slice(h * 64, (h + 1) * 64)
                last = mm(ps[r:r + 64, bank, cs], self.xdt[c][:, hs], self.sc[h % 2][:, cs], start=True, stop=c == 0)
                if c:
                    last = mm(ps[r:r + 64, bank, cs], self.st[c][:, hs], self.cth[h % 2][:, cs], start=False, stop=True)
            last.then_inc(m.sem["yh_done"], 1)

        spread(0)
        for h in range(MH):
            if h + 1 < MH:
                spread(h + 1)
            out(h)
        for t in range(4):
            e.wait_ge(m.sem["ysq_ready"], m.at("ysq_ready", t + 1))
            last = mm(ps[:, 2 + t // 2, :], m.ones[:], m.sq[:, t % 2, :], start=t % 2 == 0, stop=t % 2 == 1)
            last.then_inc(m.sem["ysq_used"], 1)

    def scalar(self, e):
        m, nc = self.m, self.m.nc
        act = nc.scalar.activation
        act(self.na, m.heads[0:MH, 2 * self.l + 1:2 * self.l + 2], ACT.Exp).then_inc(m.sem["a_ready"], 1)
        for g in range(2):
            e.wait_ge(m.sem["cb_done"], m.at("cb_done", g + 1))
            act(self.cb[g], m.ps[:, g, :], ACT.Copy).then_inc(m.sem["cb_ready"], 1)
        for g in range(2):
            e.wait_ge(m.sem["bt_done"], m.at("bt_done", g + 1))
            act(self.btok[:, g], m.ps[:, 2 + g, :].rearrange("p (c n) -> p c n", c=ST), ACT.Copy).then_inc(m.sem["bt_ready2"], 1)
        e.wait_ge(m.sem["last_spread"], m.at("last_spread", 1))
        act(self.cd, m.ps[:, 1, 0:32], ACT.Exp).then_inc(m.sem["cd_ready"], 1)
        e.wait_ge(m.sem["dec_arg"], m.at("dec_arg", 1))
        act(self.dec, self.dec, ACT.Exp).then_inc(m.sem["decay_ready"], 1)
        for h in range(MH):
            b = 6 if h % 2 else 0
            e.wait_ge(m.sem["bc_ready"], m.at("bc_ready", h + 1))
            if due(h - 1):
                e.wait_ge(m.sem["cth_ready"], m.at("cth_ready", h - 1))
            act(self.eh[h % 2], m.ps[:, b, :], ACT.Exp).then_inc(m.sem["e_ready"], 1)
            e.wait_ge(m.sem["bm_ready"], m.at("bm_ready", h + 1))
            if due(h - 1):
                e.wait_ge(m.sem["sc_ready"], m.at("sc_ready", h - 1))
            for c in range(ST):
                last = act(self.lh[h % 2][:, c * P:(c + 1) * P], m.ps[:, b + 1, c * P:(c + 1) * P], ACT.Exp, bias=self.nacs[:, 8 * c + h:8 * c + h + 1])
            last.then_inc(m.sem["l_ready"], 1)
        for t in range(4):
            e.wait_ge(m.sem["y_gated"], m.at("y_gated", t + 1))
            if due(t - 1):
                e.wait_ge(m.sem["ysq_used"], m.at("ysq_used", t - 1))
            act(m.sq[:, t % 2, :], m.h[:, 4 + t, :], ACT.Square).then_inc(m.sem["ysq_ready"], 1)
            if t % 2:
                e.wait_ge(m.sem["ysq_used"], m.at("ysq_used", t + 1))
                act(self.eh[t // 2], m.ps[:, 2 + t // 2, :], ACT.Sqrt, bias=m.eps[:, 0:1], scale=1 / 256).then_inc(m.sem["ystd_ready"], 1)

    def gpsimd(self, e):
        m, nc = self.m, self.m.nc
        tt = nc.gpsimd.tensor_tensor
        for h in range(MH):
            g = h // 4
            e.wait_ge(m.sem["e_ready"], m.at("e_ready", h + 1))
            if due(h - 1):
                e.wait_ge(m.sem["yh_done"], m.at("yh_done", h - 1))
            tt(self.cth[h % 2], self.cT(g), self.eh[h % 2], ALU.mult).then_inc(m.sem["cth_ready"], 1)

    def vector(self, e):
        m, nc = self.m, self.m.nc
        tt, ts, stt = nc.vector.tensor_tensor, nc.vector.tensor_scalar, nc.vector.scalar_tensor_tensor
        do = lambda ins: m.dve(e, ins)
        e.wait_ge(m.sem["a_ready"], m.at("a_ready", 1))
        do(nc.vector.memset(self.cmask, 1.0))
        do(nc.vector.memset(self.cmask.rearrange("p (c n) -> p c n", c=ST)[:, :, 0:1], 0.0))
        do(ts(self.na, self.na, -1.0, None, ALU.mult))
        do(ts(self.adt, self.dt, self.na, None, ALU.mult))
        nc.vector.tensor_tensor_scan(self.acs, self.cmask, self.adt, 0.0, ALU.mult, ALU.add).then_inc(m.sem["acs_ready"], 1)
        e.wait_ge(m.sem["rows_turned"], m.at("rows_turned", 1))
        nc.vector.tensor_copy(m.small[:, 0:64], m.ps[:, 0, 0:64]).then_inc(m.sem["acsT_ready"], 1)
        e.wait_ge(m.sem["acsT_ready"], m.at("acsT_ready", 1))
        do(ts(self.nacs, self.acsT, -1.0, None, ALU.mult))
        e.wait_ge(m.sem["cd_ready"], m.at("cd_ready", 1))
        tt(self.dec, m.ps[:, 1, 0:32], self.acsT, ALU.subtract).then_inc(m.sem["dec_arg"], 1)
        wide = lambda a: a.rearrange("p (h a) -> p h a", a=1).broadcast_to([P, MH, 64])
        three = lambda a: a.rearrange("p (h n) -> p h n", h=MH)

        def am(h):
            if due(h - 1):
                e.wait_ge(m.sem["bm_ready"], m.at("bm_ready", h - 1))
            ts(self.am[h % 2], self.acs, m.c("ident")[0:MH, h:h + 1], None, ALU.mult).then_inc(m.sem["am_ready"], 1)
        am(0)
        am(1)
        for c in range(ST):
            e.wait_ge(m.sem["xt_done"], m.at("xt_done", c + 1))
            tt(three(self.xdt[c]), three(m.ps[:, 4 + c, :]), wide(self.dtT[:, 8 * c:8 * c + 8]), ALU.mult).then_inc(m.sem["xdt_ready"], 1)
        e.wait_ge(m.sem["decay_ready"], m.at("decay_ready", 1))
        e.wait_ge(m.sem["xdt_ready"], m.at("xdt_ready", ST))
        for c in range(ST - 1):
            tt(three(self.xdtd[c]), three(self.xdt[c]), wide(self.dec[:, 8 * c:8 * c + 8]), ALU.mult).then_inc(m.sem["xdtd_ready"], 1)
        for c in range(ST - 1):
            e.wait_ge(m.sem["st_done"], m.at("st_done", c + 1))
            bank = m.ps[:, 2 + c % 2, :]
            if c == 0:
                nc.vector.tensor_copy(self.st[1], bank).then_inc(m.sem["st_ready"], 1)
            else:
                e.wait_ge(m.sem["st_ready"], m.at("st_ready", c))
                do(tt(three(self.st[c + 1]), three(self.st[c]), wide(self.cd[:, 8 * c:8 * c + 8]), ALU.mult))
                tt(self.st[c + 1], self.st[c + 1], bank, ALU.add).then_inc(m.sem["st_ready"], 1)

        def gate(t):
            e.wait_ge(m.sem["yh_done"], m.at("yh_done", 2 * t + 2))
            y = m.h[:, 4 + t, :]
            do(stt(y, self.xs(t), m.dskip[:, 4 * self.l + t:4 * self.l + t + 1], m.ps[:, 4 + t % 2, :], ALU.mult, ALU.add))
            tt(y, y, m.act[:, t, :], ALU.mult).then_inc(m.sem["y_gated"], 1)

        for h in range(MH):
            e.wait_ge(m.sem["l_ready"], m.at("l_ready", h + 1))
            if due(h - 1):
                e.wait_ge(m.sem["yh_done"], m.at("yh_done", h - 1))
            tt(self.sc[h % 2], self.lh[h % 2], self.cb[h // 4], ALU.mult).then_inc(m.sem["sc_ready"], 1)
            if h + 2 < MH:
                am(h + 2)
            if h % 2 == 0 and h:
                gate(h // 2 - 1)
        gate(3)
        for g in range(2):
            e.wait_ge(m.sem["ystd_ready"], m.at("ystd_ready", g + 1))
            do(nc.vector.reciprocal(self.eh[g], self.eh[g]))
            for t in (2 * g, 2 * g + 1):
                last = stt(m.h[:, 4 + t, :], m.h[:, 4 + t, :], m.col("ssd_n", 4 * self.l + t), self.eh[g], ALU.mult, ALU.mult)
        do(last)

    def end(self):
        finish(self.m, cb_done=2, bt_done=2, xt_done=ST, acs_ready=1, cb_ready=2, rows_turned=1, acsT_ready=1, last_spread=1,
               xdtd_ready=ST - 1, bt_ready2=2, st_ready=ST - 1, st_done=ST - 1, am_ready=MH, decay_ready=1, xdt_ready=ST, l_ready=MH,
               bc_ready=MH, bm_ready=MH, sc_ready=MH, cth_ready=MH, y_gated=4, yh_done=MH, ysq_ready=4, ysq_used=4,
               a_ready=1, cd_ready=1, dec_arg=1, e_ready=MH, ystd_ready=2)


class LatentUp(Stage):
    n = 1
    ITEMS = 2 * MH

    def __init__(self, m, l):
        super().__init__(m)
        self.l = l
        mi = m.misc
        self.qa = [mi[:, i * S:(i + 1) * S] for i in range(3)]
        self.kpe = mi[NOPE:QH, 3 * S:4 * S]
        self.tok_v = mi[:, 4 * S:8 * S].rearrange("p (t n) -> p t n", t=ST)
        self.rs = [m.std, m.rstd]
        self.tmp = [mi[0:QH, 8 * S:9 * S], mi[0:QH, 9 * S:10 * S]]
        self.stat = mi[0:32, 10 * S:11 * S]
        self.item = lambda n: m.act[0:QH, 4 + n, :]

    def load(self, j, slot):
        d = self.m.d
        return [(slot[:, 0:1536].rearrange("p (k n) -> p k n", k=2), d["w_q_up_2"][self.l].rearrange("(k p) n -> p k n", p=P)),
                (slot[:, 1536:2560], d["w_kv_up_2"][self.l])]

    def tensor(self, e):
        m, nc = self.m, self.m.nc
        mm, ps = nc.tensor.matmul, m.ps
        for i in range(3):
            e.wait_ge(m.sem["lsq_ready"], m.at("lsq_ready", i + 1))
            mm(ps[:, i // 2, :], m.ones[:], m.sg[:, i // 2, i % 2, :], start=i != 1, stop=i != 0).then_inc(m.sem["lsq_used"], 1)
        slot = self.c0 % 2
        self.landed(e, 0, slot)
        wq = m.w[slot][:, 0:1536].rearrange("p (k n) -> p k n", k=2)
        wkv = m.w[slot][:, 1536:2560].rearrange("p (h n) -> p h n", h=MH)
        for n in range(self.ITEMS):
            h, bank = n % MH, 2 + n % 4
            if due(n - 3):
                e.wait_ge(m.sem["raw_taken"], m.at("raw_taken", n - 3))
            if n < MH:
                if n == 0:
                    e.wait_ge(m.sem["lat_ready"], m.at("lat_ready", 2))
                for k in range(2):
                    last = mm(ps[0:QH, bank, :], wq[:, k, h * QH:(h + 1) * QH], self.qa[k], start=k == 0, stop=k == 1)
            else:
                if n == MH:
                    e.wait_ge(m.sem["lat_ready"], m.at("lat_ready", 3))
                last = mm(ps[0:NOPE, bank, :], wkv[:, h, 0:NOPE], self.qa[2], start=True, stop=True)
            last.then_inc(m.sem["raw_ready"], 1)
            if n >= 1:
                self.stats(e, n - 1)
        self.stats(e, self.ITEMS - 1)
        for t in range(ST):
            if due(t - 1):
                e.wait_ge(m.sem["lv_taken"], m.at("lv_taken", t - 1))
            if t < 2:
                e.wait_ge(m.sem["lat_ready"], m.at("lat_ready", 3))
            last = mm(ps[:, t % 2, :], self.qa[2][:, t * P:(t + 1) * P], wkv[:, :, NOPE:P], start=True, stop=True)
            if t < ST - 1:
                last.then_inc(m.sem["lv_done"], 1)
        last.then_inc(m.chunk_done, 1)
        e.wait_ge(m.sem["stat_ready"], m.at("stat_ready", 1))
        for n in range(self.ITEMS):
            if due(n - 1):
                e.wait_ge(m.sem["normed"], m.at("normed", n - 1))
            if n < 2:
                e.wait_ge(m.sem["raw_taken"], m.at("raw_taken", self.ITEMS))
            mm(ps[0:QH, 2 + n % 2, :], m.spread[:, n * QH:(n + 1) * QH], self.stat, start=True, stop=True).then_inc(m.sem["stat_spread"], 1)
            if n >= 1:
                self.rotate(e, n - 1)
        self.rotate(e, self.ITEMS - 1)

    def stats(self, e, n):
        m = self.m
        e.wait_ge(m.sem["isq_ready"], m.at("isq_ready", n + 1))
        m.nc.tensor.matmul(m.ps[0:32, 6, :], m.gather[0:QH, 30 - 2 * n:62 - 2 * n], m.sg[0:QH, n % 2, 0, :], start=n == 0, stop=n == self.ITEMS - 1).then_inc(m.sem["isq_used"], 1)

    def rotate(self, e, n):
        m = self.m
        e.wait_ge(m.sem["normed"], m.at("normed", n + 1))
        if due(n - 1):
            e.wait_ge(m.sem["rot_taken"], m.at("rot_taken", n - 1))
        m.nc.tensor.matmul(m.ps[0:QH, 4 + n % 2, :], m.c("rot")[0:QH, 0:QH], self.item(n), start=True, stop=True).then_inc(m.sem["rot_done"], 1)

    def scalar(self, e):
        m, nc = self.m, self.m.nc
        act = nc.scalar.activation
        for i in range(3):
            act(m.sg[:, i // 2, i % 2, :], self.qa[i], ACT.Square).then_inc(m.sem["lsq_ready"], 1)
        for i, (n, w) in enumerate(((2, Q_LORA), (3, KV_LORA))):
            e.wait_ge(m.sem["lsq_used"], m.at("lsq_used", n))
            act(self.rs[i][:], m.ps[:, i, :], ACT.Sqrt, bias=m.eps[:, 0:1], scale=1 / w).then_inc(m.sem["lstd_ready"], 1)
        for n in range(self.ITEMS):
            rows = QH if n < MH else NOPE
            e.wait_ge(m.sem["raw_ready"], m.at("raw_ready", n + 1))
            if n < MH:
                act(self.item(n), m.ps[0:rows, 2 + n % 4, :], ACT.Copy).then_inc(m.sem["raw_taken"], 1)
            else:
                act(self.item(n)[0:NOPE], m.ps[0:rows, 2 + n % 4, :], ACT.Copy).then_inc(m.sem["raw_taken"], 1)
            e.wait_ge(m.sem["raw_taken"], m.at("raw_taken", n + 1))
            if due(n - 1):
                e.wait_ge(m.sem["isq_used"], m.at("isq_used", n - 1))
            if n >= MH:
                e.wait_ge(m.sem["kpe_copied"], m.at("kpe_copied", n - MH + 1))
            act(m.sg[0:QH, n % 2, 0, :], self.item(n), ACT.Square).then_inc(m.sem["isq_ready"], 1)
        for t in range(ST):
            if t < ST - 1:
                e.wait_ge(m.sem["lv_done"], m.at("lv_done", t + 1))
            else:
                e.wait_ge(m.chunk_done, self.c0 + 1)
            act(self.tok_v[:, t, :], m.ps[:, t % 2, :], ACT.Copy).then_inc(m.sem["lv_taken"], 1)
        e.wait_ge(m.sem["isq_used"], m.at("isq_used", self.ITEMS))
        act(self.stat, m.ps[0:32, 6, :], ACT.Sqrt, bias=m.eps[0:32, 0:1]).then_inc(m.sem["stat_std"], 1)

    def gpsimd(self, e):
        m, nc = self.m, self.m.nc
        for h in range(MH):
            nc.gpsimd.tensor_copy(self.item(MH + h)[NOPE:QH], self.kpe).then_inc(m.sem["kpe_copied"], 1)
        for n in range(self.ITEMS):
            e.wait_ge(m.sem["rot_done"], m.at("rot_done", n + 1))
            nc.gpsimd.tensor_tensor(self.item(n), self.item(n), m.rope[0:QH, 0, :], ALU.mult).then_inc(m.sem["cos_done"], 1)

    def vector(self, e):
        m, nc = self.m, self.m.nc
        tt, ts, stt = nc.vector.tensor_tensor, nc.vector.tensor_scalar, nc.vector.scalar_tensor_tensor
        for i, (tiles, name) in enumerate((((0, 1), "q_a"), ((2,), "kv_a"))):
            e.wait_ge(m.sem["lstd_ready"], m.at("lstd_ready", i + 1))
            m.dve(e, nc.vector.reciprocal(self.rs[i][:], self.rs[i][:]))
            for t in tiles:
                col = m.col(name, 2 * self.l + t) if i == 0 else m.col(name, self.l)
                stt(self.qa[t], self.qa[t], col, self.rs[i][:], ALU.mult, ALU.mult).then_inc(m.sem["lat_ready"], 1)
        e.wait_ge(m.sem["stat_std"], m.at("stat_std", 1))
        nc.vector.reciprocal(self.stat, self.stat).then_inc(m.sem["stat_ready"], 1)

        def rotated(n):
            e.wait_ge(m.sem["rot_done"], m.at("rot_done", n + 1))
            tt(self.tmp[n % 2], m.rope[0:QH, 1, :], m.ps[0:QH, 4 + n % 2, :], ALU.mult).then_inc(m.sem["rot_taken"], 1)
            e.wait_ge(m.sem["rot_taken"], m.at("rot_taken", n + 1))
            e.wait_ge(m.sem["cos_done"], m.at("cos_done", n + 1))
            m.dve(e, tt(self.item(n), self.item(n), self.tmp[n % 2], ALU.add))
        for n in range(self.ITEMS):
            e.wait_ge(m.sem["stat_spread"], m.at("stat_spread", n + 1))
            w = m.qkn[0:QH, 2 * self.l + n // MH:2 * self.l + n // MH + 1]
            stt(self.item(n), self.item(n), w, m.ps[0:QH, 2 + n % 2, :], ALU.mult, ALU.mult).then_inc(m.sem["normed"], 1)
            if n >= 1:
                rotated(n - 1)
        rotated(self.ITEMS - 1)

    def end(self):
        n = self.ITEMS
        finish(self.m, lsq_ready=3, lsq_used=3, raw_taken=n, raw_ready=n, lat_ready=3, lv_taken=ST, lv_done=ST - 1, stat_ready=1, normed=n,
               stat_spread=n, isq_ready=n, isq_used=n, rot_taken=n, rot_done=n, lstd_ready=2, kpe_copied=MH, stat_std=1, cos_done=n)


class LatentAttention(Attention):
    units = MH
    per = ST
    scale = 1.0
    n = 0

    def __init__(self, m, up):
        super().__init__(m)
        self.up = up
        self.setup_views()
        self.qs = [m.misc[0:QH, i * S:(i + 1) * S] for i in (8, 9)]
        self.tok = m.misc[:, 14 * S:18 * S].rearrange("p (t n) -> p t n", t=ST)

    def q(self, p, j):
        return self.qs[par(p)]

    def k(self, p, j):
        return self.m.act[0:QH, bass.ds(val(p) + 12, 1), :].rearrange("p a s -> p (a s)")

    def v(self, p, j, b):
        return self.up.tok_v[:, b, bass.ds(val(p) * 64, 64)]

    def out(self, p, j):
        return self.tok[:, j, bass.ds(val(p) * 64, 64)]

    def tensor(self, e):
        m = self.m

        def now(p, j):
            if j == 0:
                e.wait_ge(m.sem["q_staged"], m.at("q_staged", val(p) + 1))
            self.logits(e, p, j)
        self.run(e, None, 0, now, [(1, self.turn), (2, self.times_v)], lambda: None)

    def logit_src(self, j):
        return self.m.ps[:, 4 + j % 2, :]

    def stage(self, e, p):
        m, nc = self.m, self.m.nc
        src = m.act[0:QH, bass.ds(val(p) + 4, 1), :].rearrange("p a s -> p (a s)")
        nc.scalar.activation(self.qs[par(p)], src, ACT.Copy, scale=QH ** -0.5).then_inc(m.sem["q_staged"], 1)

    def scalar(self, e):
        def now(p, j):
            self.exp(e, p, j)
            if j == 2 and not (isinstance(p, int) and p == self.units - 1):
                self.stage(e, p + 1 if isinstance(p, int) else (p[0], p[1] + 1))
        self.run(e, None, 0, now, [(1, self.copy_turned)], lambda: self.stage(e, 0))

    def vector(self, e):
        m, nc = self.m, self.m.nc

        def now(p, j):
            s, n = self.s(p, j), (j + 1) * P
            e.wait_ge(m.sem["logits_ready"], m.at("logits_ready", s + 1))
            nc.vector.tensor_reduce(self.nm[:, j % 4:j % 4 + 1], m.ps[:, 4 + j % 2, 0:n], AX.X, ALU.max, negate=True).then_inc(m.sem["max_ready"], 1)
        self.run(e, m.dve, self.per, now, [(2, self.output)], lambda: None)

    def end(self):
        self.finish_steps()
        finish(self.m, q_staged=self.units)


class SplitNorm:

    def __init__(self, m, gain, shift=None):
        self.m, self.gain, self.shift, self.stats = m, gain, shift, Stats(m)

    def tmp(self, k):
        return self.m.sg[:, k // 2 % 2, k % 2, :]

    def tensor(self, e):
        self.stats.tensor(e)

    def scalar(self, e):
        m, nc = self.m, self.m.nc
        self.stats.scalar(e)
        for k in range(DK):
            e.wait_ge(m.sem["h_scaled"], m.at("h_scaled", k + 1))
            shift = self.shift(k) if self.shift else 0.0
            nc.scalar.activation(m.h_hi[:, k, :], self.tmp(k), ACT.Identity if self.shift else ACT.Copy, bias=shift).then_inc(m.sem["hi_ready"], 1)

    def vector(self, e):
        m, nc = self.m, self.m.nc
        self.stats.vector(e)

        def rest(k):
            e.wait_ge(m.sem["hi_ready"], m.at("hi_ready", k + 1))
            nc.vector.scalar_tensor_tensor(m.h_lo[:, k, :], self.tmp(k), self.shift(k) if self.shift else 0.0,
                                           m.h_hi[:, k, :].bitcast(F32), ALU.add, ALU.subtract).then_inc(m.sem["h_ready"], 1)
        for k in range(DK):
            if k >= 4:
                e.wait_ge(m.sem["h_ready"], m.at("h_ready", k - 3))
            nc.vector.scalar_tensor_tensor(self.tmp(k), m.x[:, k, :], self.gain(k), m.ps[:, 6, :], ALU.mult, ALU.mult).then_inc(m.sem["h_scaled"], 1)
            if k >= 1:
                rest(k - 1)
        rest(DK - 1)

    def end(self):
        self.stats.end()
        finish(self.m, h_ready=DK, h_scaled=DK, hi_ready=DK)


class Split(Stage):

    before = after = None

    def off(self):
        return 1 if self.before else 0

    def split_count(self, name, j):
        return val(j) + (self.m.counts[name].done + 1 - self.off())

    def split_hi(self, e, j, slot, free):
        m, nc = self.m, self.m.nc
        free()
        self.landed(e, j, slot)
        nc.scalar.activation(m.w_hi[slot][:, 0:self.size], m.w[slot][:, 0:self.size], ACT.Copy).then_inc(m.sem["w_hi_ready"], 1)

    def split_lo(self, e, slot, count):
        m, nc = self.m, self.m.nc
        e.wait_ge(m.sem["w_hi_ready"], count)
        nc.vector.tensor_tensor(m.w_lo[slot][:, 0:self.size], m.w[slot][:, 0:self.size], m.w_hi[slot][:, 0:self.size].bitcast(F32), ALU.subtract).then_inc(m.chunk_done, 1)

    def ahead(self, e, j, engine):
        m = self.m
        slot = (self.c0 + par(j) + 1) % 2
        own = not isinstance(j, int) or j + 1 < self.n
        stage = self if own else self.after
        if stage is None:
            return

        def free():
            if due(val(j)):
                e.wait_ge(m.sem["prod_done"], m.at("prod_done", val(j)))
        nxt = (j + 1 if isinstance(j, int) else (j[0], j[1] + 1)) if own else 0
        if engine == "scalar":
            stage.split_hi(e, nxt, slot, free)
        else:
            free()
            count = self.split_count("w_hi_ready", j) + 1
            stage.split_lo(e, slot, count)

    def first(self, e, engine):
        if not self.before:
            slot = self.c0 % 2
            if engine == "scalar":
                self.split_hi(e, 0, slot, lambda: None)
            else:
                self.split_lo(e, slot, self.split_count("w_hi_ready", 0))

    def three(self, out, slot, at, a, k, kt):
        m, nc = self.m, self.m.nc
        hi, lo = m.w_hi[slot][:, at:at + P], m.w_lo[slot][:, at:at + P]
        nc.tensor.matmul(out, hi, a[0][:, k, :], start=k == 0, stop=False)
        nc.tensor.matmul(out, hi, a[1][:, k, :], start=False, stop=False)
        return nc.tensor.matmul(out, lo, a[0][:, k, :], start=False, stop=k == kt - 1)

    def end(self):
        finish(self.m, prod_done=self.n, w_hi_ready=self.n - self.off() + (1 if self.after else 0))


class SplitGateUp(Split):

    def __init__(self, m, w, half, norm, ada=None):
        super().__init__(m)
        self.norm, self.n, self.size, self.ada = norm, FH_K, DK * 256, ada
        self.src = w.rearrange("(k p) n -> p k n", p=P)
        self.off0 = half * FH_K * P

    def load(self, j, slot):
        v = slot[:, 0:self.size].rearrange("p (k g n) -> p k g n", k=DK, g=2)
        return [(v[:, :, g, :], self.src[:, :, bass.ds(j * P + (g * FF + self.off0), P)]) for g in range(2)]

    def tensor(self, e):
        m = self.m
        if self.norm:
            self.norm.tensor(e)

        def chunk(j):
            slot = (self.c0 + par(j)) % 2
            e.wait_ge(m.chunk_done, val(j) + (self.c0 + 1))
            if due(val(j) - 1):
                e.wait_ge(m.sem["pair_taken"], m.at("pair_taken", val(j) - 1))
            for k in range(DK):
                if self.norm and isinstance(j, int) and j == 0:
                    e.wait_ge(m.sem["h_ready"], m.at("h_ready", k + 1))
                for b in range(2):
                    last = self.three(m.ps[:, par(j) * 2 + b, :], slot, k * 256 + b * P, (m.h_hi, m.h_lo), k, DK)
            last.then_inc(m.sem["prod_done"], 1)
            if self.ada:
                self.ada_unit(e, j)
        pairs(e, self.n, 1, chunk)
        if self.ada:
            self.ada.tensor(e, self.n)

    def ada_unit(self, e, j):
        m, nc = self.m, self.m.nc
        e.wait_ge(m.sem["ada_summed"], m.at("ada_summed", val(j) + 1))
        out = m.ps[:, 4, bass.ds(val(j), 1)]
        nc.tensor.matmul(out, m.ada_p[:, par(j), 0:P], m.ones[:, 0:1], start=True, stop=True).then_inc(m.sem["ada_done"], 1)

    def gpsimd(self, e):
        if self.ada:
            self.ada.gpsimd(e)

    def scalar(self, e):
        m, nc = self.m, self.m.nc
        self.first(e, "scalar")
        if self.norm:
            self.norm.scalar(e)

        def chunk(j):
            self.ahead(e, j, "scalar")
            if due(val(j) - 1):
                e.wait_ge(m.sem["pair_taken"], m.at("pair_taken", val(j) - 1))
            e.wait_ge(m.sem["prod_done"], m.at("prod_done", val(j) + 1))
            nc.scalar.activation(m.sg[:, par(j), 0, :], m.ps[:, par(j) * 2, :], ACT.Silu).then_inc(m.sem["half_ready"], 1)
        pairs(e, self.n, 2, chunk, tail=1)

    def vector(self, e):
        m, nc = self.m, self.m.nc
        self.first(e, "vector")
        if self.norm:
            self.norm.vector(e)
            e.wait_ge(m.sem["h_ready"], m.at("h_ready", DK))

        def chunk(j):
            self.ahead(e, j, "vector")
            e.wait_ge(m.sem["half_ready"], m.at("half_ready", val(j) + 1))
            t = m.sg[:, par(j), 1, :]
            m.dve(e, nc.vector.tensor_tensor(t, m.sg[:, par(j), 0, :], m.ps[:, par(j) * 2 + 1, :], ALU.mult))
            hi = m.a_hi[:, bass.ds(val(j), 1), :].rearrange("p a s -> p (a s)")
            lo = m.a_lo[:, bass.ds(val(j), 1), :].rearrange("p a s -> p (a s)")
            m.dve(e, nc.vector.tensor_scalar(hi, t, 1.0, None, ALU.mult))
            nc.vector.tensor_tensor(lo, t, hi.bitcast(F32), ALU.subtract).then_inc(m.sem["pair_taken"], 1)
        pairs(e, self.n, 2, chunk, m.dve, 4, tail=1)
        if self.ada:
            self.ada.vector(e)

    def end(self):
        super().end()
        if self.ada:
            self.ada.end()
        if self.norm:
            self.norm.end()
        finish(self.m, pair_taken=self.n, half_ready=self.n)


class SplitDown(Split):

    def __init__(self, m, w, half, gate=None):
        super().__init__(m)
        self.gate, self.n, self.size = gate, DK, FH_K * P
        self.src = w[half * FH_K * P:(half + 1) * FH_K * P, :].rearrange("(k p) n -> p k n", p=P)

    def load(self, j, slot):
        return [(slot[:, 0:self.size].rearrange("p (k n) -> p k n", k=FH_K), self.src[:, :, bass.ds(j * P, P)])]

    def tensor(self, e):
        m = self.m

        def chunk(j):
            slot = (self.c0 + par(j)) % 2
            e.wait_ge(m.chunk_done, val(j) + (self.c0 + 1))
            if due(val(j) - 1):
                e.wait_ge(m.sem["out_taken"], m.at("out_taken", val(j) - 1))
            for k in range(FH_K):
                last = self.three(m.ps[:, par(j), :], slot, k * P, (m.a_hi, m.a_lo), k, FH_K)
            last.then_inc(m.sem["prod_done"], 1)
        pairs(e, self.n, 2, chunk, tail=1)

    def scalar(self, e):
        self.first(e, "scalar")
        pairs(e, self.n, 2, lambda j: self.ahead(e, j, "scalar"), tail=1)

    def vector(self, e):
        m, nc = self.m, self.m.nc
        self.first(e, "vector")

        def chunk(j):
            self.ahead(e, j, "vector")
            e.wait_ge(m.sem["prod_done"], m.at("prod_done", val(j) + 1))
            xs = m.x[:, bass.ds(val(j), 1), :].rearrange("p a s -> p (a s)")
            nc.vector.scalar_tensor_tensor(xs, m.ps[:, par(j), :], self.gate(val(j)) if self.gate else 1.0, xs, ALU.mult, ALU.add).then_inc(m.sem["out_taken"], 1)
        pairs(e, self.n, 2, chunk, tail=1)

    def end(self):
        super().end()
        finish(self.m, out_taken=self.n)


class Setup(Stage):

    def sync(self, e):
        m, d = self.m, self.m.d
        self.loaded = m.count("x_loaded")
        self.par = m.count("params_loaded")
        e.dma_start(m.consts[:], d["consts"]).then_inc(self.par.sem, 16)
        e.dma_start(m.spread[:], d["spread"]).then_inc(self.par.sem, 16)
        e.dma_start(m.act[:, 0:8, :].rearrange("p a s -> p (a s)").rearrange("p (t d) -> p t d", t=ST),
                    d["x"].rearrange("a (t p) d -> p (a t) d", p=P)).then_inc(self.loaded.sem, 16)
        e.wait_ge(m.sem["filled"], 1)
        rows = m.act[:, 8, 0:384].rearrange("p (a n) -> p a n", a=3)

        def put(a, name, src):
            r = COL[name] % 128 if a < 2 else COL[name] - 256
            n = src.shape[0]
            e.dma_start(rows[r:r + n, a, :], src).then_inc(self.par.sem, 16)

        put(0, "mix", d["mix_norm_g"].rearrange("l (k p) -> (l k) p", p=P))
        put(0, "ffn", d["ffn_norm_g"].rearrange("l (k p) -> (l k) p", p=P))
        put(0, "final", d["final_norm_g"].rearrange("(k p) -> k p", p=P))
        put(0, "s5_d", d["s5_d"].rearrange("l (k p) -> (l k) p", p=P))
        put(0, "pool_b", d["pool_b"].rearrange("l (k p) -> (l k) p", p=P))
        put(0, "pool_s", d["pool_scale"].rearrange("l (k p) -> (l k) p", p=P))
        put(1, "norm1", d["norm1_w_2"].rearrange("l (k p) -> (l k) p", p=P))
        put(1, "norm2", d["norm2_w_2"].rearrange("l (k p) -> (l k) p", p=P))
        put(1, "b_ada", d["b_ada_2"].rearrange("l (k p) -> (l k) p", p=P))
        put(2, "q_a", d["q_a_norm_w_2"].rearrange("l (k p) -> (l k) p", p=P))
        put(2, "kv_a", d["kv_a_norm_w_2"].rearrange("l (k p) -> (l k) p", p=P))
        put(2, "conv_b", d["conv_b_2"].rearrange("l (k p) -> (l k) p", p=P))
        put(2, "ssd_n", d["ssd_norm_w_2"].rearrange("l (k p) -> (l k) p", p=P))
        put(2, "conv_w", d["conv_w_2"].rearrange("l w (k p) -> (l w k) p", p=P))
        put(2, "c", d["c_2"].rearrange("l (k p) -> (l k) p", p=P))
        for l in range(2):
            e.dma_start(m.wf[:, l], d["fox_w_in"][l, :, 3 * D:3 * D + FH].rearrange("(k p) n -> p k n", p=P)).then_inc(self.par.sem, 16)
        with m.nc.allow_non_contiguous_dma(reason="sixteen biases of heads"):
            for l in range(2):
                e.dma_start(m.small[0:FH, l:l + 1], d["fox_b_f"][l].rearrange("(h a) -> h a", a=1)).then_inc(self.par.sem, 16)

    def gpsimd(self, e):
        m, nc = self.m, self.m.nc
        r = m.count("filled")
        nc.gpsimd.memset(m.act[:, 8, 0:384], 0.0).then_inc(r.sem, 1)
        for n, (buf, value) in enumerate(((m.mean_w, 1.0 / D), (m.ones, 1.0), (m.eps, EPS), (m.ones16, 1.0))):
            e.wait_ge(r.sem, n + 1)
            nc.gpsimd.memset(buf[:], value).then_inc(r.sem, 1)

    def tensor(self, e):
        m, nc = self.m, self.m.nc
        moved, taken = m.count("turned"), m.count("turn_taken")
        e.wait_ge(self.loaded.sem, 16)
        e.wait_ge(self.par.sem, 16 * 21)
        e.wait_ge(m.sem["filled"], 5)
        xt = m.act[:, 0:8, :].rearrange("p a s -> p (a s)").rearrange("p (t d) -> p t d", t=ST)
        for k in range(DK):
            if k >= 4:
                e.wait_ge(taken.sem, taken.at(k - 3))
            for t in range(ST):
                last = nc.tensor.transpose(m.ps[:, k % 4, t * P:(t + 1) * P], xt[:, t, k * P:(k + 1) * P], m.c("ident"))
            last.then_inc(moved.sem, 1)
        for a in range(3):
            last = nc.tensor.transpose(m.ps[:, 4, a * P:(a + 1) * P], m.act[:, 8, a * P:(a + 1) * P], m.c("ident"))
        last.then_inc(moved.sem, 1)

    def scalar(self, e):
        m, nc = self.m, self.m.nc
        e.wait_ge(m.sem["turn_taken"], m.at("turn_taken", DK + 1))
        m.acts(e, nc.scalar.activation(m.cact[:], m.cols[:, COL["c"]:COL["c"] + DK], ACT.Silu))

    def vector(self, e):
        m, nc = self.m, self.m.nc
        moved, taken = m.count("turned"), m.count("turn_taken")
        e.wait_ge(self.par.sem, 16 * 21)
        nc.vector.tensor_reduce(m.rowmask[:], m.c("ident").rearrange("p (r n) -> p r n", r=4), AX.X, ALU.add)
        nc.vector.tensor_copy(m.identb[:], m.c("ident"))
        nc.vector.tensor_copy(m.futureb[:], m.c("future"))
        nc.vector.tensor_copy(m.pastb[:], m.c("past"))
        for k in range(DK):
            e.wait_ge(moved.sem, moved.at(k + 1))
            nc.vector.tensor_copy(m.x[:, k, :], m.ps[:, k % 4, :]).then_inc(taken.sem, 1)
        e.wait_ge(moved.sem, moved.at(DK + 1))
        nc.vector.tensor_copy(m.cols[:], m.ps[:, 4, 0:384]).then_inc(taken.sem, 1)

    def end(self):
        finish(self.m, turned=DK + 1, turn_taken=DK + 1, x_loaded=16, params_loaded=16 * 21, filled=5)


class Store(Stage):

    def tensor(self, e):
        m, nc = self.m, self.m.nc
        moved, taken = m.count("turned"), m.count("turn_taken")
        for t in range(ST):
            for f in range(2):
                n = 2 * t + f
                if n >= 4:
                    e.wait_ge(taken.sem, taken.at(n - 3))
                for k in range(4):
                    last = nc.tensor.transpose(m.ps[:, n % 4, k * P:(k + 1) * P], m.x[:, 4 * f + k, t * P:(t + 1) * P], m.c("ident"))
                last.then_inc(moved.sem, 1)

    def vector(self, e):
        m, nc = self.m, self.m.nc
        moved, taken = m.count("turned"), m.count("turn_taken")
        for n in range(8):
            e.wait_ge(moved.sem, moved.at(n + 1))
            nc.vector.tensor_copy(m.act[:, n, :], m.ps[:, n % 4, :]).then_inc(taken.sem, 1)

    def sync(self, e):
        m = self.m
        taken, stored = m.count("turn_taken"), m.count("stored")
        out = m.d["out"].rearrange("a (t p) (f n) -> (a t) f p n", p=P, f=2)
        for n in range(8):
            e.wait_ge(taken.sem, taken.at(n + 1))
            e.dma_start(out[n // 2, n % 2], m.act[:, n, :]).then_inc(stored.sem, 16)
        e.wait_ge(stored.sem, stored.at(128))


class FinalNorm(Stage):

    def __init__(self, m, norm):
        super().__init__(m)
        self.norm = norm
        norm.dst = lambda k: m.x[:, k, :]

    def tensor(self, e): self.norm.tensor(e)
    def scalar(self, e): self.norm.scalar(e)
    def vector(self, e): self.norm.vector(e)
    def end(self): self.norm.end()


def build(nc, d):
    with ExitStack() as ctx:
        m = Machine(nc, ctx, d)
        stages = [Setup(m)]
        stages += plan(m, d)
        stages.append(Store(m))
        n = 0
        for s in stages:
            s.c0 = n
            n += s.n
        issued = 0
        for s in stages:
            want = min(n, s.c0 + s.n + 2)
            todo = []
            for t in stages:
                a, b = max(issued, t.c0), min(want, t.c0 + t.n)
                if b > a:
                    todo.append((t.load, t.c0, a - t.c0, b - t.c0))
            issued = max(issued, want)
            stream = m.loads(todo)
            s.pool0 = m.pool.base + m.pool.k
            with nc.Block() as block:
                @block.sync
                def _(sp):
                    s.sync(sp)
                    stream(sp)

                @block.gpsimd
                def _(pool):
                    s.gpsimd(pool)

                @block.tensor
                def _(pe):
                    s.tensor(pe)

                @block.scalar
                def _(act):
                    s.scalar(act)

                @block.vector
                def _(dve):
                    s.vector(dve)
            s.end()


def swiglu(m, out, gate_up, down, norm, gate=None, units=None):
    parts = []
    for half in range(2):
        ada = AdaUnits(m, units + half * (FH_K + 1), FH_K + 1) if units is not None else None
        parts += [SplitGateUp(m, gate_up, half, None if half else norm, ada), SplitDown(m, down, half, gate)]
    for a, b in zip(parts, parts[1:]):
        a.after, b.before = b, a
    out += parts


def plan(m, d):
    out = []
    for l in range(4):
        mix = Norm(m, lambda k, l=l: m.col("mix", 8 * l + k))
        if l % 3 == 0:
            out.append(FoxV(m, l // 3, mix))
            out.append(FoxAttention(m, l // 3))
            out.append(Project(m, d["fox_w_out"][l // 3], lambda k: m.h[:, k, :], turn=DK))
        elif l == 1:
            four = lambda j: m.act[:, 4 * j:4 * j + 4, :]
            out.append(S5In(m, d["s5_w_in"][0], mix, four))
            out.append(S5Scan(m))
            out.append(GateUp(m, d["s5_w_glu"][0], D, Gelu(m), glu=True))
        else:
            out.append(PoolMix(m, mix))
        swiglu(m, out, d["ffn_w_gate_up"][l], d["ffn_w_down"][l], SplitNorm(m, lambda k, l=l: m.col("ffn", 8 * l + k)),
               units=l * 2 * (FH_K + 1))
    out.append(FinalNorm(m, Norm(m, lambda k: m.col("final", k))))
    for l in range(2):
        mod = lambda i, k, l=l: m.mod[:, l, 8 * i + k:8 * i + k + 1]
        gain = lambda i, k, l=l: m.gains[:, l, i, k:k + 1]
        if l == 0:
            out.append(SecondSetup(m))
        out.append(SecondIn(m, l, Norm(m, lambda k, g=gain: g(0, k), lambda k, mod=mod: mod(0, k))))
        out.append(Ssd(m, l))
        up = LatentUp(m, l)
        out.append(up)
        att = LatentAttention(m, up)
        out.append(att)
        out.append(Project(m, d["w_out_2"][l], lambda k: m.h[:, k, :], turn=4, gate=lambda k, mod=mod: mod(2, k), tok=att.tok))
        swiglu(m, out, d["w_gate_up_2"][l], d["w_down_2"][l], SplitNorm(m, lambda k, g=gain: g(1, k), lambda k, mod=mod: mod(3, k)),
               lambda k, l=l: m.mod[:, l, bass.ds(k + 40, 1)])
    return out


NAMES = ["x", "mix_norm_g", "ffn_norm_g", "final_norm_g", "fox_w_in", "fox_b_f", "fox_w_out", "s5_w_in", "s5_a_re",
         "s5_a_im", "s5_log_dt", "s5_b_re", "s5_b_im", "s5_c_re", "s5_c_im", "s5_d", "s5_w_glu", "pool_w", "pool_b",
         "pool_scale", "ffn_w_gate_up", "ffn_w_down", "c_2", "positions_2", "norm1_w_2", "norm2_w_2", "w_ada_2",
         "b_ada_2", "w_in_2", "q_a_norm_w_2", "w_q_up_2", "kv_a_norm_w_2", "w_kv_up_2", "q_nope_norm_w_2",
         "q_pe_norm_w_2", "k_nope_norm_w_2", "k_pe_norm_w_2", "conv_w_2", "conv_b_2", "dt_bias_2", "a_log_2",
         "d_skip_2", "ssd_norm_w_2", "w_out_2", "w_gate_up_2", "w_down_2"]


def kernel(**inputs):
    import concourse.bacc as _bacc
    from concourse.bass_utils import run_bass_kernel_spmd as _run

    nc = _bacc.Bacc("TRN2", target_bir_lowering=False, num_devices=1)
    arrays, d = {}, {}
    for name in NAMES:
        a = np.ascontiguousarray(inputs[name])
        arrays[f"in_{name}"] = a
        d[name] = nc.dram_tensor(f"in_{name}", a.shape, mybir.dt.from_np(a.dtype), kind="ExternalInput").ap()
    arrays["in_consts"] = CONSTS
    arrays["in_spread"] = SPREAD
    d["spread"] = nc.dram_tensor("in_spread", SPREAD.shape, F32, kind="ExternalInput").ap()
    d["consts"] = nc.dram_tensor("in_consts", CONSTS.shape, F32, kind="ExternalInput").ap()
    d["out"] = nc.dram_tensor("out_0", (1, S, D), F32, kind="ExternalOutput").ap()
    build(nc, d)
    r = _run(nc, [arrays], core_ids=[0])
    return r.results[0]["out_0"]
```
